# Optimizing a Trainium2 kernel written in Bass

```python
import math
import jax, jax.numpy as jnp
from jax import lax
import numpy as np

D_MODEL = 1024
BATCH = 1
SEQ = 256
DEPTH = 1

PLE_DIM = 256
NORM_EPS = 1e-6
NEG_INF = -1e30
N_BRANCH = 4
BRANCH_WIDTH = D_MODEL // 2
ATTN_BLOCK = 128

SWA_HEADS = 8
SWA_KV_HEADS = 2
SWA_HEAD_DIM = 64
SWA_WINDOW = 128

HGRN_HEADS = 4
HGRN_KEY_DIM = 128
HGRN_VAL_DIM = 128
HGRN_CHUNK = 32
HGRN_MIN_F = 1e-6

NSA_HEADS = 8
NSA_KV_HEADS = 2
NSA_HEAD_DIM = 64
NSA_CMP_LEN = 32
NSA_CMP_STRIDE = 16
NSA_CMP_HIDDEN = 256
NSA_SEL_LEN = 64
NSA_TOP_N = 16
NSA_WINDOW = 512
NSA_FORCE_SCORE = 1e6

SSM_HEADS = 8
SSM_HEAD_DIM = 64
SSM_GROUPS = 2
SSM_STATE = 64
SSM_CONV = 4
SSM_CHUNK = 64
SSM_INNER = SSM_HEADS * SSM_HEAD_DIM
SSM_CONV_DIM = SSM_INNER + 2 * SSM_GROUPS * SSM_STATE

MOE_GROUPS = 4
MOE_EXPERTS_PER_GROUP = 8
MOE_EXPERTS = MOE_GROUPS * MOE_EXPERTS_PER_GROUP
MOE_TOP_K = 2
MOE_FF = D_MODEL // 4

IN_SPLITS = (
    ('swa_q', SWA_HEADS * SWA_HEAD_DIM),
    ('swa_k', SWA_KV_HEADS * SWA_HEAD_DIM),
    ('swa_v', SWA_KV_HEADS * SWA_HEAD_DIM),
    ('hgrn_q', HGRN_HEADS * HGRN_KEY_DIM),
    ('hgrn_f', HGRN_HEADS * HGRN_KEY_DIM),
    ('hgrn_i', HGRN_HEADS * HGRN_VAL_DIM),
    ('hgrn_g', HGRN_HEADS * HGRN_VAL_DIM),
    ('nsa_q', NSA_HEADS * NSA_HEAD_DIM),
    ('nsa_k_cmp', NSA_KV_HEADS * NSA_HEAD_DIM),
    ('nsa_v_cmp', NSA_KV_HEADS * NSA_HEAD_DIM),
    ('nsa_k_slc', NSA_KV_HEADS * NSA_HEAD_DIM),
    ('nsa_v_slc', NSA_KV_HEADS * NSA_HEAD_DIM),
    ('nsa_k_win', NSA_KV_HEADS * NSA_HEAD_DIM),
    ('nsa_v_win', NSA_KV_HEADS * NSA_HEAD_DIM),
    ('nsa_gate', NSA_HEADS * 3),
    ('ssm_z', SSM_INNER),
    ('ssm_xbc', SSM_CONV_DIM),
    ('ssm_dt', SSM_HEADS),
    ('merge_gate', N_BRANCH * D_MODEL),
)
IN_WIDTH = sum(w for _, w in IN_SPLITS)

kernel_name = 'hybrid_parallel_swa_hgrn2_nsa_ssd_hmoe'

def rmsnorm(x, g):
    xf = x.astype(jnp.float32)
    y = xf * lax.rsqrt(jnp.mean(xf * xf, axis=-1, keepdims=True) + NORM_EPS)
    return (y * g.astype(jnp.float32)).astype(x.dtype)

def alibi_slopes(n_heads):
    return 2.0 ** (-8.0 * jnp.arange(1, n_heads + 1, dtype=jnp.float32) / n_heads)

def split_proj(proj):
    out = {}
    off = 0
    for name, w in IN_SPLITS:
        out[name] = proj[..., off:off + w]
        off += w
    return out

def banded_attention(q, k, v, window, slopes, sinks=None):
    B, L, H, d = q.shape
    G = k.shape[2]
    R = H // G
    blk = ATTN_BLOCK
    nb = L // blk
    nprev = (window - 1 + blk - 1) // blk
    nk = (nprev + 1) * blk
    qb = q.reshape(B, nb, blk, G, R, d)
    pad = ((0, 0), (nprev * blk, 0), (0, 0), (0, 0))
    kp = jnp.pad(k, pad).reshape(B, nb + nprev, blk, G, d)
    vp = jnp.pad(v, pad).reshape(B, nb + nprev, blk, G, d)
    kb = jnp.concatenate([kp[:, j:j + nb] for j in range(nprev + 1)], axis=2)
    vb = jnp.concatenate([vp[:, j:j + nb] for j in range(nprev + 1)], axis=2)
    s = jnp.einsum('bnqgrd,bnkgd->bngrqk', qb, kb).astype(jnp.float32) * (d ** -0.5)
    qi = jnp.arange(blk)[:, None]
    kj = jnp.arange(nk)[None, :]
    rel = qi + nprev * blk - kj
    kpos = jnp.arange(nb)[:, None, None] * blk + kj - nprev * blk
    mask = (rel >= 0) & (rel < window) & (kpos >= 0)
    s = s - slopes.reshape(G, R)[:, :, None, None] * rel.astype(jnp.float32)
    s = jnp.where(mask[None, :, None, None], s, NEG_INF)
    if sinks is not None:
        sink = sinks.astype(jnp.float32).reshape(1, 1, G, R, 1, 1)
        m = jnp.maximum(jnp.max(s, axis=-1, keepdims=True), sink)
        e = jnp.exp(s - m)
        pr = e / (jnp.sum(e, axis=-1, keepdims=True) + jnp.exp(sink - m))
    else:
        pr = jax.nn.softmax(s, axis=-1)
    o = jnp.einsum('bngrqk,bnkgd->bnqgrd', pr.astype(v.dtype), vb)
    return o.reshape(B, L, H * d).astype(q.dtype)

def swa_mixer(seg, sinks, slopes):
    B, L, _ = seg['swa_q'].shape
    q = seg['swa_q'].reshape(B, L, SWA_HEADS, SWA_HEAD_DIM)
    k = seg['swa_k'].reshape(B, L, SWA_KV_HEADS, SWA_HEAD_DIM)
    v = seg['swa_v'].reshape(B, L, SWA_KV_HEADS, SWA_HEAD_DIM)
    return banded_attention(q, k, v, SWA_WINDOW, slopes, sinks)

def gla_chunked(q, k, v, log_f, chunk):
    B, L, H, dk = q.shape
    dv = v.shape[-1]
    nc = L // chunk
    f32 = jnp.float32
    qc = q.astype(f32).reshape(B, nc, chunk, H, dk)
    kc = k.astype(f32).reshape(B, nc, chunk, H, dk)
    vc = v.astype(f32).reshape(B, nc, chunk, H, dv)
    b = jnp.cumsum(log_f.astype(f32).reshape(B, nc, chunk, H, dk), axis=2)
    b_mid = b[:, :, chunk // 2:chunk // 2 + 1]
    b_last = b[:, :, -1:]
    A = jnp.einsum('bcthk,bcshk->bchts', qc * jnp.exp(b - b_mid), kc * jnp.exp(b_mid - b))
    causal = jnp.tril(jnp.ones((chunk, chunk), dtype=bool))
    A = jnp.where(causal, A, 0.0)
    o_intra = jnp.einsum('bchts,bcshv->bcthv', A, vc)
    u = jnp.einsum('bcshk,bcshv->bchkv', kc * jnp.exp(b_last - b), vc)
    decay = jnp.exp(b_last[:, :, 0])

    def step(S, inp):
        d_c, u_c = inp
        return d_c[..., None] * S + u_c, S

    _, S_prev = lax.scan(step, jnp.zeros((B, H, dk, dv), f32),
                         (jnp.moveaxis(decay, 1, 0), jnp.moveaxis(u, 1, 0)))
    S_prev = jnp.moveaxis(S_prev, 0, 1)
    o_inter = jnp.einsum('bcthk,bchkv->bcthv', qc * jnp.exp(b), S_prev)
    return (o_intra + o_inter).reshape(B, L, H, dv).astype(v.dtype)

def hgrn2_mixer(seg, lb, norm_g):
    B, L, _ = seg['hgrn_q'].shape
    H, dk, dv = HGRN_HEADS, HGRN_KEY_DIM, HGRN_VAL_DIM
    q = seg['hgrn_q'].reshape(B, L, H, dk)
    z = seg['hgrn_f'].reshape(B, L, H, dk).astype(jnp.float32)
    i_in = seg['hgrn_i'].reshape(B, L, H, dv)
    lb = lb.reshape(H, dk)
    f = lb + (1.0 - lb) * jax.nn.sigmoid(z)
    log_f = jnp.log(jnp.maximum(f, HGRN_MIN_F))
    k = (1.0 - lb) * jax.nn.sigmoid(-z)
    o = gla_chunked(q, k, i_in, log_f, HGRN_CHUNK)
    o = rmsnorm(o, norm_g.reshape(H, dv)).reshape(B, L, H * dv)
    return o * jax.nn.silu(seg['hgrn_g'])

def nsa_mixer(seg, pos_k, pos_v, w1_k, w2_k, w1_v, w2_v, slopes):
    B, L, _ = seg['nsa_q'].shape
    H, G, d = NSA_HEADS, NSA_KV_HEADS, NSA_HEAD_DIM
    R = H // G
    blk = ATTN_BLOCK
    nb = L // blk
    scale = d ** -0.5
    q = seg['nsa_q'].reshape(B, L, H, d)

    def kvh(name):
        return seg[name].reshape(B, L, G, d)

    n_cmp = (L - NSA_CMP_LEN) // NSA_CMP_STRIDE + 1
    cmp_start = np.arange(n_cmp, dtype=np.int32) * NSA_CMP_STRIDE
    cmp_idx = cmp_start[:, None] + np.arange(NSA_CMP_LEN, dtype=np.int32)[None, :]
    cmp_end = cmp_start + NSA_CMP_LEN - 1

    def compress(kx, pos, w1, w2):
        blocks = kx[:, cmp_idx] + pos[None, None, :, None, :]
        flat = blocks.transpose(0, 1, 3, 2, 4).reshape(B, n_cmp, G, NSA_CMP_LEN * d)
        return jax.nn.gelu(flat @ w1) @ w2

    k_cmp = compress(kvh('nsa_k_cmp'), pos_k, w1_k, w2_k)
    v_cmp = compress(kvh('nsa_v_cmp'), pos_v, w1_v, w2_v)

    n_sel_blocks = L // NSA_SEL_LEN
    top_n = min(NSA_TOP_N, n_sel_blocks)
    sel_start = np.arange(n_sel_blocks, dtype=np.int32) * NSA_SEL_LEN
    overlap = np.clip(np.minimum(cmp_start[:, None] + NSA_CMP_LEN, sel_start[None, :] + NSA_SEL_LEN)
                      - np.maximum(cmp_start[:, None], sel_start[None, :]), 0, None) / NSA_CMP_LEN
    overlap = jnp.asarray(overlap, dtype=jnp.float32)
    k_sel = kvh('nsa_k_slc').reshape(B, n_sel_blocks, NSA_SEL_LEN, G, d).transpose(0, 3, 1, 2, 4)
    v_sel = kvh('nsa_v_slc').reshape(B, n_sel_blocks, NSA_SEL_LEN, G, d).transpose(0, 3, 1, 2, 4)
    sl = slopes.reshape(G, R)
    b_idx = jnp.arange(B)[:, None, None, None]
    g_idx = jnp.arange(G)[None, :, None, None]
    jblk = jnp.arange(n_sel_blocks)
    q_blocks = q.reshape(B, nb, blk, G, R, d).transpose(1, 0, 2, 3, 4, 5)

    def per_block(args):
        qb, n = args
        qpos = n * blk + jnp.arange(blk)
        dist_c = (qpos[:, None] - cmp_end[None, :]).astype(jnp.float32)
        valid_c = dist_c >= 0
        s_c = jnp.einsum('bqgrd,bcgd->bgrqc', qb, k_cmp).astype(jnp.float32) * scale
        s_c = jnp.where(valid_c, s_c - sl[:, :, None, None] * dist_c, NEG_INF)
        p_c = jnp.where(valid_c, jax.nn.softmax(s_c, axis=-1), 0.0)
        o_c = jnp.einsum('bgrqc,bcgd->bqgrd', p_c.astype(v_cmp.dtype), v_cmp)
        imp = jnp.einsum('bgrqc,cj->bgqj', p_c, overlap)
        cur = qpos[:, None] // NSA_SEL_LEN
        forced = (jblk[None, :] == 0) | (jblk[None, :] == cur) | (jblk[None, :] == cur - 1)
        causal_blk = jblk[None, :] * NSA_SEL_LEN <= qpos[:, None]
        score = jnp.where(forced, NSA_FORCE_SCORE, jnp.where(causal_blk, imp, NEG_INF))
        _, sel = lax.top_k(score, top_n)
        ks = k_sel[b_idx, g_idx, sel]
        vs = v_sel[b_idx, g_idx, sel]
        kpos = sel[..., None] * NSA_SEL_LEN + jnp.arange(NSA_SEL_LEN)
        dist_s = (qpos[None, None, :, None, None] - kpos).astype(jnp.float32)
        valid_s = (dist_s >= 0)[:, :, None]
        s_s = jnp.einsum('bqgrd,bgqjkd->bgrqjk', qb, ks).astype(jnp.float32) * scale
        s_s = jnp.where(valid_s, s_s - sl[None, :, :, None, None, None] * dist_s[:, :, None], NEG_INF)
        p_s = jax.nn.softmax(s_s.reshape(B, G, R, blk, top_n * NSA_SEL_LEN), axis=-1)
        p_s = p_s.reshape(s_s.shape).astype(vs.dtype)
        o_s = jnp.einsum('bgrqjk,bgqjkd->bqgrd', p_s, vs)
        return o_c, o_s

    o_c, o_s = lax.map(per_block, (q_blocks, jnp.arange(nb)))
    o_c = o_c.transpose(1, 0, 2, 3, 4, 5).reshape(B, L, H, d)
    o_s = o_s.transpose(1, 0, 2, 3, 4, 5).reshape(B, L, H, d)
    o_w = banded_attention(q, kvh('nsa_k_win'), kvh('nsa_v_win'), NSA_WINDOW, slopes).reshape(B, L, H, d)
    gate = jax.nn.sigmoid(seg['nsa_gate'].reshape(B, L, H, 3))
    o = gate[..., 0:1] * o_c + gate[..., 1:2] * o_s + gate[..., 2:3] * o_w
    return o.reshape(B, L, H * d)

def causal_conv(x, w, b):
    K = w.shape[0]
    L = x.shape[1]
    xp = jnp.pad(x, ((0, 0), (K - 1, 0), (0, 0)))
    y = b + w[0] * xp[:, 0:L]
    for j in range(1, K):
        y = y + w[j] * xp[:, j:j + L]
    return y

def ssd_chunked(x, dt, A, Bm, Cm, chunk):
    Bsz, L, G, R, P = x.shape
    N = Bm.shape[-1]
    nc = L // chunk
    f32 = jnp.float32
    xc = x.astype(f32).reshape(Bsz, nc, chunk, G, R, P)
    dtc = dt.astype(f32).reshape(Bsz, nc, chunk, G, R)
    Bc = Bm.astype(f32).reshape(Bsz, nc, chunk, G, N)
    Cc = Cm.astype(f32).reshape(Bsz, nc, chunk, G, N)
    acs = jnp.cumsum(dtc * A.reshape(G, R), axis=2)
    at = acs.transpose(0, 1, 3, 4, 2)
    seg = at[..., :, None] - at[..., None, :]
    causal = jnp.tril(jnp.ones((chunk, chunk), dtype=bool))
    Lmat = jnp.exp(jnp.where(causal, seg, NEG_INF))
    CB = jnp.einsum('bctgn,bcsgn->bcgts', Cc, Bc)
    y_diag = jnp.einsum('bcgts,bcgrts,bcsgr,bcsgrp->bctgrp', CB, Lmat, dtc, xc)
    decay_s = jnp.exp(acs[:, :, -1:] - acs)
    states = jnp.einsum('bcsgn,bcsgr,bcsgrp->bcgrpn', Bc, decay_s * dtc, xc)
    chunk_decay = jnp.exp(acs[:, :, -1])

    def step(S, inp):
        d_c, s_c = inp
        return d_c[..., None, None] * S + s_c, S

    _, S_prev = lax.scan(step, jnp.zeros((Bsz, G, R, P, N), f32),
                         (jnp.moveaxis(chunk_decay, 1, 0), jnp.moveaxis(states, 1, 0)))
    S_prev = jnp.moveaxis(S_prev, 0, 1)
    y_off = jnp.einsum('bctgn,bcgrpn,bctgr->bctgrp', Cc, S_prev, jnp.exp(acs))
    return (y_diag + y_off).reshape(Bsz, L, G, R, P)

def mamba2_mixer(seg, conv_w, conv_b, dt_bias, A_log, D_skip, norm_g):
    B, L, _ = seg['ssm_z'].shape
    G, N, P = SSM_GROUPS, SSM_STATE, SSM_HEAD_DIM
    R = SSM_HEADS // G
    xbc = jax.nn.silu(causal_conv(seg['ssm_xbc'], conv_w, conv_b))
    xs = xbc[..., :SSM_INNER].reshape(B, L, G, R, P)
    Bm = xbc[..., SSM_INNER:SSM_INNER + G * N].reshape(B, L, G, N)
    Cm = xbc[..., SSM_INNER + G * N:].reshape(B, L, G, N)
    dt = jax.nn.softplus(seg['ssm_dt'].astype(jnp.float32) + dt_bias.astype(jnp.float32))
    A = -jnp.exp(A_log.astype(jnp.float32))
    y = ssd_chunked(xs, dt, A, Bm, Cm, SSM_CHUNK)
    y = y + D_skip.astype(jnp.float32).reshape(G, R)[:, :, None] * xs.astype(jnp.float32)
    y = y.reshape(B, L, SSM_INNER).astype(seg['ssm_z'].dtype)
    return rmsnorm(y * jax.nn.silu(seg['ssm_z']), norm_g)

def hier_moe(h, w_grp, w_exp, w_gate, w_up, w_down):
    B, L, D = h.shape
    T = B * L
    ht = h.reshape(T, D)
    grp_p = jax.nn.softmax((ht @ w_grp).astype(jnp.float32), axis=-1)
    g_w, g_i = lax.top_k(grp_p, 1)
    exp_logits = (ht @ w_exp).astype(jnp.float32).reshape(T, MOE_GROUPS, MOE_EXPERTS_PER_GROUP)
    in_grp = jnp.take_along_axis(exp_logits, g_i[:, :, None], axis=1)[:, 0]
    e_l, e_i = lax.top_k(in_grp, MOE_TOP_K)
    e_w = jax.nn.softmax(e_l, axis=-1) * g_w
    expert_id = g_i * MOE_EXPERTS_PER_GROUP + e_i
    comb = jnp.sum(jax.nn.one_hot(expert_id, MOE_EXPERTS, dtype=jnp.float32) * e_w[..., None], axis=1)
    comb = comb.astype(h.dtype)
    out = jnp.zeros_like(ht)
    for g in range(MOE_GROUPS):
        sl = slice(g * MOE_EXPERTS_PER_GROUP, (g + 1) * MOE_EXPERTS_PER_GROUP)
        a = jnp.einsum('td,edf->tef', ht, w_gate[sl])
        u = jnp.einsum('td,edf->tef', ht, w_up[sl])
        out = out + jnp.einsum('tef,efd,te->td', jax.nn.silu(a) * u, w_down[sl], comb[:, sl])
    return out.reshape(B, L, D)

def setup_inputs(seed: int = 0) -> dict:
    key = jax.random.key(seed)
    ks = jax.random.split(key, 31)
    f32 = jnp.float32

    def nrm(k, shape, scale):
        return jax.random.normal(k, shape, f32) * scale

    def gain(k, shape):
        return 1.0 + 0.01 * jax.random.normal(k, shape, f32)

    cmp_in = NSA_CMP_LEN * NSA_HEAD_DIM
    dt0 = jnp.exp(jax.random.uniform(ks[16], (DEPTH, SSM_HEADS), f32,
                                     minval=math.log(1e-3), maxval=math.log(1e-1)))
    return {
        'x': nrm(ks[0], (BATCH, SEQ, D_MODEL), 1.0),
        'p': nrm(ks[1], (DEPTH, BATCH, SEQ, PLE_DIM), 1.0),
        'w_in': nrm(ks[2], (DEPTH, D_MODEL, IN_WIDTH), D_MODEL ** -0.5),
        'g_mix': gain(ks[3], (DEPTH, D_MODEL)),
        'attn_sinks': nrm(ks[4], (DEPTH, SWA_HEADS), 0.5),
        'hgrn_lower_bounds': nrm(ks[5], (DEPTH, HGRN_HEADS * HGRN_KEY_DIM), 0.1),
        'hgrn_norm_g': gain(ks[6], (DEPTH, HGRN_HEADS * HGRN_VAL_DIM)),
        'nsa_pos_k': nrm(ks[7], (DEPTH, NSA_CMP_LEN, NSA_HEAD_DIM), 0.1),
        'nsa_pos_v': nrm(ks[8], (DEPTH, NSA_CMP_LEN, NSA_HEAD_DIM), 0.1),
        'nsa_cmp_w1_k': nrm(ks[9], (DEPTH, cmp_in, NSA_CMP_HIDDEN), cmp_in ** -0.5),
        'nsa_cmp_w2_k': nrm(ks[10], (DEPTH, NSA_CMP_HIDDEN, NSA_HEAD_DIM), NSA_CMP_HIDDEN ** -0.5),
        'nsa_cmp_w1_v': nrm(ks[11], (DEPTH, cmp_in, NSA_CMP_HIDDEN), cmp_in ** -0.5),
        'nsa_cmp_w2_v': nrm(ks[12], (DEPTH, NSA_CMP_HIDDEN, NSA_HEAD_DIM), NSA_CMP_HIDDEN ** -0.5),
        'ssm_conv_w': nrm(ks[13], (DEPTH, SSM_CONV, SSM_CONV_DIM), SSM_CONV ** -0.5),
        'ssm_conv_b': nrm(ks[14], (DEPTH, SSM_CONV_DIM), 0.01),
        'ssm_dt_bias': dt0 + jnp.log(-jnp.expm1(-dt0)),
        'ssm_A_log': jnp.log(jax.random.uniform(ks[15], (DEPTH, SSM_HEADS), f32, minval=1.0, maxval=16.0)),
        'ssm_D': gain(ks[17], (DEPTH, SSM_HEADS)),
        'ssm_norm_g': gain(ks[18], (DEPTH, SSM_INNER)),
        'w_branch': nrm(ks[19], (DEPTH, N_BRANCH, BRANCH_WIDTH, D_MODEL), BRANCH_WIDTH ** -0.5),
        'w_out': nrm(ks[20], (DEPTH, D_MODEL, D_MODEL), D_MODEL ** -0.5),
        'g_ffn': gain(ks[21], (DEPTH, D_MODEL)),
        'w_router_grp': nrm(ks[22], (DEPTH, D_MODEL, MOE_GROUPS), D_MODEL ** -0.5),
        'w_router_exp': nrm(ks[23], (DEPTH, D_MODEL, MOE_EXPERTS), D_MODEL ** -0.5),
        'w_exp_gate': nrm(ks[24], (DEPTH, MOE_EXPERTS, D_MODEL, MOE_FF), D_MODEL ** -0.5),
        'w_exp_up': nrm(ks[25], (DEPTH, MOE_EXPERTS, D_MODEL, MOE_FF), D_MODEL ** -0.5),
        'w_exp_down': nrm(ks[26], (DEPTH, MOE_EXPERTS, MOE_FF, D_MODEL), MOE_FF ** -0.5),
        'g_ple': gain(ks[27], (DEPTH, D_MODEL)),
        'w_ple_gate': nrm(ks[28], (DEPTH, D_MODEL, D_MODEL), D_MODEL ** -0.5),
        'w_ple_proj': nrm(ks[29], (DEPTH, PLE_DIM, D_MODEL), PLE_DIM ** -0.5),
        'g_final': gain(ks[30], (D_MODEL,)),
    }

def reference(x, p, w_in, g_mix, attn_sinks, hgrn_lower_bounds, hgrn_norm_g,
              nsa_pos_k, nsa_pos_v, nsa_cmp_w1_k, nsa_cmp_w2_k, nsa_cmp_w1_v, nsa_cmp_w2_v,
              ssm_conv_w, ssm_conv_b, ssm_dt_bias, ssm_A_log, ssm_D, ssm_norm_g,
              w_branch, w_out, g_ffn, w_router_grp, w_router_exp,
              w_exp_gate, w_exp_up, w_exp_down, g_ple, w_ple_gate, w_ple_proj, g_final):
    B, L, D = x.shape
    swa_slopes = alibi_slopes(SWA_HEADS)
    nsa_slopes = alibi_slopes(NSA_HEADS)
    sm = jax.nn.softmax(hgrn_lower_bounds.astype(jnp.float32), axis=0)
    lbs = jnp.cumsum(sm, axis=0) - sm[0:1]
    for i in range(DEPTH):
        h = rmsnorm(x, g_mix[i])
        seg = split_proj(h @ w_in[i])
        y_a = swa_mixer(seg, attn_sinks[i], swa_slopes)
        y_b = hgrn2_mixer(seg, lbs[i], hgrn_norm_g[i])
        y_c = nsa_mixer(seg, nsa_pos_k[i], nsa_pos_v[i], nsa_cmp_w1_k[i], nsa_cmp_w2_k[i],
                        nsa_cmp_w1_v[i], nsa_cmp_w2_v[i], nsa_slopes)
        y_d = mamba2_mixer(seg, ssm_conv_w[i], ssm_conv_b[i], ssm_dt_bias[i], ssm_A_log[i],
                           ssm_D[i], ssm_norm_g[i])
        ys = jnp.stack([y_a, y_b, y_c, y_d], axis=0)
        yp = jnp.einsum('nblc,nce->nble', ys, w_branch[i])
        gates = jax.nn.sigmoid(seg['merge_gate'].reshape(B, L, N_BRANCH, D))
        u = jnp.einsum('blne,nble->ble', gates, yp)
        x = x + u @ w_out[i]
        x = x + hier_moe(rmsnorm(x, g_ffn[i]), w_router_grp[i], w_router_exp[i],
                         w_exp_gate[i], w_exp_up[i], w_exp_down[i])
        ple_gate = jax.nn.sigmoid(rmsnorm(x, g_ple[i]) @ w_ple_gate[i])
        x = x + (p[i] @ w_ple_proj[i]) * ple_gate
    return rmsnorm(x, g_final)


_drawn_inputs = setup_inputs


def setup_inputs(seed=0):
    import zlib

    import numpy as np

    out = dict(_drawn_inputs(seed))
    spreads = {}
    factors = {'g_mix': 4.073,
     'attn_sinks': 51.311,
     'hgrn_norm_g': 4.693,
     'nsa_pos_k': 8.0,
     'ssm_conv_b': 34.12,
     'ssm_D': 200.0,
     'ssm_norm_g': 9.84,
     'g_ffn': 3.717,
     'g_ple': 200.0,
     'g_final': 170.116,
     'nsa_pos_v': 8.0}
    for name, (base, spread) in spreads.items():
        noise = np.random.default_rng([zlib.crc32(name.encode()), seed]).standard_normal(out[name].shape)
        drawn = base * np.exp(spread * noise) if base else spread * noise
        out[name] = __import__('jax').numpy.asarray(drawn.astype(out[name].dtype))
    for name, factor in factors.items():
        out[name] = (out[name] * factor).astype(out[name].dtype)
    return out
```

```python
from contextlib import ExitStack

import concourse.bass as bass
import numpy as np
from concourse import mybir

F32 = mybir.dt.float32
ALU = mybir.AluOpType
ACT = mybir.ActivationFunctionType
X = mybir.AxisListType.X

P = 128
T = 256
QT = T // P
D = 1024
KD = D // P
HEADS, HD = 8, 64
CMP_LEN, CMP_STRIDE = 32, 16
N_CMP = (T - CMP_LEN) // CMP_STRIDE + 1
CMP_PAIRS = CMP_LEN // 2
H_HEADS, H_CHUNK, H_NC = 4, 32, T // 32
S_CHUNK = 64
GROUPS, EXPERTS, FF = 4, 32, 256
EPG = EXPERTS // GROUPS
PLE = 256
EPS = 1e-6
NEG = -1e30
GELU_A, GELU_B = 0.7978845608028654, 0.044715

SWA_Q, SWA_KV, H_Q, H_F, H_I, H_G, NSA_Q = 0, 512, 768, 1280, 1792, 2304, 2816
NSA_KV, NSA_GATE, SSM_Z, SSM_X, SSM_DT, MERGE = 3328, 4096, 4120, 4632, 5400, 5408

SLOTS = 3
SLOT = KD * 776

C_ID, C_TRI64, C_BLK64, C_TRI32 = 0, 128, 256, 384
C_CM32, C_CM64, C_SCAN, C_CBIAS = 512, 516, 518, 774
C_CVALID = C_CBIAS + HEADS * QT * N_CMP
C_IOTA = C_CVALID + QT * N_CMP
C_BIAS = C_IOTA + EXPERTS
C_ALL = C_BIAS + HEADS * 3 * P

V_GMIX, V_GPLE, V_GH, V_GS, V_CB, V_CW, V_LB, V_PK, V_PV, V_ALL = 0, 8, 16, 20, 24, 30, 54, 58, 74, 90


def shape_constants():
    c = np.zeros((P, C_ALL), np.float32)
    i, j = np.arange(P)[:, None], np.arange(P)[None, :]
    c[:, C_ID:C_ID + P] = i == j
    c[:, C_TRI64:C_TRI64 + P] = (i <= j) & (i // S_CHUNK == j // S_CHUNK)
    c[:, C_BLK64:C_BLK64 + P] = i // S_CHUNK == j // S_CHUNK
    c[:, C_TRI32:C_TRI32 + P] = (i <= j) & (i // H_CHUNK == j // H_CHUNK)
    c[:, C_CM32:C_CM32 + 4] = i // H_CHUNK == np.arange(4)[None, :]
    c[:, C_CM64:C_CM64 + 2] = i // S_CHUNK == np.arange(2)[None, :]
    c[:, C_SCAN:C_SCAN + T] = np.arange(T)[None, :] % H_CHUNK != 0
    slopes = 2.0 ** (-8.0 * np.arange(1, HEADS + 1) / HEADS)
    end = np.arange(N_CMP) * CMP_STRIDE + CMP_LEN - 1
    pos = np.arange(T).reshape(QT, P).T
    dist = (pos[:, :, None] - end[None, None, :]).astype(np.float32)
    cb = np.where(dist[:, None] >= 0, -slopes[None, :, None, None] * dist[:, None], NEG)
    c[:, C_CBIAS:C_CVALID] = cb.reshape(P, -1)
    c[:, C_CVALID:C_IOTA] = (dist >= 0).reshape(P, -1)
    c[:, C_IOTA:C_BIAS] = np.arange(EXPERTS)[None, :]
    for h in range(HEADS):
        at = C_BIAS + h * 3 * P
        c[:, at:at + P] = np.where(j <= i, -slopes[h] * (i - j), NEG)
        c[:, at + P:at + 2 * P] = np.where(j > i, -slopes[h] * (i - j + P), NEG)
        c[:, at + 2 * P:at + 3 * P] = -slopes[h] * (i - j + P)
    return c


class Count:

    def __init__(self, sem):
        self.sem, self.n = sem, 0

    def on(self, ins):
        ins.then_inc(self.sem, 1)
        self.n += 1
        return self.n


def hybrid_layer(nc, a):
    ctx = ExitStack()
    with ctx:
        def sb(name, n):
            return ctx.enter_context(nc.sbuf_tensor("s_" + name, [P, n], F32))

        def sem(name):
            return ctx.enter_context(nc.semaphore(name))

        w_in = a["w_in"][0].rearrange("(c p) n -> p c n", p=P)
        w_branch = a["w_branch"][0]
        w_out = a["w_out"][0].rearrange("(c p) n -> p c n", p=P)
        x_dram = a["x"][0].rearrange("(q p) d -> p q d", p=P)
        out_dram = a["out"][0].rearrange("(q p) d -> p q d", p=P)
        p_dram = a["p"][0, 0].rearrange("(q p) d -> p q d", p=P)

        ring = [sb(f"wslot{i}", SLOT) for i in range(SLOTS)]
        x = sb("x", QT * D)
        xn = sb("xn", QT * D)
        hT = sb("hT", KD * T)
        cst = sb("cst", C_ALL)
        vrows = sb("vrows", P)
        vec = sb("vec", V_ALL)
        kv_swa, kv_slc, kv_win = sb("kv_swa", 768), sb("kv_slc", 768), sb("kv_win", 768)
        q_swa, q_nsa = sb("q_swa", 1024), sb("q_nsa", 1024)
        kc_raw, vc_raw = sb("kc_raw", 512), sb("vc_raw", 512)
        gate_raw, dt_raw = sb("gate_raw", QT * 24), sb("dt_raw", QT * 8)
        z_seg = sb("z_seg", 1024)
        hq, hf, hi, hg = sb("hq", 1024), sb("hf", 1024), sb("hi", 1024), sb("hg", 1024)
        xbc = sb("xbc", 1536)
        yT_a, yT_c = sb("yT_a", 1024), sb("yT_c", 1024)
        small = sb("small", 512)
        work = sb("work", 8064)

        so = [0]

        def sm(n):
            v = small[:, so[0]:so[0] + n]
            so[0] += n
            assert so[0] <= 512
            return v

        wo = [0]

        def wk(n, at=None):
            if at is not None:
                wo[0] = at
            v = work[:, wo[0]:wo[0] + n]
            wo[0] += n
            assert wo[0] <= 8064, wo[0]
            return v

        ident = cst[:, C_ID:C_ID + P]
        tri64, blk64 = cst[:, C_TRI64:C_TRI64 + P], cst[:, C_BLK64:C_BLK64 + P]
        tri32 = cst[:, C_TRI32:C_TRI32 + P]
        cm32, cm64 = cst[:, C_CM32:C_CM32 + 4], cst[:, C_CM64:C_CM64 + 2]
        scan_keep = cst[:, C_SCAN:C_SCAN + T]
        cbias = cst[:, C_CBIAS:C_CVALID].rearrange("p (h q c) -> p h q c", h=HEADS, q=QT)
        cvalid = cst[:, C_CVALID:C_IOTA].rearrange("p (q c) -> p q c", q=QT)
        iota = cst[:, C_IOTA:C_BIAS]
        bias = cst[:, C_BIAS:C_ALL].rearrange("p (g j b k) -> p g j b k", g=2, j=4, b=3)

        xv = x[:, :].rearrange("p (q d) -> p q d", q=QT)
        xnv = xn[:, :].rearrange("p (q d) -> p q d", q=QT)
        hTv = hT[:, :].rearrange("p (c t) -> p c t", c=KD)
        yT_b, yT_d = q_swa, q_nsa
        uT = cst[:, C_BIAS:C_BIAS + KD * T]
        spare = cst[:, C_BIAS + KD * T:C_ALL]

        sc = wk(768, 0).rearrange("p (u k) -> p u k", u=2)
        pT = wk(768).rearrange("p (u k) -> p u k", u=2)
        kcP = wk(480).rearrange("p (g l c) -> p g l c", g=2, l=CMP_PAIRS)
        vcP = wk(480).rearrange("p (g l c) -> p g l c", g=2, l=CMP_PAIRS)
        hid = wk(256).rearrange("p (v h g c) -> p v h g c", v=2, h=2, g=2)
        hidx, hidg = wk(120), wk(120)
        kcZ = wk(2 * N_CMP).rearrange("p (g c) -> p g c", g=2)
        vcZ = wk(512).rearrange("p (g r d) -> p g r d", g=2, r=4)
        cs = wk(240).rearrange("p (h q c) -> p h q c", h=8, q=2)
        csP = wk(512).rearrange("p (q g r c) -> p q g r c", q=2, g=2, r=4)
        csT = wk(512).rearrange("p (g t) -> p g t", g=2)
        w2k, w2v = wk(128).rearrange("p (c d) -> p c d", c=2), wk(128).rearrange("p (c d) -> p c d", c=2)

        h_k, h_b = xn[:, 0:1024], xn[:, 1024:2048]
        t1, t4 = wk(256, 0), wk(256)
        e1, e2, e3, e4 = wk(256), wk(256), wk(256), wk(256)
        qq, kk, kkL, kd = wk(256), wk(256), wk(256), wk(256)
        qe = [wk(256), wk(256)]
        hS = wk(7 * P).rearrange("p (c v) -> p c v", c=7)
        Am = wk(256).rearrange("p (q t) -> p q t", q=2)
        kdT = wk(256).rearrange("p (q k) -> p q k", q=2)
        iB = wk(1024).rearrange("p (q c v) -> p q c v", q=2, c=4)
        osb = wk(1024).rearrange("p (q h v) -> p q h v", q=2, h=4)
        conv_at = wo[0]
        conv = wk(1536)
        square_junk = vrows[:, :]

        BZ = wk(512, 0).rearrange("p (g t) -> p g t", g=2)
        Lb = wk(1024).rearrange("p (h t) -> p h t", h=8)
        Lm = wk(1024).rearrange("p (h t) -> p h t", h=8)
        xwB = wk(1024).rearrange("p (c h n) -> p c h n", c=2, h=8)
        sS = wk(2048).rearrange("p (c n) -> p c n", c=4)
        assert wo[0] <= conv_at
        CBm = kv_slc[:, 0:512].rearrange("p (q g t) -> p q g t", q=2, g=2)
        Btok = kv_win[:, 0:256].rearrange("p (q n) -> p q n", q=2)
        xtok = hq[:, :].rearrange("p (q h n) -> p q h n", q=2, h=8)
        xdt = hi[:, :].rearrange("p (q h n) -> p q h n", q=2, h=8)
        yd = hg[:, :].rearrange("p (q n) -> p q n", q=2)
        ytmp = hf[:, :].rearrange("p (a h n) -> p a h n", a=2, h=8)
        conv_th = [q_nsa[:, 0:512], q_nsa[:, 512:1024], kc_raw[:, :]]
        z_th = spare
        g_th = q_nsa[:, :]

        gth = [sb("gth0", 512), sb("gth1", 512)]

        ps = ctx.enter_context(nc.psum_tensor("ps", [P, 8, 512], F32))

        ssq, ms, rms, rstd = sm(2), sm(2), sm(2), sm(2)
        negm, esum, rr, es = sm(4), sm(4), sm(4), sm(4)
        sinks, nsinks = sm(8), sm(8)
        gsig = sm(QT * 24)
        lb, olb, lbt, lbr = sm(4), sm(4), sm(4), sm(4)
        vgh = sm(4)
        hdec = [sm(8), sm(8)]
        hssq, hms, hrms, hrstd = sm(8), sm(8), sm(8), sm(8)
        cmx, csum = sm(16), sm(16)
        alog, dtb, dskip = sm(8), sm(8), sm(8)
        dtr, dta, dtm, dt, dtA = sm(16), sm(16), sm(16), sm(16), sm(16)
        acs, sdec, eacs, swt = sm(32), sm(16), sm(16), sm(16)
        swB = sm(32)
        cdec = sm(16)
        sssq, sms, srms, srstd = sm(2), sm(2), sm(2), sm(2)
        assert so[0] <= 512, so[0]

        comb = z_seg[:, 0:QT * EXPERTS]
        wr = hq[:, 0:KD * 36]
        actT = [hf[:, 0:512], hf[:, 512:1024]]
        sil = [hi[:, 0:512], hi[:, 512:1024]]
        rt = hg[:, :]
        gf = xbc[:, 0:1024]
        gffn = z_seg[:, 64:72]
        pT_ple = q_nsa[:, 0:512]
        p_tok = q_swa[:, 0:512]

        ld_cmp, ld_vec, ld_cst, ld_bias, ld_small = sem("ld_cmp"), sem("ld_vec"), sem("ld_cst"), sem("ld_bias"), sem("ld_small")
        ld_x = [sem("ld_x0"), sem("ld_x1")]
        ld_moe, ld_p = sem("ld_moe"), sem("ld_p")
        ld_w = [sem(f"ld_w{i}") for i in range(SLOTS)]
        dve_step, act_step, pool_step = sem("dve_step"), sem("act_step"), sem("pool_step")
        ssq_done, ms_done, sqrt_done = sem("ssq_done"), sem("ms_done"), sem("sqrt_done")
        xn_done, xT_done, hT_done = sem("xn_done"), sem("xT_done"), sem("hT_done")
        vec_t, vec_ready, zeroed = sem("vec_t"), sem("vec_ready"), sem("zeroed")
        proj_done, seg_ready = sem("proj_done"), sem("seg_ready")
        scores_done, max_done, sink_ready = sem("scores_done"), sem("max_done"), sem("sink_ready")
        exp_done, prob_done = sem("exp_done"), sem("prob_done")
        pT_done, pT_copied, pv_done, y_copied = sem("pT_done"), sem("pT_copied"), sem("pv_done"), sem("y_copied")
        gate_tanh = sem("gate_tanh")
        cmp_in, cmp_hid, cmp_gel, cmp_tanh, cmp_hready = (
            sem("cmp_in"), sem("cmp_hid"), sem("cmp_gel"), sem("cmp_tanh"), sem("cmp_hready"))
        cmp_kv, cmp_kvc, cmp_sc, cmp_sub, cmp_exp, cmp_p, cmp_pT, cmp_pTc = (
            sem("cmp_kv"), sem("cmp_kvc"), sem("cmp_sc"), sem("cmp_sub"), sem("cmp_exp"), sem("cmp_p"),
            sem("cmp_pT"), sem("cmp_pTc"))
        h_arg, h_exp, h_f, h_log, hg_tanh = sem("h_arg"), sem("h_exp"), sem("h_f"), sem("h_log"), sem("hg_tanh")
        h_diff, h_e, h_ops = sem("h_diff"), sem("h_e"), sem("h_ops")
        h_A, h_Am, h_U, h_S, h_O, h_osb, h_iB, h_sq = (
            sem("h_A"), sem("h_Am"), sem("h_U"), sem("h_S"), sem("h_O"), sem("h_osb"), sem("h_iB"), sem("h_sq"))
        h_ms, h_rms, h_y, h_yT, h_yTc = sem("h_ms"), sem("h_rms"), sem("h_y"), sem("h_yT"), sem("h_yTc")
        dt_arg, dt_log, s_conv, s_tanh, s_silu = sem("dt_arg"), sem("dt_log"), sem("s_conv"), sem("s_tanh"), sem("s_silu")
        s_X, s_Xcopy, s_acs, s_dec, s_B, s_Larg, s_Lexp, s_L = (
            sem("s_X"), sem("s_Xcopy"), sem("s_acs"), sem("s_dec"), sem("s_B"), sem("s_Larg"), sem("s_Lexp"), sem("s_L"))
        s_Y, s_state, s_off, s_y, s_sq, s_ms, s_rms, s_n, s_yT, s_yTc = (
            sem("s_Y"), sem("s_state"), sem("s_off"), sem("s_y"), sem("s_sq"), sem("s_ms"), sem("s_rms"), sem("s_n"),
            sem("s_yT"), sem("s_yTc"))
        g_done, g_tanh, yp_done, u_done = sem("g_done"), sem("g_tanh"), sem("yp_done"), sem("u_done")
        wo_done, x2_done = sem("wo_done"), sem("x2_done")
        rt_done, rt_sub, rt_exp, rt_d, rt_e = sem("rt_done"), sem("rt_sub"), sem("rt_exp"), sem("rt_d"), sem("rt_e")
        gu_done, silu_done, act_done, down_done, acc_free = (
            sem("gu_done"), sem("silu_done"), sem("act_done"), sem("down_done"), sem("acc_free"))
        ple_T, ple_Tc, ple_p, ple_g, ple_tanh, x4_done = (
            sem("ple_T"), sem("ple_Tc"), sem("ple_p"), sem("ple_g"), sem("ple_tanh"), sem("x4_done"))
        out_done, o_dma = sem("out_done"), sem("o_dma")

        def cols(c0, n):
            return [(0, KD * n, w_in[:, :, c0:c0 + n])]

        def pair_cols(c0):
            return [(g * HD, w_in[:, :, c0 + g * 256:c0 + (g + 1) * 256]) for g in range(2)]

        items = []

        def item(name, parts, freed_by, count):
            items.append((name, parts, freed_by, count))

        item("swa", [("pairs", 768, v) for v in pair_cols(SWA_Q)] + [("plain", 768, (512, w_in[:, :, SWA_KV:SWA_KV + 256]))], proj_done, 3)
        item("gz", cols(NSA_GATE, 536), proj_done, 6)
        item("nkv", cols(NSA_KV, 768), proj_done, 10)
        item("nq", [("pairs", 512, v) for v in pair_cols(NSA_Q)], proj_done, 12)
        item("w1k", [(0, 4096, a["nsa_cmp_w1_k"][0].rearrange("(c p) n -> p c n", p=P))], cmp_hid, 1)
        item("w1v", [(0, 4096, a["nsa_cmp_w1_v"][0].rearrange("(c p) n -> p c n", p=P))], cmp_hid, 2)
        item("hq", cols(H_Q, 512), proj_done, 14)
        item("hf", cols(H_F, 512), proj_done, 16)
        item("hi", cols(H_I, 512), proj_done, 18)
        item("hg", cols(H_G, 512), proj_done, 20)
        item("xd", cols(SSM_X, 776), proj_done, 24)
        ORDER = (0, 2, 1, 3)
        for ni, n in enumerate(ORDER):
            if n in (0, 2):
                wb = w_branch[n].rearrange("(g j d) e -> g d j e", g=2, d=HD)
                parts = [(0, 4096, wb[0], 0), (0, 4096, wb[1], HD)]
            else:
                parts = [(0, 4096, w_branch[n].rearrange("(c p) e -> p c e", p=P))]
            item(f"g{n}0", cols(MERGE + n * D, 512), g_done, 4 * ni + 2)
            item(f"b{n}", parts, yp_done, 4 * ni + 4)
            item(f"g{n}1", cols(MERGE + n * D + 512, 512), g_done, 4 * ni + 4)
        item("wo0", [(0, 4096, w_out[:, :, 0:512])], wo_done, 3)
        item("wo1", [(0, 4096, w_out[:, :, 512:1024])], wo_done, 4)

        landed, slot_of = {}, {}
        count = [0] * SLOTS
        for i, (name, parts, *_) in enumerate(items):
            count[i % SLOTS] += 16 * sum(KD if part[0] == "pairs" else 1 for part in parts)
            landed[name], slot_of[name] = count[i % SLOTS], i % SLOTS

        def weights(name, c, n):
            return ring[slot_of[name]][:, 0:c * n].rearrange("p (c n) -> p c n", c=c)

        def arrived(eng, name):
            eng.wait_ge(ld_w[slot_of[name]], landed[name])

        GRP = []
        for half in range(2):
            GRP.append(("q_swa", "swa", 768, [("headpair", 2 * half + i, 0) for i in range(2)]))
        GRP.append(("kv_swa", "swa", 768, [("feat", 512, 128), ("tok", 640, 128)]))
        GRP.append(("gate", "gz", 536, [("tok", 0, 24)]))
        for q in range(2):
            GRP.append((f"z{q}", "gz", 536, [("tokq", 24, 512, q)]))
        GRP.append(("kc", "nkv", 768, [("feat", 0, 128)]))
        GRP.append(("vc", "nkv", 768, [("feat", 128, 128)]))
        GRP.append(("kv_slc", "nkv", 768, [("feat", 256, 128), ("tok", 384, 128)]))
        GRP.append(("kv_win", "nkv", 768, [("feat", 512, 128), ("tok", 640, 128)]))
        for half in range(2):
            GRP.append(("q_nsa", "nq", 512, [("headpair", 2 * half + i, 0) for i in range(2)]))
        for nm in ("hq", "hf"):
            for half in range(2):
                GRP.append((nm, nm, 512, [("feat", (2 * half + i) * P, P) for i in range(2)]))
        for nm in ("hi", "hg"):
            for q in range(2):
                GRP.append((nm, nm, 512, [("tokq", 0, 512, q)]))
        for k in range(3):
            GRP.append(("xbc", "xd", 776, [("feat", (2 * k + i) * P, P) for i in range(2)]))
        GRP.append(("dt", "xd", 776, [("tok", 768, 8)]))
        NG = len(GRP)
        assert NG == 24


        def e_slot(e):
            return (len(items) + e) % SLOTS

        def e_landed(e):
            return count[e_slot(e)] + 48 * (e // SLOTS + 1)

        ple_slot = [e_slot(EXPERTS + k) for k in range(3)]
        ple_landed = [e_landed(EXPERTS + k) - 32 for k in range(3)]

        lg = rt[:, 0:72]
        gexp, gm, m1, m2, mn = rt[:, 72:80], rt[:, 80:82], rt[:, 82:84], rt[:, 84:86], rt[:, 86:88]
        gw, e21, w1, w2 = rt[:, 88:90], rt[:, 90:92], rt[:, 92:94], rt[:, 94:96]
        goh = rt[:, 96:104].rearrange("p (q n) -> p q n", q=2)
        gpen = rt[:, 104:112].rearrange("p (q n) -> p q n", q=2)
        iom = rt[:, 128:160]
        cand = rt[:, 160:224].rearrange("p (q n) -> p q n", q=2)
        vmask = rt[:, 224:288].rearrange("p (q n) -> p q n", q=2)
        oh1 = rt[:, 288:352].rearrange("p (q n) -> p q n", q=2)
        oh2 = rt[:, 352:416].rearrange("p (q n) -> p q n", q=2)

        SLOT_LIST = [("swa", kv_swa, q_swa, j, 0) for j in range(4)]
        for j in range(4):
            SLOT_LIST += [("slc", kv_slc, q_nsa, j, 1), ("win", kv_win, q_nsa, j, 2)]
        NS = len(SLOT_LIST)
        SLOT_GROUPS = [[3, 4], [5, 6], [7, 8], [9, 10]] + [[12 + i] for i in range(8)]

        def tile_of(s):
            if s < 4:
                return s, True, True
            return 4 + (s - 4) // 2, s % 2 == 0, s % 2 == 1

        block = ctx.enter_context(nc.Block())

        @block.sync
        def _(sp):
            def load(i):
                name, parts, _, _ = items[i]
                if i >= SLOTS:
                    sp.wait_ge(items[i - SLOTS][2], items[i - SLOTS][3])
                for part in parts:
                    if part[0] in ("pairs", "plain"):
                        kind, width, (at, src) = part
                        wide = ring[i % SLOTS][:, 0:KD * width].rearrange("p (c n) -> p c n", c=KD)
                        if kind == "pairs":
                            for c in range(KD):
                                dst = wide[:, c, 0:512].rearrange("p (j h d) -> p j h d", j=4, h=2)[:, :, at // HD, :]
                                sp.dma_start(dst, src[:, c, :].rearrange("p (j d) -> p j d", j=4)).then_inc(ld_w[i % SLOTS], 16)
                        else:
                            sp.dma_start(wide[:, :, at:at + src.shape[2]], src).then_inc(ld_w[i % SLOTS], 16)
                        continue
                    at, n, src = part[:3]
                    p0 = part[3] if len(part) > 3 else 0
                    np_, c, w = src.shape
                    dst = ring[i % SLOTS][p0:p0 + np_, at:at + n].rearrange("p (c n) -> p c n", c=c)
                    sp.dma_start(dst, src).then_inc(ld_w[i % SLOTS], 16)

            def rows(at, src, n):
                sp.dma_start(vrows[at:at + n, :], src).then_inc(ld_vec, 16)

            for q in range(QT):
                sp.dma_start(xv[:, q, :], x_dram[:, q, :]).then_inc(ld_x[q], 16)
            sp.dma_start(cst[:, 0:C_BIAS], a["cst"][:, 0:C_BIAS]).then_inc(ld_cst, 16)
            rows(V_GMIX, a["g_mix"][0].rearrange("(c p) -> c p", p=P), 8)
            rows(V_GPLE, a["g_ple"][0].rearrange("(c p) -> c p", p=P), 8)
            rows(V_GH, a["hgrn_norm_g"][0].rearrange("(c p) -> c p", p=P), 4)
            rows(V_GS, a["ssm_norm_g"][0].rearrange("(c p) -> c p", p=P), 4)
            rows(V_CB, a["ssm_conv_b"][0].rearrange("(c p) -> c p", p=P), 6)
            rows(V_CW, a["ssm_conv_w"][0].rearrange("j (c p) -> (j c) p", p=P), 24)
            rows(V_LB, a["hgrn_lower_bounds"][0].rearrange("(c p) -> c p", p=P), 4)
            rows(V_PK, a["nsa_pos_k"][0].rearrange("(l m) d -> l (m d)", m=2), 16)
            rows(V_PV, a["nsa_pos_v"][0].rearrange("(l m) d -> l (m d)", m=2), 16)
            load(0)
            for dst, src in ((sinks, "attn_sinks"), (alog, "ssm_A_log"), (dtb, "ssm_dt_bias"), (dskip, "ssm_D")):
                sp.dma_start(dst, a[src][0].partition_broadcast(P)).then_inc(ld_small, 16)
            load(1)
            sp.dma_start(cst[:, C_BIAS:C_ALL], a["cst"][:, C_BIAS:C_ALL]).then_inc(ld_bias, 16)
            sp.dma_start(w2k, a["nsa_cmp_w2_k"][0].rearrange("(c p) d -> p c d", p=P)).then_inc(ld_cmp, 16)
            sp.dma_start(w2v, a["nsa_cmp_w2_v"][0].rearrange("(c p) d -> p c d", p=P)).then_inc(ld_cmp, 16)
            for i in range(2, len(items)):
                load(i)

            sp.wait_ge(s_yTc, 2)
            wrv = wr.rearrange("p (c n) -> p c n", c=KD)
            sp.dma_start(wrv[:, :, 0:GROUPS], a["w_router_grp"][0].rearrange("(p c) n -> p c n", c=KD)).then_inc(ld_moe, 16)
            sp.dma_start(wrv[:, :, GROUPS:36], a["w_router_exp"][0].rearrange("(p c) n -> p c n", c=KD)).then_inc(ld_moe, 16)
            sp.dma_start(gffn, a["g_ffn"][0].rearrange("(p c) -> p c", c=KD)).then_inc(ld_moe, 16)
            sp.dma_start(gf, a["g_final"].partition_broadcast(P)).then_inc(ld_moe, 16)
            sp.wait_ge(yp_done, 16)
            sp.dma_start(p_tok.rearrange("p (q n) -> p q n", q=2), p_dram).then_inc(ld_p, 16)

            def load_expert(e, slot):
                dst = ring[slot]
                for at, src in ((0, w_gate), (2048, w_up), (4096, w_down)):
                    sp.dma_start(dst[:, at:at + 2048], src[e]).then_inc(ld_w[slot], 16)

            w_gate = a["w_exp_gate"][0].rearrange("e (p c) n -> e p (c n)", c=KD)
            w_up = a["w_exp_up"][0].rearrange("e (p c) n -> e p (c n)", c=KD)
            w_down = a["w_exp_down"][0].rearrange("e (p c) n -> e p (c n)", c=2)
            for e in range(SLOTS):
                before = items[len(items) - SLOTS + e]
                sp.wait_ge(before[2], before[3])
                load_expert(e, e_slot(e))
            with sp.Fori(0, 9) as it:
                for k in range(SLOTS):
                    sp.wait_ge(down_done, it * SLOTS + (k + 1))
                    load_expert(bass.ds(it * SLOTS + (k + SLOTS), 1), e_slot(k))
            for e in (30, 31):
                sp.wait_ge(down_done, e - 2)
                load_expert(e, e_slot(e))
            wp = a["w_ple_proj"][0].rearrange("(c p) n -> p c n", p=P)
            wg = a["w_ple_gate"][0].rearrange("(c p) n -> p c n", p=P)
            for k, src in enumerate((wp, wg[:, :, 0:512], wg[:, :, 512:1024])):
                sp.wait_ge(down_done, 30 + k)
                n = src.shape[1] * src.shape[2]
                sp.dma_start(ring[ple_slot[k]][:, 0:n].rearrange("p (c n) -> p c n", c=src.shape[1]), src)\
                  .then_inc(ld_w[ple_slot[k]], 16)
            for q in range(QT):
                sp.wait_ge(out_done, q + 1)
                sp.dma_start(out_dram[:, q, :], xnv[:, q, :]).then_inc(o_dma, 16)
            sp.wait_ge(o_dma, 32)

        @block.tensor
        def _(pe):
            def mm(out, lhsT, rhs, start, stop):
                return pe.matmul(out, lhsT, rhs, start=start, stop=stop, skip_group_check=True)

            def norm_T(m):
                for k in range(4):
                    for i in range(2):
                        c = 2 * k + i
                        for q in range(QT):
                            pe.wait_ge(xn_done, 2 * m + q + 1)
                            src = xnv[:, q, c:D:KD] if m == 1 else xnv[:, q, c * P:(c + 1) * P]
                            last = pe.transpose(ps[:, k, (i * 2 + q) * P:(i * 2 + q + 1) * P], src, ident)
                    last.then_inc(xT_done, 1)

            pe.wait_ge(ld_vec, 16 * 9)
            pe.wait_ge(ld_cst, 16)
            pe.transpose(ps[:, 6, 0:V_ALL], vrows[0:V_ALL, :], ident[0:V_ALL, 0:V_ALL]).then_inc(vec_t, 1)
            norm_T(0)

            def project(g):
                name, it, width, parts = GRP[g]
                bank = g % 2
                arrived(pe, it)
                if g == 0:
                    pe.wait_ge(hT_done, 4)
                if g >= 2:
                    pe.wait_ge(seg_ready, g - 1)
                w = weights(it, KD, width)
                at = 0
                for part in parts:
                    kind, c0 = part[:2]
                    if kind == "tokq":
                        todo = [(part[2], lambda c: hTv[:, c, part[3] * P:(part[3] + 1) * P],
                                 lambda c: w[:, c, c0:c0 + part[2]])]
                    elif kind == "tok":
                        todo = [(part[2], lambda c, q=q: hTv[:, c, q * P:(q + 1) * P],
                                 lambda c: w[:, c, c0:c0 + part[2]]) for q in range(QT)]
                    elif kind == "headpair":
                        todo = [(T, lambda c: w[:, c, c0 * P:(c0 + 1) * P], lambda c: hTv[:, c, :])]
                    else:
                        todo = [(T, lambda c: w[:, c, c0:c0 + P], lambda c: hTv[:, c, :])]
                    for n, lhsT, rhs in todo:
                        for c in range(KD):
                            last = mm(ps[:, bank, at:at + n], lhsT(c), rhs(c), c == 0, c == KD - 1)
                        at += n
                last.then_inc(proj_done, 1)

            def scores(s):
                _, kv, qs, j, _ = SLOT_LIST[s]
                if s in (0, 4):
                    pe.wait_ge(seg_ready, 3 if s == 0 else 12)
                if s >= 1:
                    pe.wait_ge(max_done, s)
                kZ = kv[:, 0:512].rearrange("p (g t) -> p g t", g=2)
                q0, q1 = qs[:, j * T:j * T + P], qs[:, j * T + P:(j + 1) * T]
                for u in range(2):
                    mm(ps[:, 2 + u, 0:128], q0, kZ[:, u, 0:128], True, True)
                    mm(ps[:, 2 + u, 128:256], q1, kZ[:, u, 128:256], True, True)
                    last = mm(ps[:, 2 + u, 256:384], q1, kZ[:, u, 0:128], True, True)
                last.then_inc(scores_done, 1)

            def weights_T(s):
                pe.wait_ge(prob_done, s + 1)
                if s >= 1:
                    pe.wait_ge(pT_copied, s)
                for u in range(2):
                    for at, src in ((0, 0), (128, 256), (256, 128)):
                        last = pe.transpose(ps[:, 4 + u, at:at + P], sc[:, u, src:src + P], ident)
                last.then_inc(pT_done, 1)

            def pv(s):
                _, kv, _, j, br = SLOT_LIST[s]
                tile, opens, closes = tile_of(s)
                pe.wait_ge(pT_copied, s + 1)
                if opens and tile >= 2:
                    pe.wait_ge(y_copied, tile - 1)
                if s == 3:
                    pe.wait_ge(cmp_gel, 1)
                v = kv[:, 512:768].rearrange("p (q n) -> p q n", q=2)
                bank = 6 + tile % 2
                if closes and s >= 4:
                    if s == 5:
                        pe.wait_ge(cmp_pTc, 1)
                    for u in range(2):
                        mm(ps[HD * u:HD * (u + 1), bank, 0:T], vcZ[:, u, j, :], csT[:, u, :], False, False)
                for u in range(2):
                    out = ps[HD * u:HD * (u + 1), bank, :]
                    mm(out[:, 0:T], v[:, 0, HD * u:HD * (u + 1)], pT[:, u, 0:256], opens, False)
                    last = mm(out[:, P:T], v[:, 1, HD * u:HD * (u + 1)], pT[:, u, 256:384], False, closes)
                last.then_inc(pv_done, 1)

            def compress_hidden():
                pe.wait_ge(cmp_in, 2)
                pe.wait_ge(y_copied, 2)
                for v, (it, src) in enumerate((("w1k", kcP), ("w1v", vcP))):
                    arrived(pe, it)
                    w = weights(it, CMP_PAIRS, 256)
                    for hc in range(2):
                        at = 256 + (v * 2 + hc) * 2 * N_CMP
                        for l in range(CMP_PAIRS):
                            last = mm(ps[:, 7, at:at + 2 * N_CMP], w[:, l, hc * P:(hc + 1) * P],
                                      src[:, :, l, :], l == 0, l == CMP_PAIRS - 1)
                    last.then_inc(cmp_hid, 1)

            def compress_kv():
                pe.wait_ge(cmp_hready, 1)
                pe.wait_ge(ld_cmp, 16 * 2)
                pe.wait_ge(y_copied, 4)
                for g in range(2):
                    for hc in range(2):
                        mm(ps[HD * g:HD * (g + 1), 7, 256:256 + N_CMP], w2k[:, hc, :],
                           hid[:, 0, hc, g, 0:N_CMP], hc == 0, hc == 1)
                for g in range(2):
                    for r in range(4):
                        for hc in range(2):
                            last = mm(ps[32 * r:32 * (r + 1), 7, 384 + HD * g:384 + HD * (g + 1)],
                                      hid[:, 1, hc, g, :], w2v[:, hc, :], hc == 0, hc == 1)
                last.then_inc(cmp_kv, 1)

            def compress_scores():
                pe.wait_ge(cmp_kvc, 1)
                out = ps[:, 7, 256:496].rearrange("p (g j q c) -> p g j q c", g=2, j=4, q=2)
                for j in range(4):
                    for q in range(QT):
                        last = mm(out[:, :, j, q, :], q_nsa[:, j * T + q * P:j * T + (q + 1) * P], kcZ, True, True)
                last.then_inc(cmp_sc, 1)

            def compress_T():
                pe.wait_ge(cmp_p, 1)
                for g in range(2):
                    for q in range(QT):
                        last = pe.transpose(ps[:, 7, g * T + q * P:g * T + (q + 1) * P], csP[:, q, g, :, :], ident)
                last.then_inc(cmp_pT, 1)

            for g in range(3):
                project(g)
            for s in range(NS):
                scores(s)
                if s >= 1:
                    weights_T(s - 1)
                if s == 5:
                    compress_scores()
                if s == 6:
                    compress_T()
                for g in SLOT_GROUPS[s]:
                    project(g)
                if s >= 1:
                    pv(s - 1)
                if s == 3:
                    project(11)
                    compress_hidden()
                if s == 4:
                    compress_kv()
            weights_T(NS - 1)
            project(20)
            pv(NS - 1)
            for g in range(21, 24):
                project(g)

            def hgrn_A(h):
                pe.wait_ge(h_ops, h + 1)
                if h >= 1:
                    pe.wait_ge(h_Am, h)
                for q in range(QT):
                    o = ps[:, 4, q * P:(q + 1) * P].rearrange("p (c a) -> p c a", c=4)
                    c = slice(q * P, (q + 1) * P)
                    qc = qq[:, c].rearrange("p (c a) -> p c a", c=4)
                    mm(o[:, :, 16:32], kk[:, c], qc[:, :, 16:32], True, True)
                    mm(o[:, :, 0:16], kkL[:, c], qc[:, :, 0:16], True, True)
                for q in range(QT):
                    last = pe.transpose(ps[:, 4, (2 + q) * P:(3 + q) * P], kd[:, q * P:(q + 1) * P], ident)
                last.then_inc(h_A, 1)

            def hgrn_U(h):
                pe.wait_ge(h_Am, h + 1)
                pe.wait_ge(h_iB, h + 1)
                if h >= 1:
                    pe.wait_ge(h_S, h)
                mm(ps[:, 5, :], kdT[:, 0, :], iB[:, 0, :, :], True, True)
                mm(ps[:, 6, 0:384], kdT[:, 1, :], iB[:, 1, 0:3, :], True, True).then_inc(h_U, 1)

            def hgrn_O(h):
                pe.wait_ge(h_S, h + 1)
                if h >= 1:
                    pe.wait_ge(h_osb, h)
                for q in range(QT):
                    mm(ps[:, 7, q * P:(q + 1) * P], Am[:, q, :], hi[:, q * 512 + h * P:q * 512 + (h + 1) * P], True, False)
                    for c in range(4):
                        cc = 4 * q + c
                        if cc == 0:
                            continue
                        last = mm(ps[32 * c:32 * (c + 1), 7, q * P:(q + 1) * P], qe[h % 2][:, 32 * cc:32 * (cc + 1)],
                                  hS[:, cc - 1, :], False, c == 3)
                last.then_inc(h_O, 1)

            def hgrn_T():
                pe.wait_ge(h_y, 1)
                for k in range(2):
                    for i in range(2):
                        for q in range(QT):
                            last = pe.transpose(ps[:, 4 + k, (2 * i + q) * P:(2 * i + q + 1) * P],
                                                osb[:, q, 2 * k + i, :], ident)
                    last.then_inc(h_yT, 1)

            def ssd_X():
                pe.wait_ge(s_silu, 2)
                pe.wait_ge(h_yTc, 2)
                for q in range(QT):
                    for k in range(4):
                        pe.transpose(ps[:, 4 + q, k * P:(k + 1) * P], conv[:, k * T + q * P:k * T + (q + 1) * P], ident)
                for q in range(QT):
                    pe.transpose(ps[:, 6, q * P:(q + 1) * P], conv[:, 4 * T + q * P:4 * T + (q + 1) * P], ident)
                for q in range(QT):
                    mm(ps[:, 6, 256 + 8 * q:264 + 8 * q], tri64, dtA[:, 8 * q:8 * q + 8], True, True)
                    last = mm(ps[:, 6, 272 + 8 * q:280 + 8 * q], blk64, dtA[:, 8 * q:8 * q + 8], True, True)
                last.then_inc(s_X, 1)

            def ssd_B(q):
                if q == 0:
                    pe.wait_ge(s_Xcopy, 1)
                    pe.wait_ge(s_acs, 1)
                else:
                    pe.wait_ge(s_state, 1)
                    pe.wait_ge(s_y, 1)
                for h in range(HEADS):
                    mm(ps[:, 4 + h // 4, (h % 4) * P:(h % 4 + 1) * P],
                       dtA[:, 8 * q + h:8 * q + h + 1].to_broadcast([P, P]), tri64, True, True)
                for g in range(2):
                    last = mm(ps[:, 6, g * P:(g + 1) * P], BZ[:, g, q * P:(q + 1) * P],
                              conv[:, 5 * T + q * P:5 * T + (q + 1) * P], True, True)
                last.then_inc(s_B, 1)

            def ssd_Y(q):
                pe.wait_ge(s_L, q + 1)
                for h in range(HEADS):
                    mm(ps[:, 7, h * HD:(h + 1) * HD], Lm[:, h, :], xdt[:, q, h, :], True, True)
                for c in range(2 - q):
                    last = mm(ps[:, 4 + c, :], Btok[:, q, :], xwB[:, c, :, :], True, True)
                last.then_inc(s_Y, 1)

            def ssd_off(q):
                pe.wait_ge(s_state, q + 1)
                for c in range(2):
                    t0 = 5 * T + (2 * q + c) * S_CHUNK
                    last = mm(ps[S_CHUNK * c:S_CHUNK * (c + 1), 6, :], conv[:, t0:t0 + S_CHUNK], sS[:, 2 * q + c, :],
                              True, True)
                last.then_inc(s_off, 1)

            def ssd_T():
                pe.wait_ge(s_n, 1)
                for k in range(2):
                    for i in range(2):
                        c = (2 * k + i) * P
                        for q in range(QT):
                            last = pe.transpose(ps[:, 4 + k, (2 * i + q) * P:(2 * i + q + 1) * P], yd[:, q, c:c + P], ident)
                    last.then_inc(s_yT, 1)

            def merge_gate(i):
                n, k = ORDER[i // 4], i % 4
                it = f"g{n}{k // 2}"
                arrived(pe, it)
                if i == 0:
                    pe.wait_ge(seg_ready, NG)
                if i >= 2:
                    pe.wait_ge(g_tanh, i - 1)
                w = weights(it, KD, 512)
                for e in range(2):
                    c0 = ((2 * k + e) % 4) * P
                    for c in range(KD):
                        last = mm(ps[:, i % 2, e * T:(e + 1) * T], w[:, c, c0:c0 + P], hTv[:, c, :], c == 0, c == KD - 1)
                last.then_inc(g_done, 1)

            def merge_branch(i):
                n, k = ORDER[i // 4], i % 4
                arrived(pe, f"b{n}")
                if i == 0:
                    pe.wait_ge(y_copied, 8)
                if i >= 2:
                    pe.wait_ge(u_done, i - 1)
                if i == 8:
                    pe.wait_ge(h_yTc, 2)
                if i == 12:
                    pe.wait_ge(s_yTc, 2)
                w = weights(f"b{n}", 4, D)
                yT = (yT_a, yT_b, yT_c, yT_d)[n][:, :].rearrange("p (c t) -> p c t", c=4)
                for e in range(2):
                    c0 = (2 * k + e) * P
                    for c in range(4):
                        last = mm(ps[:, 2 + i % 2, e * T:(e + 1) * T], w[:, c, c0:c0 + P], yT[:, c, :], c == 0, c == 3)
                last.then_inc(yp_done, 1)

            for i in range(16):
                if 1 <= i <= 4:
                    hgrn_O(i - 1)
                if i < 4:
                    hgrn_A(i)
                if i == 5:
                    hgrn_T()
                if i == 7:
                    ssd_X()
                if i == 8:
                    ssd_Y(0)
                if i == 9:
                    ssd_B(1)
                if i == 10:
                    ssd_off(1)
                if i == 11:
                    ssd_T()
                merge_gate(i)
                if i < 4:
                    hgrn_U(i)
                if i == 7:
                    ssd_B(0)
                if i == 8:
                    ssd_off(0)
                if i == 9:
                    ssd_Y(1)
                merge_branch(i)

            for q in range(QT):
                for dh in range(2):
                    arrived(pe, f"wo{dh}")
                    if q == 0 and dh == 0:
                        pe.wait_ge(u_done, 16)
                    w = weights(f"wo{dh}", KD, 512)
                    for c in range(KD):
                        last = mm(ps[:, 4 + 2 * q + dh, :], uT[:, c * T + q * P:c * T + (q + 1) * P], w[:, c, :],
                                  c == 0, c == KD - 1)
                    last.then_inc(wo_done, 1)

            norm_T(1)
            pe.wait_ge(ld_moe, 16 * 4)
            pe.wait_ge(hT_done, 8)
            wrv = wr.rearrange("p (c n) -> p c n", c=KD)
            for q in range(QT):
                for c in range(KD):
                    last = mm(ps[:, 4, 64 * q:64 * q + 36], hTv[:, c, q * P:(q + 1) * P], wrv[:, c, :], c == 0, c == KD - 1)
            last.then_inc(rt_done, 1)
            pe.wait_ge(ld_p, 16)
            for k in range(2):
                for q in range(QT):
                    last = pe.transpose(ps[:, 5, (2 * k + q) * P:(2 * k + q + 1) * P],
                                        p_tok[:, q * PLE + k * P:q * PLE + (k + 1) * P], ident)
            last.then_inc(ple_T, 1)

            def gate_up(e, slot, sets, ready):
                ready(e)
                w = ring[slot]
                for b in range(2):
                    wv = w[:, b * 2048:(b + 1) * 2048].rearrange("p (c n) -> p c n", c=KD)
                    for j in range(2):
                        for c in range(KD):
                            last = mm(ps[:, 2 * sets + b, j * T:(j + 1) * T], wv[:, c, j:FF:2], hTv[:, c, :],
                                      c == 0, c == KD - 1)
                last.then_inc(gu_done, 1)

            def down(e, slot, sets):
                pe.wait_ge(act_done, e + 1)
                pe.wait_ge(acc_free, e + 1)
                wv = ring[slot][:, 4096:6144].rearrange("p (j n) -> p j n", j=2)
                av = actT[sets].rearrange("p (j t) -> p j t", j=2)
                for q in range(QT):
                    for dh in range(2):
                        for j in range(2):
                            last = mm(ps[:, 4 + 2 * q + dh, :], av[:, j, q * P:(q + 1) * P],
                                      wv[:, j, dh * 512:(dh + 1) * 512], j == 0, j == 1)
                last.then_inc(down_done, 1)

            def first(e):
                pe.wait_ge(ld_w[e_slot(e)], e_landed(e))

            gate_up(0, e_slot(0), 0, first)
            with pe.Fori(0, 5) as it:
                for k in range(6):
                    def ready(e, k=k):
                        n = k + 1
                        pe.wait_ge(ld_w[e_slot(n)], it * 96 + e_landed(n))
                        if n >= 2:
                            pe.wait_ge(act_done, it * 6 + (n - 1))
                        else:
                            pe.wait_ge(acc_free, it * 6 + 1)
                    gate_up(None, e_slot(k + 1), (k + 1) % 2, ready)
                    down(it * 6 + k, e_slot(k), k % 2)

            def last_ready(e):
                pe.wait_ge(ld_w[e_slot(e)], e_landed(e))
                pe.wait_ge(act_done, e - 1)
            gate_up(31, e_slot(31), 1, last_ready)
            down(30, e_slot(30), 0)
            down(31, e_slot(31), 1)

            arrived_ple = lambda k: pe.wait_ge(ld_w[ple_slot[k]], ple_landed[k])
            arrived_ple(0)
            pe.wait_ge(ple_Tc, 1)
            pe.wait_ge(acc_free, 33)
            w = ring[ple_slot[0]][:, 0:2048].rearrange("p (c n) -> p c n", c=2)
            pv_ = pT_ple.rearrange("p (c t) -> p c t", c=2)
            for q in range(QT):
                for dh in range(2):
                    for c in range(2):
                        last = mm(ps[:, 4 + 2 * q + dh, :], pv_[:, c, q * P:(q + 1) * P], w[:, c, dh * 512:(dh + 1) * 512],
                                  c == 0, c == 1)
            last.then_inc(ple_p, 1)
            norm_T(2)
            pe.wait_ge(hT_done, 12)
            for dh in range(2):
                arrived_ple(1 + dh)
                w = ring[ple_slot[1 + dh]][:, 0:4096].rearrange("p (c n) -> p c n", c=KD)
                for q in range(QT):
                    for c in range(KD):
                        last = mm(ps[:, 2 * q + dh, :], hTv[:, c, q * P:(q + 1) * P], w[:, c, :], c == 0, c == KD - 1)
                    last.then_inc(ple_g, 1)

        @block.scalar
        def _(act):
            cp, A = act.copy, act.activation

            def square_root(m):
                for q in range(QT):
                    if m == 0:
                        act.wait_ge(ld_x[q], 16)
                    elif m == 1:
                        act.wait_ge(x2_done, 2 * (q + 1))
                    elif m == 2:
                        act.wait_ge(acc_free, 33)
                    else:
                        act.wait_ge(x4_done, 4)
                    A(xnv[:, q, :], xv[:, q, :], ACT.Square, accum_out=ssq[:, q:q + 1]).then_inc(ssq_done, 1)
                for q in range(QT):
                    act.wait_ge(ms_done, 2 * m + q + 1)
                    act.sqrt(rms[:, q:q + 1], ms[:, q:q + 1]).then_inc(sqrt_done, 1)

            square_root(0)

            def evac(g):
                name = GRP[g][0]
                b = ps[:, g % 2, :]
                act.wait_ge(proj_done, g + 1)
                if name in ("kv_swa", "kv_slc", "kv_win"):
                    t = {"kv_swa": kv_swa, "kv_slc": kv_slc, "kv_win": kv_win}[name]
                    act.wait_ge(zeroed, 1)
                    cp(t[0:64, 0:256], b[0:64, 0:256])
                    cp(t[64:128, 256:512], b[64:128, 0:256])
                    cp(t[:, 512:768], b[:, 256:512]).then_inc(seg_ready, 1)
                    return
                if name in ("kc", "vc"):
                    t = kc_raw if name == "kc" else vc_raw
                    for g2 in range(2):
                        for m in range(2):
                            last = cp(t[HD * m:HD * (m + 1), g2 * T:(g2 + 1) * T], b[HD * g2:HD * (g2 + 1), 0:T])
                    last.then_inc(seg_ready, 1)
                    return
                dst = {0: q_swa[:, 0:512], 1: q_swa[:, 512:1024], 3: gate_raw[:, :], 4: z_seg[:, 0:512],
                       5: z_seg[:, 512:1024], 10: q_nsa[:, 0:512],
                       11: q_nsa[:, 512:1024], 12: hq[:, 0:512], 13: hq[:, 512:1024], 14: hf[:, 0:512],
                       15: hf[:, 512:1024], 16: hi[:, 0:512], 17: hi[:, 512:1024], 18: hg[:, 0:512],
                       19: hg[:, 512:1024], 20: xbc[:, 0:512], 21: xbc[:, 512:1024], 22: xbc[:, 1024:1536],
                       23: dt_raw[:, :]}[g]
                scale = HD ** -0.5 if name in ("q_swa", "q_nsa") else 1.0
                act.mul(dst, b[:, 0:dst.shape[1]], scale).then_inc(seg_ready, 1)

            def exps(s):
                act.wait_ge(max_done, s + 1)
                for u in range(2):
                    for q, (lo, up) in enumerate(((0, 128), (128, 384))):
                        last = A(sc[:, u, lo:up], sc[:, u, lo:up], ACT.Exp, bias=negm[:, 2 * q + u:2 * q + u + 1],
                                 accum_out=esum[:, 2 * q + u:2 * q + u + 1])
                if s < 4:
                    last = A(es, es, ACT.Exp)
                last.then_inc(exp_done, 1)

            def y_tile(s):
                tile, _, closes = tile_of(s)
                if closes:
                    act.wait_ge(pv_done, s + 1)
                    dst = (yT_a if tile < 4 else yT_c)[:, (tile % 4) * T:(tile % 4 + 1) * T]
                    cp(dst, ps[:, 6 + tile % 2, 0:T]).then_inc(y_copied, 1)

            for g in range(3):
                evac(g)
            for s in range(NS):
                exps(s)
                if s == 6:
                    act.wait_ge(cmp_sub, 1)
                    A(cs, cs, ACT.Exp).then_inc(cmp_exp, 1)
                for g in SLOT_GROUPS[s]:
                    evac(g)
                    if g == 3:
                        act.wait_ge(seg_ready, 4)
                        A(gsig, gate_raw[:, :], ACT.Tanh, scale=0.5).then_inc(gate_tanh, 1)
                if s >= 1:
                    y_tile(s - 1)
                if s == 3:
                    evac(11)
                    act.wait_ge(cmp_gel, 1)
                    A(hidg, hidg, ACT.Tanh, scale=GELU_A).then_inc(cmp_tanh, 1)
                if s == 4:
                    act.wait_ge(cmp_kv, 1)
                    act.wait_ge(zeroed, 1)
                    for g in range(2):
                        act.mul(kcZ[HD * g:HD * (g + 1), g, :], ps[HD * g:HD * (g + 1), 7, 256:256 + N_CMP], 0.5)
                    for r in range(4):
                        last = act.mul(vcZ[32 * r:32 * (r + 1), :, r, :],
                                       ps[32 * r:32 * (r + 1), 7, 384:512].rearrange("p (g d) -> p g d", g=2), 0.5)
                    last.then_inc(cmp_kvc, 1)
            evac(20)
            y_tile(NS - 1)

            act.wait_ge(h_arg, 1)
            A(lbt, lbt, ACT.Exp)
            A(h_k, hf[:, :], ACT.Exp).then_inc(h_exp, 1)
            act.wait_ge(scores_done, NS)
            A(g_th, hg[:, :], ACT.Tanh, scale=0.5).then_inc(hg_tanh, 1)
            act.wait_ge(h_f, 1)
            A(hf[:, :], hf[:, :], ACT.Ln).then_inc(h_log, 1)
            for g in range(21, 24):
                evac(g)

            def hgrn_exps(h):
                act.wait_ge(h_diff, h + 1)
                b = h_b[:, h * T:(h + 1) * T]
                A(e1, t1, ACT.Exp).then_inc(h_e, 1)
                A(e2, t1, ACT.Exp, scale=-1.0).then_inc(h_e, 1)
                A(e3, b, ACT.Exp).then_inc(h_e, 1)
                A(hdec[h % 2], b[:, H_CHUNK - 1:T:H_CHUNK], ACT.Exp)
                A(e4, t4, ACT.Exp).then_inc(h_e, 1)

            def merge_tanh(i):
                act.wait_ge(g_done, i + 1)
                if i >= 2:
                    act.wait_ge(u_done, i - 1)
                A(gth[i % 2][:, :], ps[:, i % 2, :], ACT.Tanh, scale=0.5).then_inc(g_tanh, 1)

            def hgrn_square(h):
                act.wait_ge(h_osb, h + 1)
                for q in range(QT):
                    if h or q:
                        act.wait_ge(h_sq, 2 * h + q)
                    A(square_junk, osb[:, q, h, :], ACT.Square,
                      accum_out=hssq[:, 4 * q + h:4 * q + h + 1]).then_inc(h_sq, 1)

            def ssd_exp(q):
                act.wait_ge(s_Larg, q + 1)
                for g in range(2):
                    for c in range(2):
                        t = S_CHUNK * (c + 1) - 1
                        src = ps[HD * g:HD * (g + 1), 4 + g, t:512:P]
                        A(cdec[HD * g:HD * (g + 1), 4 * (2 * q + c):4 * (2 * q + c) + 4], src, ACT.Exp)
                A(Lb, Lb, ACT.Exp).then_inc(s_Lexp, 1)

            hgrn_exps(0)
            for i in range(16):
                if 1 <= i <= 4:
                    hgrn_square(i - 1)
                if i == 4:
                    act.wait_ge(h_ms, 1)
                    act.sqrt(hrms, hms).then_inc(h_rms, 1)
                if i == 6:
                    for k in range(3):
                        act.wait_ge(s_conv, k + 1)
                        A(conv_th[k], conv[:, k * 512:(k + 1) * 512], ACT.Tanh, scale=0.5).then_inc(s_tanh, 1)
                    A(z_th, z_seg[:, :], ACT.Tanh, scale=0.5).then_inc(s_tanh, 1)
                    act.wait_ge(dt_arg, 1)
                    A(dta, dtr, ACT.Abs).then_inc(act_step, 1)
                    act.wait_ge(act_step, 1)
                    A(dta, dta, ACT.Exp, scale=-1.0).then_inc(act_step, 1)
                    A(alog, alog, ACT.Exp)
                    act.wait_ge(act_step, 2)
                    A(dta, dta, ACT.Ln, bias=1.0).then_inc(dt_log, 1)
                if i == 7:
                    act.wait_ge(s_X, 1)
                    cp(hq[:, 0:512], ps[:, 4, :])
                    cp(hq[:, 512:1024], ps[:, 5, :])
                    act.wait_ge(s_acs, 1)
                    cp(kv_win[:, 0:256], ps[:, 6, 0:256])
                    act.wait_ge(zeroed, 3)
                    for g in range(2):
                        last = cp(BZ[HD * g:HD * (g + 1), g, :], conv[HD * g:HD * (g + 1), 4 * T:5 * T])
                    last.then_inc(s_Xcopy, 1)
                    A(eacs, acs[:, 0:16], ACT.Exp)
                    A(sdec, sdec, ACT.Exp).then_inc(s_dec, 1)
                merge_tanh(i)
                if i < 3:
                    hgrn_exps(i + 1)
                if i == 7:
                    ssd_exp(0)
                if i == 9:
                    ssd_exp(1)
                if i == 10:
                    act.wait_ge(s_y, 2)
                    for q in range(QT):
                        if q:
                            act.wait_ge(s_sq, 1)
                        A(ytmp[:, 1, :, :], yd[:, q, :].rearrange("p (h n) -> p h n", h=8), ACT.Square,
                          accum_out=sssq[:, q:q + 1]).then_inc(s_sq, 1)
                    act.wait_ge(s_ms, 1)
                    act.sqrt(srms, sms).then_inc(s_rms, 1)

            square_root(1)
            act.wait_ge(rt_sub, 1)
            A(gexp, gexp, ACT.Exp).then_inc(rt_exp, 1)
            act.wait_ge(rt_d, 1)
            A(e21, e21, ACT.Exp).then_inc(rt_e, 1)
            act.wait_ge(ple_T, 1)
            cp(pT_ple, ps[:, 5, :]).then_inc(ple_Tc, 1)

            def silu(e, b, waits):
                waits()
                A(sil[b], ps[:, 2 * b, :], ACT.Silu).then_inc(silu_done, 1)

            def silu_ready(e, used):
                act.wait_ge(gu_done, e)
                if used is not None:
                    act.wait_ge(act_done, used)

            silu(0, 0, lambda: silu_ready(1, None))
            silu(1, 1, lambda: silu_ready(2, None))
            with act.Fori(1, 16) as it:
                for k in range(2):
                    silu(None, k, lambda k=k: silu_ready(it * 2 + (k + 1), it * 2 + (k - 1)))

            square_root(2)
            for dh in range(2):
                for q in range(QT):
                    act.wait_ge(ple_g, 2 * dh + q + 1)
                    A(gth[q][:, :], ps[:, 2 * q + dh, :], ACT.Tanh, scale=0.5).then_inc(ple_tanh, 1)
                if dh == 0:
                    act.wait_ge(x4_done, 2)
            square_root(3)

        @block.vector
        def _(dve):
            step = Count(dve_step)

            def dep(ins):
                step.on(ins)
                dve.wait_ge(dve_step, step.n)

            tt, ts, stt, cp = dve.tensor_tensor, dve.tensor_scalar, dve.scalar_tensor_tensor, dve.tensor_copy

            def norm(m):
                for q in range(QT):
                    dve.wait_ge(ssq_done, 2 * m + q + 1)
                    ts(ms[:, q:q + 1], ssq[:, q:q + 1], 1.0 / D, EPS, ALU.mult, ALU.add).then_inc(ms_done, 1)
                for q in range(QT):
                    dve.wait_ge(sqrt_done, 2 * m + q + 1)
                    dep(dve.reciprocal(rstd[:, q:q + 1], rms[:, q:q + 1]))
                    if m < 3:
                        ts(xnv[:, q, :], xv[:, q, :], rstd[:, q:q + 1], None, ALU.mult).then_inc(xn_done, 1)
                    else:
                        stt(xnv[:, q, :], xv[:, q, :], rstd[:, q:q + 1], gf, ALU.mult, ALU.mult).then_inc(out_done, 1)

            def to_hT(m, gain):
                for k in range(4):
                    dve.wait_ge(xT_done, 4 * m + k + 1)
                    tt(hTv[:, 2 * k:2 * k + 2, :], ps[:, k, :].rearrange("p (c t) -> p c t", c=2),
                       gain[:, 2 * k:2 * k + 2, None].to_broadcast([P, 2, T]), ALU.mult).then_inc(hT_done, 1)

            norm(0)
            dve.wait_ge(vec_t, 1)
            dep(cp(vec[:, :], ps[:, 6, 0:V_ALL]))
            to_hT(0, vec[:, V_GMIX:V_GMIX + 8])
            dve.wait_ge(ld_small, 16 * 4)
            dep(ts(nsinks, sinks, -1.0, None, ALU.mult))
            ts(vgh, vec[:, V_GH:V_GH + 4], 0.5, None, ALU.mult)

            def slot_max(s):
                _, _, _, j, br = SLOT_LIST[s]
                dve.wait_ge(scores_done, s + 1)
                if s == 0:
                    dve.wait_ge(ld_bias, 16)
                tt(sc[:, :, 0:256].rearrange("p u (b k) -> p u b k", b=2),
                   ps[:, 2:4, 0:256].rearrange("p u (b k) -> p u b k", b=2),
                   bias[:, :, j, 0:1, :].to_broadcast([P, 2, 2, P]), ALU.add)
                dep(tt(sc[:, :, 256:384], ps[:, 2:4, 256:384], bias[:, :, j, 1 if br == 0 else 2, :], ALU.add))
                dve.tensor_reduce(negm[:, 0:2], sc[:, :, 0:128], X, ALU.max, negate=True)
                last = dve.tensor_reduce(negm[:, 2:4], sc[:, :, 128:384], X, ALU.max, negate=True)
                if br == 0:
                    dep(last)
                    nv = negm.rearrange("p (q u) -> p q u", q=2)
                    ev = es.rearrange("p (q u) -> p q u", q=2)
                    dep(tt(nv, nv, nsinks[:, None, j:8:4].to_broadcast([P, 2, 2]), ALU.min))
                    last = tt(ev, nv, sinks[:, None, j:8:4].to_broadcast([P, 2, 2]), ALU.add)
                last.then_inc(max_done, 1)

            def slot_norm(s):
                _, _, _, j, br = SLOT_LIST[s]
                dve.wait_ge(exp_done, s + 1)
                if br == 0:
                    dep(tt(esum, esum, es, ALU.add))
                dep(dve.reciprocal(rr, esum))
                if br:
                    rv = rr.rearrange("p (q u) -> p q u", q=2)
                    dep(tt(rv, rv, gsig.rearrange("p (q h b) -> p q h b", q=2, b=3)[:, :, j:8:4, br], ALU.mult))
                for u in range(2):
                    for q, (lo, up) in enumerate(((0, 128), (128, 384))):
                        last = ts(sc[:, u, lo:up], sc[:, u, lo:up], rr[:, 2 * q + u:2 * q + u + 1], None, ALU.mult)
                last.then_inc(prob_done, 1)

            def slot_copy(s):
                dve.wait_ge(pT_done, s + 1)
                cp(pT[:, :, :], ps[:, 4:6, 0:384]).then_inc(pT_copied, 1)

            def compress_inputs():
                dve.wait_ge(seg_ready, 8)
                for raw, dst, at in ((kc_raw, kcP, V_PK), (vc_raw, vcP, V_PV)):
                    for g in range(2):
                        for m in range(2):
                            rows = slice(HD * m, HD * (m + 1))
                            v = raw[rows, g * T + m:g * T + m + 1]
                            windows = bass.AP(v.tensor, v.offset,
                                              [v.ap[0], [2, CMP_PAIRS], [CMP_STRIDE, N_CMP]])
                            last = tt(dst[rows, g, :, :], windows,
                                      vec[rows, at:at + CMP_PAIRS, None].to_broadcast([HD, CMP_PAIRS, N_CMP]), ALU.add)
                    last.then_inc(cmp_in, 1)

            def compress_gelu():
                dve.wait_ge(cmp_hid, 2)
                dep(cp(hidx, ps[:, 7, 256:256 + 120]))
                dep(tt(hidg, hidx, hidx, ALU.mult))
                dep(ts(hidg, hidg, GELU_B, 1.0, ALU.mult, ALU.add))
                tt(hidg, hidg, hidx, ALU.mult).then_inc(cmp_gel, 1)
                dve.wait_ge(cmp_tanh, 1)
                dve.wait_ge(zeroed, 1)
                out = hid.rearrange("p v h g c -> p (v h g) c")[:, :, 0:N_CMP]
                stt(out, hidg.rearrange("p (a c) -> p a c", c=N_CMP), 1.0, hidx.rearrange("p (a c) -> p a c", c=N_CMP),
                    ALU.add, ALU.mult).then_inc(cmp_hready, 1)

            def compress_max():
                dve.wait_ge(cmp_sc, 1)
                dep(tt(cs, ps[:, 7, 256:496].rearrange("p (h q c) -> p h q c", h=8, q=2), cbias, ALU.add))
                cv = cs.rearrange("p h q c -> p (h q) c")
                dep(dve.tensor_reduce(cmx, cv, X, ALU.max, negate=True))
                tt(cv, cv, cmx[:, :, None].to_broadcast([P, 16, N_CMP]), ALU.add).then_inc(cmp_sub, 1)

            def compress_norm():
                dve.wait_ge(cmp_exp, 1)
                dve.wait_ge(zeroed, 1)
                cv = cs.rearrange("p h q c -> p (h q) c")
                dep(dve.tensor_reduce(csum, cv, X, ALU.add))
                dep(dve.reciprocal(csum, csum))
                sv = csum.rearrange("p (h q) -> p h q", q=2)
                dep(tt(sv, sv, gsig.rearrange("p (q h b) -> p h q b", q=2, b=3)[:, :, :, 0], ALU.mult))
                dep(tt(cv, cv, csum[:, :, None].to_broadcast([P, 16, N_CMP]), ALU.mult))
                out = csP.rearrange("p q g r c -> p (g r) q c")[:, :, :, 0:N_CMP]
                tt(out, cs, cvalid[:, None, :, :].to_broadcast([P, 8, 2, N_CMP]), ALU.mult).then_inc(cmp_p, 1)
                dve.wait_ge(cmp_pT, 1)
                cp(csT, ps[:, 7, :].rearrange("p (g t) -> p g t", g=2)).then_inc(cmp_pTc, 1)

            for s in range(NS):
                slot_max(s)
                if s == 1:
                    dve.wait_ge(gate_tanh, 1)
                    dep(ts(gsig, gsig, 1.0, 0.5, ALU.add, ALU.mult))
                slot_norm(s)
                if s == 3:
                    compress_inputs()
                if s == 5:
                    compress_max()
                if s == 6:
                    compress_norm()
                slot_copy(s)
                if s == 3:
                    compress_gelu()

            dve.wait_ge(seg_ready, 20)
            tt(lbt, vec[:, V_LB:V_LB + 4], vec[:, V_LB:V_LB + 4], ALU.subtract)
            ts(hf[:, :], hf[:, :], -1.0, 80.0, ALU.mult, ALU.min).then_inc(h_arg, 1)
            dve.wait_ge(h_exp, 1)
            dep(dve.reciprocal(lbr, lbt))
            dep(tt(lbt, lbt, lbr, ALU.mult))
            dep(tt(lb, lbt, lbt, ALU.subtract))
            dep(ts(olb, lb, -1.0, 1.0, ALU.mult, ALU.add))
            dep(ts(h_b, h_k, 1.0, None, ALU.add))
            dep(dve.reciprocal(h_b, h_b))
            for h in range(H_HEADS):
                c = slice(h * T, (h + 1) * T)
                last = ts(hf[:, c], h_b[:, c], olb[:, h:h + 1], lb[:, h:h + 1], ALU.mult, ALU.add)
            dep(last)
            ts(hf[:, :], hf[:, :], 1e-6, None, ALU.max).then_inc(h_f, 1)
            for h in range(H_HEADS):
                c = slice(h * T, (h + 1) * T)
                last = stt(h_k[:, c], h_k[:, c], olb[:, h:h + 1], h_b[:, c], ALU.mult, ALU.mult)
            dep(last)
            dve.wait_ge(hg_tanh, 1)
            stt(hg[:, :], g_th, 1.0, hg[:, :], ALU.add, ALU.mult)
            dve.wait_ge(h_log, 1)
            for h in range(H_HEADS):
                c = slice(h * T, (h + 1) * T)
                last = dve.tensor_tensor_scan(h_b[:, c], scan_keep, hf[:, c], 0.0, ALU.mult, ALU.add)
            dep(last)

            def hgrn_diff(h):
                b = h_b[:, h * T:(h + 1) * T].rearrange("p (c a) -> p c a", c=H_NC)
                full = [P, H_NC, H_CHUNK]
                mid = b[:, :, H_CHUNK // 2:H_CHUNK // 2 + 1].to_broadcast(full)
                end = b[:, :, H_CHUNK - 1:H_CHUNK].to_broadcast(full)
                tt(t1.rearrange("p (c a) -> p c a", c=H_NC), b, mid, ALU.subtract)
                tt(t4.rearrange("p (c a) -> p c a", c=H_NC), end, b, ALU.subtract).then_inc(h_diff, 1)

            def hgrn_ops(h):
                c = slice(h * T, (h + 1) * T)
                if h >= 1:
                    dve.wait_ge(h_A, h)
                if h >= 2:
                    dve.wait_ge(h_O, h - 1)
                dve.wait_ge(h_e, 4 * h + 1)
                tt(qq, hq[:, c], e1, ALU.mult)
                dve.wait_ge(h_e, 4 * h + 2)
                tt(kk, h_k[:, c], e2, ALU.mult)
                half = lambda v: v.rearrange("p (c a) -> p c a", c=H_NC)[:, :, 0:H_CHUNK // 2]
                tt(half(kkL), half(h_k[:, c]), half(e2), ALU.mult)
                dve.wait_ge(h_e, 4 * h + 3)
                tt(qe[h % 2], hq[:, c], e3, ALU.mult)
                dve.wait_ge(h_e, 4 * h + 4)
                tt(kd, h_k[:, c], e4, ALU.mult).then_inc(h_ops, 1)

            def hgrn_mask(h):
                dve.wait_ge(h_A, h + 1)
                tt(Am, ps[:, 4, 0:256].rearrange("p (q t) -> p q t", q=2), tri32[:, None, :].to_broadcast([P, 2, P]), ALU.mult)
                cp(kdT, ps[:, 4, 256:512].rearrange("p (q t) -> p q t", q=2)).then_inc(h_Am, 1)

            def hgrn_chain(h):
                dve.wait_ge(h_U, h + 1)
                dep(cp(hS[:, 0, :], ps[:, 5, 0:P]))
                for c in range(1, H_NC - 1):
                    u = ps[:, 5 + c // 4, (c % 4) * P:(c % 4 + 1) * P]
                    ins = stt(hS[:, c, :], hS[:, c - 1, :], hdec[h % 2][:, c:c + 1], u, ALU.mult, ALU.add)
                    if c < H_NC - 2:
                        dep(ins)
                ins.then_inc(h_S, 1)

            def hgrn_out(h):
                dve.wait_ge(h_O, h + 1)
                cp(osb[:, :, h, :], ps[:, 7, 0:256].rearrange("p (q v) -> p q v", q=2)).then_inc(h_osb, 1)

            def hgrn_finish():
                dve.wait_ge(h_sq, 8)
                ts(hms, hssq, 1.0 / P, EPS, ALU.mult, ALU.add).then_inc(h_ms, 1)
                dve.wait_ge(h_rms, 1)
                dep(dve.reciprocal(hrstd, hrms))
                dve.wait_ge(h_osb, 4)
                for q in range(QT):
                    for h in range(H_HEADS):
                        last = stt(osb[:, q, h, :], osb[:, q, h, :], hrstd[:, 4 * q + h:4 * q + h + 1],
                                   hg[:, q * 512 + h * P:q * 512 + (h + 1) * P], ALU.mult, ALU.mult)
                last.then_inc(h_y, 1)

            def gain_copy(dst, gain, done, copied):
                for k in range(2):
                    dve.wait_ge(done, k + 1)
                    tt(dst[:, 2 * k * T:(2 * k + 2) * T].rearrange("p (c t) -> p c t", c=2),
                       ps[:, 4 + k, :].rearrange("p (c t) -> p c t", c=2),
                       gain[:, 2 * k:2 * k + 2, None].to_broadcast([P, 2, T]), ALU.mult).then_inc(copied, 1)

            def conv_pair(k):
                dve.wait_ge(seg_ready, 21 + k)
                for f in (2 * k, 2 * k + 1):
                    w = lambda j: vec[:, V_CW + 6 * j + f:V_CW + 6 * j + f + 1]
                    xi, yo = xbc[:, f * T:(f + 1) * T], conv[:, f * T:(f + 1) * T]
                    dep(ts(yo, xi, w(3), vec[:, V_CB + f:V_CB + f + 1], ALU.mult, ALU.add))
                    for j in (2, 1, 0):
                        d = 3 - j
                        ins = stt(yo[:, d:T], xi[:, 0:T - d], w(j), yo[:, d:T], ALU.mult, ALU.add)
                        if j:
                            dep(ins)
                ins.then_inc(s_conv, 1)

            def ssd_silu():
                for k in range(3):
                    dve.wait_ge(s_tanh, k + 1)
                    dep(ts(conv_th[k], conv_th[k], 0.5, 0.5, ALU.mult, ALU.add))
                    c = conv[:, k * 512:(k + 1) * 512]
                    last = tt(c, conv_th[k], c, ALU.mult)
                last.then_inc(s_silu, 1)
                dve.wait_ge(s_tanh, 4)
                dep(ts(z_th, z_th, 0.5, 0.5, ALU.mult, ALU.add))
                dep(tt(z_seg[:, :], z_th, z_seg[:, :], ALU.mult))
                dve.wait_ge(dt_log, 1)
                dep(tt(dt, dtm, dta, ALU.add))
                stt(dtA.rearrange("p (q h) -> p q h", q=2), dt.rearrange("p (q h) -> p q h", q=2), -1.0,
                    alog[:, None, :].to_broadcast([P, 2, 8]), ALU.mult, ALU.mult).then_inc(s_silu, 1)

            def ssd_weights():
                dve.wait_ge(s_X, 1)
                dep(cp(acs, ps[:, 6, 256:288]))
                tt(sdec, acs[:, 16:32], acs[:, 0:16], ALU.subtract).then_inc(s_acs, 1)
                dve.wait_ge(s_dec, 1)
                dep(tt(swt, sdec, dt, ALU.mult))
                dep(tt(swB.rearrange("p (q c h) -> p q c h", q=2, c=2),
                       swt.rearrange("p (q h) -> p q h", q=2)[:, :, None, :].to_broadcast([P, 2, 2, 8]),
                       cm64[:, None, :, None].to_broadcast([P, 2, 2, 8]), ALU.mult))
                dve.wait_ge(s_Xcopy, 1)
                tt(xdt.rearrange("p q h n -> p (q h) n"), xtok.rearrange("p q h n -> p (q h) n"),
                   dt[:, :, None].to_broadcast([P, 16, HD]), ALU.mult)

            def ssd_xw(q):
                for c in range(2 - q):
                    w = swB[:, 16 * q + 8 * c:16 * q + 8 * c + 8, None].to_broadcast([P, 8, HD])
                    tt(xwB[:, c, :, :], xtok[:, q, :, :], w, ALU.mult)

            def ssd_L(q):
                dve.wait_ge(s_B, q + 1)
                b = ps[:, 4:6, :].rearrange("p a (h t) -> p (a h) t", h=4)
                dep(tt(Lb, b, acs[:, 8 * q:8 * q + 8, None].to_broadcast([P, 8, P]), ALU.subtract))
                ts(Lb, Lb, 0.0, None, ALU.min).then_inc(s_Larg, 1)
                dep(tt(CBm[:, q, :, :], ps[:, 6, 0:256].rearrange("p (g t) -> p g t", g=2),
                       tri64[:, None, :].to_broadcast([P, 2, P]), ALU.mult))
                if q:
                    dve.wait_ge(s_Y, 1)
                ssd_xw(q)
                dve.wait_ge(s_Lexp, q + 1)
                tt(Lm.rearrange("p (g r) t -> p g r t", g=2), Lb.rearrange("p (g r) t -> p g r t", g=2),
                   CBm[:, q, :, None, :].to_broadcast([P, 2, 4, P]), ALU.mult).then_inc(s_L, 1)

            def ssd_state(q):
                dve.wait_ge(s_Y, q + 1)
                dve.wait_ge(zeroed, 3)
                if q == 0:
                    for g in range(2):
                        r, c = slice(HD * g, HD * (g + 1)), slice(256 * g, 256 * (g + 1))
                        last = cp(sS[r, 1, c], ps[r, 4, c])
                    dep(last)
                chunk = 1 + q
                for g in range(2):
                    r, c = slice(HD * g, HD * (g + 1)), slice(256 * g, 256 * (g + 1))
                    last = tt(sS[r, chunk + 1, c].rearrange("p (r n) -> p r n", r=4),
                              sS[r, chunk, c].rearrange("p (r n) -> p r n", r=4),
                              cdec[r, 4 * chunk:4 * chunk + 4, None].to_broadcast([HD, 4, HD]), ALU.mult)
                dep(last)
                for g in range(2):
                    r, c = slice(HD * g, HD * (g + 1)), slice(256 * g, 256 * (g + 1))
                    last = tt(sS[r, chunk + 1, c], sS[r, chunk + 1, c], ps[r, 5 - q, c], ALU.add)
                last.then_inc(s_state, 1)

            def ssd_y(q):
                dve.wait_ge(s_off, q + 1)
                y1, y2 = ytmp[:, 0, :, :], ytmp[:, 1, :, :]
                hn = lambda v: v.rearrange("p (h n) -> p h n", h=8)
                tt(y2, xtok[:, q, :, :], dskip[:, :, None].to_broadcast([P, 8, HD]), ALU.mult)
                dep(tt(y1, hn(ps[:, 6, :]), eacs[:, 8 * q:8 * q + 8, None].to_broadcast([P, 8, HD]), ALU.mult))
                dep(tt(y1, y1, hn(ps[:, 7, :]), ALU.add))
                dep(tt(y1, y1, y2, ALU.add))
                tt(hn(yd[:, q, :]), y1, hn(z_seg[:, q * 512:(q + 1) * 512]), ALU.mult).then_inc(s_y, 1)

            def merge_update(i):
                k = i % 4
                dve.wait_ge(yp_done, i + 1)
                dve.wait_ge(g_tanh, i + 1)
                u = uT[:, 2 * k * T:(2 * k + 2) * T]
                b = gth[i % 2][:, :]
                if i < 4:
                    stt(u, b, 1.0, ps[:, 2 + i % 2, :], ALU.add, ALU.mult).then_inc(u_done, 1)
                else:
                    dep(stt(b, b, 1.0, ps[:, 2 + i % 2, :], ALU.add, ALU.mult))
                    tt(u, u, b, ALU.add).then_inc(u_done, 1)

            dve.wait_ge(pv_done, NS)
            hgrn_diff(0)
            dve.wait_ge(zeroed, 2)
            hgrn_ops(0)
            for i in range(16):
                if 1 <= i <= 4:
                    hgrn_out(i - 1)
                if i < 4:
                    hgrn_mask(i)
                    if i < 3:
                        hgrn_diff(i + 1)
                    hgrn_chain(i)
                    if i < 3:
                        hgrn_ops(i + 1)
                if i == 4:
                    hgrn_finish()
                    conv_pair(0)
                if i == 5:
                    gain_copy(yT_b, vgh, h_yT, h_yTc)
                    conv_pair(1)
                    conv_pair(2)
                    dep(tt(dtr.rearrange("p (q h) -> p q h", q=2), dt_raw[:, :].rearrange("p (q h) -> p q h", q=2),
                           dtb[:, None, :].to_broadcast([P, 2, 8]), ALU.add))
                    ts(dtm, dtr, 0.0, None, ALU.max).then_inc(dt_arg, 1)
                if i == 6:
                    ssd_silu()
                if i == 7:
                    ssd_weights()
                    ssd_L(0)
                if i == 8:
                    ssd_state(0)
                    ssd_y(0)
                if i == 9:
                    ssd_L(1)
                    ssd_state(1)
                if i == 10:
                    ssd_y(1)
                    dve.wait_ge(s_sq, 2)
                    ts(sms, sssq, 1.0 / 512, EPS, ALU.mult, ALU.add).then_inc(s_ms, 1)
                    dve.wait_ge(s_rms, 1)
                    dep(dve.reciprocal(srstd, srms))
                    dve.wait_ge(s_y, 2)
                    for q in range(QT):
                        last = ts(yd[:, q, :], yd[:, q, :], srstd[:, q:q + 1], None, ALU.mult)
                    last.then_inc(s_n, 1)
                if i == 11:
                    gain_copy(yT_d, vec[:, V_GS:V_GS + 4], s_yT, s_yTc)
                merge_update(i)

            for n in range(4):
                dve.wait_ge(wo_done, n + 1)
                c = x[:, n * 512:(n + 1) * 512]
                stt(c, ps[:, 4 + n, :], 0.5, c, ALU.mult, ALU.add).then_inc(x2_done, 1)

            dve.wait_ge(x2_done, 4)
            norm(1)
            dve.wait_ge(ld_moe, 16 * 4)
            to_hT(1, gffn)
            dve.wait_ge(rt_done, 1)
            lv = lg.rearrange("p (q n) -> p q n", q=2)
            dep(cp(lv, ps[:, 4, 0:128].rearrange("p (q n) -> p q n", q=2)[:, :, 0:36]))
            L4, L32 = lv[:, :, 0:4], lv[:, :, 4:36]

            def b3(v, n):
                return v[:, :, None].to_broadcast([P, 2, n])

            def first_max(out, vals, top, n):
                dep(tt(cand[:, :, 0:n], vals, b3(top, n), ALU.is_equal))
                dep(tt(cand[:, :, 0:n], cand[:, :, 0:n], iom[:, None, 0:n].to_broadcast([P, 2, n]), ALU.mult))
                dep(dve.tensor_reduce(mn, cand[:, :, 0:n], X, ALU.min))
                dep(tt(out, cand[:, :, 0:n], b3(mn, n), ALU.is_equal))

            dep(ts(iom, iota, -64.0, None, ALU.add))
            dep(dve.tensor_reduce(gm, L4, X, ALU.max))
            tt(gexp.rearrange("p (q n) -> p q n", q=2), L4, b3(gm, 4), ALU.subtract).then_inc(rt_sub, 1)
            first_max(goh, L4, gm, 4)
            dep(ts(gpen, goh, -1.0, 1e30, ALU.add, ALU.mult))
            v4 = vmask.rearrange("p q (g e) -> p q g e", g=GROUPS)
            dep(tt(v4, L32.rearrange("p q (g e) -> p q g e", g=GROUPS), goh[:, :, :, None].to_broadcast([P, 2, GROUPS, EPG]), ALU.mult))
            dep(tt(v4, v4, gpen[:, :, :, None].to_broadcast([P, 2, GROUPS, EPG]), ALU.add))
            dep(dve.tensor_reduce(m1, vmask, X, ALU.max))
            first_max(oh1, vmask, m1, EXPERTS)
            dep(stt(vmask, oh1, -3e30, vmask, ALU.mult, ALU.add))
            dep(dve.tensor_reduce(m2, vmask, X, ALU.max))
            tt(e21, m2, m1, ALU.subtract).then_inc(rt_d, 1)
            first_max(oh2, vmask, m2, EXPERTS)
            dve.wait_ge(rt_exp, 1)
            dep(dve.tensor_reduce(gw, gexp.rearrange("p (q n) -> p q n", q=2), X, ALU.add))
            dep(dve.reciprocal(gw, gw))
            dve.wait_ge(rt_e, 1)
            dep(ts(w1, e21, 1.0, None, ALU.add))
            dep(dve.reciprocal(w1, w1))
            dep(tt(w1, w1, gw, ALU.mult))
            dep(tt(w2, w1, e21, ALU.mult))
            dep(tt(oh1, oh1, b3(w1, EXPERTS), ALU.mult))
            dep(tt(oh2, oh2, b3(w2, EXPERTS), ALU.mult))
            cv = comb.rearrange("p (q e) -> p q e", q=2)
            tt(cv, oh1, oh2, ALU.add).then_inc(acc_free, 1)

            def expert_act(b, wait):
                wait()
                tt(actT[b], sil[b], ps[:, 2 * b + 1, :], ALU.mult).then_inc(act_done, 1)

            def accumulate(e, w, wait):
                wait()
                for q in range(QT):
                    for dh in range(2):
                        c = xv[:, q, dh * 512:(dh + 1) * 512]
                        last = stt(c, ps[:, 4 + 2 * q + dh, :], w(q), c, ALU.mult, ALU.add)
                last.then_inc(acc_free, 1)

            def at(sem_, v):
                return lambda: dve.wait_ge(sem_, v)

            def acc_wait(v):
                def f():
                    dve.wait_ge(down_done, v)
                    dve.wait_ge(acc_free, v)
                return f

            expert_act(0, at(silu_done, 1))
            with dve.Fori(0, 15) as it:
                for k in range(2):
                    expert_act((k + 1) % 2, at(silu_done, it * 2 + (k + 2)))
                    accumulate(None, lambda q, k=k: cv[:, q, bass.ds(it * 2 + k, 1)], acc_wait(it * 2 + (k + 1)))
            expert_act(1, at(silu_done, 32))
            for e in (30, 31):
                accumulate(e, lambda q, e=e: cv[:, q, e:e + 1], acc_wait(e + 1))

            dve.wait_ge(acc_free, 33)
            norm(2)
            to_hT(2, vec[:, V_GPLE:V_GPLE + 8])
            dve.wait_ge(ple_p, 1)
            for dh in range(2):
                for q in range(QT):
                    dve.wait_ge(ple_tanh, 2 * dh + q + 1)
                    b = gth[q][:, :]
                    dep(stt(b, b, 1.0, ps[:, 4 + 2 * q + dh, :], ALU.add, ALU.mult))
                    c = xv[:, q, dh * 512:(dh + 1) * 512]
                    stt(c, b, 0.5, c, ALU.mult, ALU.add).then_inc(x4_done, 1)
            dve.wait_ge(x4_done, 4)
            norm(3)

        @block.gpsimd
        def _(pool):
            pstep = Count(pool_step)

            def clear(dst):
                pstep.on(pool.memset(dst, 0.0))
                pool.wait_ge(pool_step, pstep.n)

            for kv in (kv_swa, kv_slc, kv_win):
                clear(kv[:, 0:512])
            clear(kcZ)
            clear(vcZ)
            clear(hid)
            pool.memset(csP, 0.0).then_inc(zeroed, 1)
            pool.wait_ge(pv_done, NS)
            pool.wait_ge(zeroed, 1)
            pool.memset(kkL, 0.0).then_inc(zeroed, 1)
            pool.wait_ge(seg_ready, 18)
            pool.wait_ge(zeroed, 2)
            for h in range(H_HEADS):
                if h >= 1:
                    pool.wait_ge(h_U, h)
                    pool.wait_ge(h_iB, h)
                v = hi[:, :].rearrange("p (q n) -> p q n", q=2)[:, :, None, h * P:(h + 1) * P].to_broadcast([P, 2, 4, P])
                pool.tensor_tensor(iB, v, cm32[:, None, :, None].to_broadcast([P, 2, 4, P]), ALU.mult).then_inc(h_iB, 1)
            pool.wait_ge(h_yTc, 2)
            pool.wait_ge(h_iB, 4)
            clear(BZ)
            pool.memset(sS, 0.0).then_inc(zeroed, 1)


_INS = ['x', 'p', 'w_in', 'g_mix', 'attn_sinks', 'hgrn_lower_bounds', 'hgrn_norm_g', 'nsa_pos_k', 'nsa_pos_v',
        'nsa_cmp_w1_k', 'nsa_cmp_w2_k', 'nsa_cmp_w1_v', 'nsa_cmp_w2_v', 'ssm_conv_w', 'ssm_conv_b', 'ssm_dt_bias',
        'ssm_A_log', 'ssm_D', 'ssm_norm_g', 'w_branch', 'w_out', 'g_ffn', 'w_router_grp', 'w_router_exp',
        'w_exp_gate', 'w_exp_up', 'w_exp_down', 'g_ple', 'w_ple_gate', 'w_ple_proj', 'g_final']


def kernel(**inputs):
    import concourse.bacc as _bacc
    from concourse.bass_utils import run_bass_kernel_spmd as _run

    nc = _bacc.Bacc("TRN2", target_bir_lowering=False, num_devices=1)
    arrays = {name: np.ascontiguousarray(inputs[name]) for name in _INS}
    arrays["cst"] = shape_constants()
    args = {name: nc.dram_tensor(name, v.shape, mybir.dt.from_np(v.dtype), kind="ExternalInput").ap()
            for name, v in arrays.items()}
    args["out"] = nc.dram_tensor("out", (1, T, D), F32, kind="ExternalOutput").ap()
    hybrid_layer(nc, args)
    r = _run(nc, [arrays], core_ids=[0])
    return r.results[0]["out"]
```

```python
from contextlib import ExitStack

import concourse.bass as bass
import numpy as np
from concourse import mybir

F32 = mybir.dt.float32
ALU = mybir.AluOpType
ACT = mybir.ActivationFunctionType
X = mybir.AxisListType.X

P = 128
T = 256
QT = T // P
D = 1024
KD = D // P
HEADS, HD = 8, 64
CMP_LEN, CMP_STRIDE = 32, 16
N_CMP = (T - CMP_LEN) // CMP_STRIDE + 1
CMP_PAIRS = CMP_LEN // 2
H_HEADS, H_CHUNK, H_NC = 4, 32, T // 32
S_CHUNK = 64
GROUPS, EXPERTS, FF = 4, 32, 256
CAP = 32
QUADS = EXPERTS // 4
MAX_OVER = 2 * T // (CAP + 1)
EPG = EXPERTS // GROUPS
PLE = 256
EPS = 1e-6
NEG = -1e30
GELU_A, GELU_B = 0.7978845608028654, 0.044715

SWA_Q, SWA_KV, H_Q, H_F, H_I, H_G, NSA_Q = 0, 512, 768, 1280, 1792, 2304, 2816
NSA_KV, NSA_GATE, SSM_Z, SSM_X, SSM_DT, MERGE = 3328, 4096, 4120, 4632, 5400, 5408

SLOTS = 3
SLOT_E = 3 * KD * FF
SLOT = KD * 776

C_ID, C_TRI64, C_BLK64, C_TRI32 = 0, 128, 256, 384
C_CM32, C_CM64, C_SCAN, C_CBIAS = 512, 516, 518, 774
C_CVALID = C_CBIAS + HEADS * QT * N_CMP
C_IOTA = C_CVALID + QT * N_CMP
C_BIAS = C_IOTA + EXPERTS
C_MOE = C_BIAS + HEADS * 3 * P
C_ALL = C_MOE + 2 * P

V_GMIX, V_GPLE, V_GH, V_GS, V_CB, V_CW, V_LB, V_PK, V_PV, V_ALL = 0, 8, 16, 20, 24, 30, 54, 58, 74, 90


def shape_constants():
    c = np.zeros((P, C_ALL), np.float32)
    i, j = np.arange(P)[:, None], np.arange(P)[None, :]
    c[:, C_ID:C_ID + P] = i == j
    c[:, C_TRI64:C_TRI64 + P] = (i <= j) & (i // S_CHUNK == j // S_CHUNK)
    c[:, C_BLK64:C_BLK64 + P] = i // S_CHUNK == j // S_CHUNK
    c[:, C_TRI32:C_TRI32 + P] = (i <= j) & (i // H_CHUNK == j // H_CHUNK)
    c[:, C_CM32:C_CM32 + 4] = i // H_CHUNK == np.arange(4)[None, :]
    c[:, C_CM64:C_CM64 + 2] = i // S_CHUNK == np.arange(2)[None, :]
    c[:, C_SCAN:C_SCAN + T] = np.arange(T)[None, :] % H_CHUNK != 0
    slopes = 2.0 ** (-8.0 * np.arange(1, HEADS + 1) / HEADS)
    end = np.arange(N_CMP) * CMP_STRIDE + CMP_LEN - 1
    pos = np.arange(T).reshape(QT, P).T
    dist = (pos[:, :, None] - end[None, None, :]).astype(np.float32)
    cb = np.where(dist[:, None] >= 0, -slopes[None, :, None, None] * dist[:, None], NEG)
    c[:, C_CBIAS:C_CVALID] = cb.reshape(P, -1)
    c[:, C_CVALID:C_IOTA] = (dist >= 0).reshape(P, -1)
    c[:, C_IOTA:C_BIAS] = np.arange(EXPERTS)[None, :]
    for h in range(HEADS):
        at = C_BIAS + h * 3 * P
        c[:, at:at + P] = np.where(j <= i, -slopes[h] * (i - j), NEG)
        c[:, at + P:at + 2 * P] = np.where(j > i, -slopes[h] * (i - j + P), NEG)
        c[:, at + 2 * P:at + 3 * P] = -slopes[h] * (i - j + P)
    c[:, C_MOE:C_MOE + P] = i < j
    c[:, C_MOE + P:C_ALL] = 1.0
    return c


class Count:

    def __init__(self, sem):
        self.sem, self.n = sem, 0

    def on(self, ins):
        ins.then_inc(self.sem, 1)
        self.n += 1
        return self.n


def hybrid_layer(nc, a):
    ctx = ExitStack()
    with ctx:
        def sb(name, n):
            return ctx.enter_context(nc.sbuf_tensor("s_" + name, [P, n], F32))

        def sem(name):
            return ctx.enter_context(nc.semaphore(name))

        w_in = a["w_in"][0].rearrange("(c p) n -> p c n", p=P)
        w_branch = a["w_branch"][0]
        w_out = a["w_out"][0].rearrange("(c p) n -> p c n", p=P)
        x_dram = a["x"][0].rearrange("(q p) d -> p q d", p=P)
        out_dram = a["out"][0].rearrange("(q p) d -> p q d", p=P)
        p_dram = a["p"][0, 0].rearrange("(q p) d -> p q d", p=P)

        ring = [sb(f"wslot{i}", SLOT) for i in range(SLOTS)]
        x = sb("x", QT * D)
        xn = sb("xn", QT * D)
        hT = sb("hT", KD * T)
        cst = sb("cst", C_MOE)
        vrows = sb("vrows", P)
        vec = sb("vec", V_ALL)
        kv_swa, kv_slc, kv_win = sb("kv_swa", 768), sb("kv_slc", 768), sb("kv_win", 768)
        q_swa, q_nsa = sb("q_swa", 1024), sb("q_nsa", 1024)
        kc_raw, vc_raw = sb("kc_raw", 512), sb("vc_raw", 512)
        gate_raw, dt_raw = sb("gate_raw", QT * 24), sb("dt_raw", QT * 8)
        z_seg = sb("z_seg", 1024)
        hq, hf, hi, hg = sb("hq", 1024), sb("hf", 1024), sb("hi", 1024), sb("hg", 1024)
        xbc = sb("xbc", 1536)
        yT_a, yT_c = sb("yT_a", 1024), sb("yT_c", 1024)
        small = sb("small", 512)
        over = ctx.enter_context(nc.sbuf_tensor("s_over", [P, 16], mybir.dt.int32))
        work = sb("work", 8064)

        so = [0]

        def sm(n):
            v = small[:, so[0]:so[0] + n]
            so[0] += n
            assert so[0] <= 512
            return v

        wo = [0]

        def wk(n, at=None):
            if at is not None:
                wo[0] = at
            v = work[:, wo[0]:wo[0] + n]
            wo[0] += n
            assert wo[0] <= 8064, wo[0]
            return v

        ident = cst[:, C_ID:C_ID + P]
        tri64, blk64 = cst[:, C_TRI64:C_TRI64 + P], cst[:, C_BLK64:C_BLK64 + P]
        tri32 = cst[:, C_TRI32:C_TRI32 + P]
        cm32, cm64 = cst[:, C_CM32:C_CM32 + 4], cst[:, C_CM64:C_CM64 + 2]
        scan_keep = cst[:, C_SCAN:C_SCAN + T]
        cbias = cst[:, C_CBIAS:C_CVALID].rearrange("p (h q c) -> p h q c", h=HEADS, q=QT)
        cvalid = cst[:, C_CVALID:C_IOTA].rearrange("p (q c) -> p q c", q=QT)
        iota = cst[:, C_IOTA:C_BIAS]
        bias = cst[:, C_BIAS:C_MOE].rearrange("p (g j b k) -> p g j b k", g=2, j=4, b=3)

        xv = x[:, :].rearrange("p (q d) -> p q d", q=QT)
        xnv = xn[:, :].rearrange("p (q d) -> p q d", q=QT)
        hTv = hT[:, :].rearrange("p (c t) -> p c t", c=KD)
        yT_b, yT_d = q_swa, q_nsa
        uT = cst[:, C_BIAS:C_BIAS + KD * T]
        spare = cst[:, C_BIAS + KD * T:C_MOE]

        sc = wk(768, 0).rearrange("p (u k) -> p u k", u=2)
        pT = wk(768).rearrange("p (u k) -> p u k", u=2)
        kcP = wk(480).rearrange("p (g l c) -> p g l c", g=2, l=CMP_PAIRS)
        vcP = wk(480).rearrange("p (g l c) -> p g l c", g=2, l=CMP_PAIRS)
        hid = wk(256).rearrange("p (v h g c) -> p v h g c", v=2, h=2, g=2)
        hidx, hidg = wk(120), wk(120)
        kcZ = wk(2 * N_CMP).rearrange("p (g c) -> p g c", g=2)
        vcZ = wk(512).rearrange("p (g r d) -> p g r d", g=2, r=4)
        cs = wk(240).rearrange("p (h q c) -> p h q c", h=8, q=2)
        csP = wk(512).rearrange("p (q g r c) -> p q g r c", q=2, g=2, r=4)
        csT = wk(512).rearrange("p (g t) -> p g t", g=2)
        w2k, w2v = wk(128).rearrange("p (c d) -> p c d", c=2), wk(128).rearrange("p (c d) -> p c d", c=2)

        h_k, h_b = xn[:, 0:1024], xn[:, 1024:2048]
        t1, t4 = wk(256, 0), wk(256)
        e1, e2, e3, e4 = wk(256), wk(256), wk(256), wk(256)
        qq, kk, kkL, kd = wk(256), wk(256), wk(256), wk(256)
        qe = [wk(256), wk(256)]
        hS = wk(7 * P).rearrange("p (c v) -> p c v", c=7)
        Am = wk(256).rearrange("p (q t) -> p q t", q=2)
        kdT = wk(256).rearrange("p (q k) -> p q k", q=2)
        iB = wk(1024).rearrange("p (q c v) -> p q c v", q=2, c=4)
        osb = wk(1024).rearrange("p (q h v) -> p q h v", q=2, h=4)
        conv_at = wo[0]
        conv = wk(1536)
        square_junk = vrows[:, :]

        BZ = wk(512, 0).rearrange("p (g t) -> p g t", g=2)
        Lb = wk(1024).rearrange("p (h t) -> p h t", h=8)
        Lm = wk(1024).rearrange("p (h t) -> p h t", h=8)
        xwB = wk(1024).rearrange("p (c h n) -> p c h n", c=2, h=8)
        sS = wk(2048).rearrange("p (c n) -> p c n", c=4)
        assert wo[0] <= conv_at
        CBm = kv_slc[:, 0:512].rearrange("p (q g t) -> p q g t", q=2, g=2)
        Btok = kv_win[:, 0:256].rearrange("p (q n) -> p q n", q=2)
        xtok = hq[:, :].rearrange("p (q h n) -> p q h n", q=2, h=8)
        xdt = hi[:, :].rearrange("p (q h n) -> p q h n", q=2, h=8)
        yd = hg[:, :].rearrange("p (q n) -> p q n", q=2)
        ytmp = hf[:, :].rearrange("p (a h n) -> p a h n", a=2, h=8)
        conv_th = [q_nsa[:, 0:512], q_nsa[:, 512:1024], kc_raw[:, :]]
        z_th = spare
        g_th = q_nsa[:, :]

        gth = [sb("gth0", 512), sb("gth1", 512)]

        ps = ctx.enter_context(nc.psum_tensor("ps", [P, 8, 512], F32))

        ssq, ms, rms, rstd = sm(2), sm(2), sm(2), sm(2)
        negm, esum, rr, es = sm(4), sm(4), sm(4), sm(4)
        sinks, nsinks = sm(8), sm(8)
        gsig = sm(QT * 24)
        lb, olb, lbt, lbr = sm(4), sm(4), sm(4), sm(4)
        vgh = sm(4)
        hdec = [sm(8), sm(8)]
        hssq, hms, hrms, hrstd = sm(8), sm(8), sm(8), sm(8)
        cmx, csum = sm(16), sm(16)
        alog, dtb, dskip = sm(8), sm(8), sm(8)
        dtr, dta, dtm, dt, dtA = sm(16), sm(16), sm(16), sm(16), sm(16)
        acs, sdec, eacs, swt = sm(32), sm(16), sm(16), sm(16)
        swB = sm(32)
        cdec = sm(16)
        sssq, sms, srms, srstd = sm(2), sm(2), sm(2), sm(2)
        assert so[0] <= 512, so[0]

        comb = z_seg[:, 0:QT * EXPERTS]
        wr = hq[:, 0:KD * 36]
        gffn = hi[:, :]
        ys = hi[:, :]
        sil, act_tok = hf[:, 0:256], hf[:, 256:512]
        actT = [hf[:, 512:576], hf[:, 576:640]]
        strict, ones = kv_slc[:, 0:P], kv_slc[:, P:2 * P]
        gath = work[:, SLOT_E:SLOT_E + 1024].rearrange("p (c s) -> p c s", c=KD)
        onehot = work[:, SLOT_E + 1024:SLOT_E + 1280]
        onehot_w = work[:, SLOT_E + 1280:SLOT_E + 1536]
        scat = work[:, SLOT_E + 1536:SLOT_E + 1792].rearrange("p (q t) -> p q t", q=QT)
        f_sil, f_act = q_swa[:, 512:1024], q_nsa[:, 512:1024]
        rt = hg[:, :]
        gf = xbc[:, 0:1024]
        pT_ple = q_nsa[:, 0:512]
        p_tok = q_swa[:, 0:512]

        ld_cmp, ld_vec, ld_cst, ld_bias, ld_small = sem("ld_cmp"), sem("ld_vec"), sem("ld_cst"), sem("ld_bias"), sem("ld_small")
        ld_x = [sem("ld_x0"), sem("ld_x1")]
        ld_moe, ld_p = sem("ld_moe"), sem("ld_p")
        ld_w = [sem(f"ld_w{i}") for i in range(SLOTS)]
        dve_step, act_step, pool_step = sem("dve_step"), sem("act_step"), sem("pool_step")
        ssq_done, ms_done, sqrt_done = sem("ssq_done"), sem("ms_done"), sem("sqrt_done")
        xn_done, xT_done, hT_done = sem("xn_done"), sem("xT_done"), sem("hT_done")
        vec_t, vec_ready, zeroed = sem("vec_t"), sem("vec_ready"), sem("zeroed")
        proj_done, seg_ready = sem("proj_done"), sem("seg_ready")
        scores_done, max_done, sink_ready = sem("scores_done"), sem("max_done"), sem("sink_ready")
        exp_done, prob_done = sem("exp_done"), sem("prob_done")
        pT_done, pT_copied, pv_done, y_copied = sem("pT_done"), sem("pT_copied"), sem("pv_done"), sem("y_copied")
        gate_tanh = sem("gate_tanh")
        cmp_in, cmp_hid, cmp_gel, cmp_tanh, cmp_hready = (
            sem("cmp_in"), sem("cmp_hid"), sem("cmp_gel"), sem("cmp_tanh"), sem("cmp_hready"))
        cmp_kv, cmp_kvc, cmp_sc, cmp_sub, cmp_exp, cmp_p, cmp_pT, cmp_pTc = (
            sem("cmp_kv"), sem("cmp_kvc"), sem("cmp_sc"), sem("cmp_sub"), sem("cmp_exp"), sem("cmp_p"),
            sem("cmp_pT"), sem("cmp_pTc"))
        h_arg, h_exp, h_f, h_log, hg_tanh = sem("h_arg"), sem("h_exp"), sem("h_f"), sem("h_log"), sem("hg_tanh")
        h_diff, h_e, h_ops = sem("h_diff"), sem("h_e"), sem("h_ops")
        h_A, h_Am, h_U, h_S, h_O, h_osb, h_iB, h_sq = (
            sem("h_A"), sem("h_Am"), sem("h_U"), sem("h_S"), sem("h_O"), sem("h_osb"), sem("h_iB"), sem("h_sq"))
        h_ms, h_rms, h_y, h_yT, h_yTc = sem("h_ms"), sem("h_rms"), sem("h_y"), sem("h_yT"), sem("h_yTc")
        dt_arg, dt_log, s_conv, s_tanh, s_silu = sem("dt_arg"), sem("dt_log"), sem("s_conv"), sem("s_tanh"), sem("s_silu")
        s_X, s_Xcopy, s_acs, s_dec, s_B, s_Larg, s_Lexp, s_L = (
            sem("s_X"), sem("s_Xcopy"), sem("s_acs"), sem("s_dec"), sem("s_B"), sem("s_Larg"), sem("s_Lexp"), sem("s_L"))
        s_Y, s_state, s_off, s_y, s_sq, s_ms, s_rms, s_n, s_yT, s_yTc = (
            sem("s_Y"), sem("s_state"), sem("s_off"), sem("s_y"), sem("s_sq"), sem("s_ms"), sem("s_rms"), sem("s_n"),
            sem("s_yT"), sem("s_yTc"))
        g_done, g_tanh, yp_done, u_done = sem("g_done"), sem("g_tanh"), sem("yp_done"), sem("u_done")
        wo_done, x2_done = sem("wo_done"), sem("x2_done")
        rt_done, rt_sub, rt_exp, rt_d, rt_e = sem("rt_done"), sem("rt_sub"), sem("rt_exp"), sem("rt_d"), sem("rt_e")
        gu_done, silu_done, act_done, down_done, sc_done, acc_done = (
            sem("gu_done"), sem("silu_done"), sem("act_done"), sem("down_done"), sem("sc_done"), sem("acc_done"))
        m_mask, m_pos, m_S, m_Sw, m_G, m_Gc, m_ST, m_STc, m_y = (
            sem("m_mask"), sem("m_pos"), sem("m_S"), sem("m_Sw"), sem("m_G"), sem("m_Gc"), sem("m_ST"), sem("m_STc"),
            sem("m_y"))
        a_T, a_Tc = sem("a_T"), sem("a_Tc")
        ld_e = [sem(f"ld_e{i}") for i in range(4)]
        over_ready, ld_f, f_gu, f_silu, f_act_done, f_down, f_acc = (
            sem("over_ready"), sem("ld_f"), sem("f_gu"), sem("f_silu"), sem("f_act"), sem("f_down"), sem("f_acc"))
        x3_done = sem("x3_done")
        ple_T, ple_Tc, ple_p, ple_g, ple_tanh, x4_done = (
            sem("ple_T"), sem("ple_Tc"), sem("ple_p"), sem("ple_g"), sem("ple_tanh"), sem("x4_done"))
        out_done, o_dma = sem("out_done"), sem("o_dma")

        def cols(c0, n):
            return [(0, KD * n, w_in[:, :, c0:c0 + n])]

        def pair_cols(c0):
            return [(g * HD, w_in[:, :, c0 + g * 256:c0 + (g + 1) * 256]) for g in range(2)]

        items = []

        def item(name, parts, freed_by, count):
            items.append((name, parts, freed_by, count))

        item("swa", [("pairs", 768, v) for v in pair_cols(SWA_Q)] + [("plain", 768, (512, w_in[:, :, SWA_KV:SWA_KV + 256]))], proj_done, 3)
        item("gz", cols(NSA_GATE, 536), proj_done, 6)
        item("nkv", cols(NSA_KV, 768), proj_done, 10)
        item("nq", [("pairs", 512, v) for v in pair_cols(NSA_Q)], proj_done, 12)
        item("w1k", [(0, 4096, a["nsa_cmp_w1_k"][0].rearrange("(c p) n -> p c n", p=P))], cmp_hid, 1)
        item("w1v", [(0, 4096, a["nsa_cmp_w1_v"][0].rearrange("(c p) n -> p c n", p=P))], cmp_hid, 2)
        item("hq", cols(H_Q, 512), proj_done, 14)
        item("hf", cols(H_F, 512), proj_done, 16)
        item("hi", cols(H_I, 512), proj_done, 18)
        item("hg", cols(H_G, 512), proj_done, 20)
        item("xd", cols(SSM_X, 776), proj_done, 24)
        ORDER = (0, 2, 1, 3)
        for ni, n in enumerate(ORDER):
            if n in (0, 2):
                wb = w_branch[n].rearrange("(g j d) e -> g d j e", g=2, d=HD)
                parts = [(0, 4096, wb[0], 0), (0, 4096, wb[1], HD)]
            else:
                parts = [(0, 4096, w_branch[n].rearrange("(c p) e -> p c e", p=P))]
            item(f"g{n}0", cols(MERGE + n * D, 512), g_done, 4 * ni + 2)
            item(f"b{n}", parts, yp_done, 4 * ni + 4)
            item(f"g{n}1", cols(MERGE + n * D + 512, 512), g_done, 4 * ni + 4)
        item("wo0", [(0, 4096, w_out[:, :, 0:512])], wo_done, 3)
        item("wo1", [(0, 4096, w_out[:, :, 512:1024])], wo_done, 4)

        landed, slot_of = {}, {}
        count = [0] * SLOTS
        for i, (name, parts, *_) in enumerate(items):
            count[i % SLOTS] += 16 * sum(KD if part[0] == "pairs" else 1 for part in parts)
            landed[name], slot_of[name] = count[i % SLOTS], i % SLOTS

        def weights(name, c, n):
            return ring[slot_of[name]][:, 0:c * n].rearrange("p (c n) -> p c n", c=c)

        def arrived(eng, name):
            eng.wait_ge(ld_w[slot_of[name]], landed[name])

        GRP = []
        for half in range(2):
            GRP.append(("q_swa", "swa", 768, [("headpair", 2 * half + i, 0) for i in range(2)]))
        GRP.append(("kv_swa", "swa", 768, [("feat", 512, 128), ("tok", 640, 128)]))
        GRP.append(("gate", "gz", 536, [("tok", 0, 24)]))
        for q in range(2):
            GRP.append((f"z{q}", "gz", 536, [("tokq", 24, 512, q)]))
        GRP.append(("kc", "nkv", 768, [("feat", 0, 128)]))
        GRP.append(("vc", "nkv", 768, [("feat", 128, 128)]))
        GRP.append(("kv_slc", "nkv", 768, [("feat", 256, 128), ("tok", 384, 128)]))
        GRP.append(("kv_win", "nkv", 768, [("feat", 512, 128), ("tok", 640, 128)]))
        for half in range(2):
            GRP.append(("q_nsa", "nq", 512, [("headpair", 2 * half + i, 0) for i in range(2)]))
        for nm in ("hq", "hf"):
            for half in range(2):
                GRP.append((nm, nm, 512, [("feat", (2 * half + i) * P, P) for i in range(2)]))
        for nm in ("hi", "hg"):
            for q in range(2):
                GRP.append((nm, nm, 512, [("tokq", 0, 512, q)]))
        for k in range(3):
            GRP.append(("xbc", "xd", 776, [("feat", (2 * k + i) * P, P) for i in range(2)]))
        GRP.append(("dt", "xd", 776, [("tok", 768, 8)]))
        NG = len(GRP)
        assert NG == 24


        e_slot = [ring[(len(items) + k) % SLOTS] for k in range(SLOTS)] + [work]

        lg = rt[:, 0:72]
        mask = rt[:, 416:480].rearrange("p (q n) -> p q n", q=2)
        nmask = rt[:, 480:544].rearrange("p (q n) -> p q n", q=2)
        posm = rt[:, 544:616].rearrange("p (q n) -> p q n", q=2)
        comb_over = rt[:, 616:680].rearrange("p (q n) -> p q n", q=2)
        cnt, isover, rank, over_f = rt[:, 680:712], rt[:, 712:744], rt[:, 744:776], rt[:, 776:792]
        pick = q_swa[:, 512:512 + MAX_OVER * EXPERTS].rearrange("p (k e) -> p k e", k=MAX_OVER)
        gexp, gm, m1, m2, mn = rt[:, 72:80], rt[:, 80:82], rt[:, 82:84], rt[:, 84:86], rt[:, 86:88]
        gw, e21, w1, w2 = rt[:, 88:90], rt[:, 90:92], rt[:, 92:94], rt[:, 94:96]
        goh = rt[:, 96:104].rearrange("p (q n) -> p q n", q=2)
        gpen = rt[:, 104:112].rearrange("p (q n) -> p q n", q=2)
        iom = rt[:, 128:160]
        cand = rt[:, 160:224].rearrange("p (q n) -> p q n", q=2)
        vmask = rt[:, 224:288].rearrange("p (q n) -> p q n", q=2)
        oh1 = rt[:, 288:352].rearrange("p (q n) -> p q n", q=2)
        oh2 = rt[:, 352:416].rearrange("p (q n) -> p q n", q=2)

        SLOT_LIST = [("swa", kv_swa, q_swa, j, 0) for j in range(4)]
        for j in range(4):
            SLOT_LIST += [("slc", kv_slc, q_nsa, j, 1), ("win", kv_win, q_nsa, j, 2)]
        NS = len(SLOT_LIST)
        SLOT_GROUPS = [[3, 4], [5, 6], [7, 8], [9, 10]] + [[12 + i] for i in range(8)]

        def tile_of(s):
            if s < 4:
                return s, True, True
            return 4 + (s - 4) // 2, s % 2 == 0, s % 2 == 1

        block = ctx.enter_context(nc.Block())

        @block.sync
        def _(sp):
            def load(i):
                name, parts, _, _ = items[i]
                if i >= SLOTS:
                    sp.wait_ge(items[i - SLOTS][2], items[i - SLOTS][3])
                for part in parts:
                    if part[0] in ("pairs", "plain"):
                        kind, width, (at, src) = part
                        wide = ring[i % SLOTS][:, 0:KD * width].rearrange("p (c n) -> p c n", c=KD)
                        if kind == "pairs":
                            for c in range(KD):
                                dst = wide[:, c, 0:512].rearrange("p (j h d) -> p j h d", j=4, h=2)[:, :, at // HD, :]
                                sp.dma_start(dst, src[:, c, :].rearrange("p (j d) -> p j d", j=4)).then_inc(ld_w[i % SLOTS], 16)
                        else:
                            sp.dma_start(wide[:, :, at:at + src.shape[2]], src).then_inc(ld_w[i % SLOTS], 16)
                        continue
                    at, n, src = part[:3]
                    p0 = part[3] if len(part) > 3 else 0
                    np_, c, w = src.shape
                    dst = ring[i % SLOTS][p0:p0 + np_, at:at + n].rearrange("p (c n) -> p c n", c=c)
                    sp.dma_start(dst, src).then_inc(ld_w[i % SLOTS], 16)

            def rows(at, src, n):
                sp.dma_start(vrows[at:at + n, :], src).then_inc(ld_vec, 16)

            for q in range(QT):
                sp.dma_start(xv[:, q, :], x_dram[:, q, :]).then_inc(ld_x[q], 16)
            sp.dma_start(cst[:, 0:C_BIAS], a["cst"][:, 0:C_BIAS]).then_inc(ld_cst, 16)
            rows(V_GMIX, a["g_mix"][0].rearrange("(c p) -> c p", p=P), 8)
            rows(V_GPLE, a["g_ple"][0].rearrange("(c p) -> c p", p=P), 8)
            rows(V_GH, a["hgrn_norm_g"][0].rearrange("(c p) -> c p", p=P), 4)
            rows(V_GS, a["ssm_norm_g"][0].rearrange("(c p) -> c p", p=P), 4)
            rows(V_CB, a["ssm_conv_b"][0].rearrange("(c p) -> c p", p=P), 6)
            rows(V_CW, a["ssm_conv_w"][0].rearrange("j (c p) -> (j c) p", p=P), 24)
            rows(V_LB, a["hgrn_lower_bounds"][0].rearrange("(c p) -> c p", p=P), 4)
            rows(V_PK, a["nsa_pos_k"][0].rearrange("(l m) d -> l (m d)", m=2), 16)
            rows(V_PV, a["nsa_pos_v"][0].rearrange("(l m) d -> l (m d)", m=2), 16)
            load(0)
            for dst, src in ((sinks, "attn_sinks"), (alog, "ssm_A_log"), (dtb, "ssm_dt_bias"), (dskip, "ssm_D")):
                sp.dma_start(dst, a[src][0].partition_broadcast(P)).then_inc(ld_small, 16)
            load(1)
            sp.dma_start(cst[:, C_BIAS:C_MOE], a["cst"][:, C_BIAS:C_MOE]).then_inc(ld_bias, 16)
            sp.dma_start(w2k, a["nsa_cmp_w2_k"][0].rearrange("(c p) d -> p c d", p=P)).then_inc(ld_cmp, 16)
            sp.dma_start(w2v, a["nsa_cmp_w2_v"][0].rearrange("(c p) d -> p c d", p=P)).then_inc(ld_cmp, 16)
            for i in range(2, len(items)):
                load(i)

            sp.wait_ge(s_yTc, 2)
            wrv = wr.rearrange("p (c n) -> p c n", c=KD)
            sp.dma_start(wrv[:, :, 0:GROUPS], a["w_router_grp"][0].rearrange("(p c) n -> p c n", c=KD)).then_inc(ld_moe, 16)
            sp.dma_start(wrv[:, :, GROUPS:36], a["w_router_exp"][0].rearrange("(p c) n -> p c n", c=KD)).then_inc(ld_moe, 16)
            sp.dma_start(gffn, a["g_ffn"][0].partition_broadcast(P)).then_inc(ld_moe, 16)
            sp.dma_start(kv_slc[:, 0:2 * P], a["cst"][:, C_MOE:C_ALL]).then_inc(ld_moe, 16)
            sp.dma_start(gf, a["g_final"].partition_broadcast(P)).then_inc(ld_moe, 16)
            sp.wait_ge(yp_done, 16)
            sp.dma_start(p_tok.rearrange("p (q n) -> p q n", q=2), p_dram).then_inc(ld_p, 16)

            w_gate = a["w_exp_gate"][0].rearrange("e (p c) n -> e p (c n)", c=KD)
            w_up = a["w_exp_up"][0].rearrange("e (p c) n -> e p (c n)", c=KD)
            w_down = a["w_exp_down"][0].rearrange("e (p c) n -> e p (c n)", c=2)

            def load_expert(e, slot, arrived):
                for at, src in ((0, w_gate), (2048, w_up), (4096, w_down)):
                    sp.dma_start(slot[:, at:at + 2048], src[e]).then_inc(arrived, 16)

            load_expert(3, e_slot[3], ld_e[3])
            for k in range(SLOTS):
                before = items[len(items) - SLOTS + k]
                sp.wait_ge(before[2], before[3])
                load_expert(k, e_slot[k], ld_e[k])
            with sp.Fori(1, QUADS) as it:
                for k in range(4):
                    sp.wait_ge(down_done, it * 4 + (k - 3))
                    load_expert(bass.ds(it * 4 + k, 1), e_slot[k], ld_e[k])
            wp = a["w_ple_proj"][0].rearrange("(c p) n -> p c n", p=P)
            wg = a["w_ple_gate"][0].rearrange("(c p) n -> p c n", p=P)
            for k, src in enumerate((wp, wg[:, :, 0:512], wg[:, :, 512:1024])):
                sp.wait_ge(down_done, EXPERTS - 3 + k)
                n = src.shape[1] * src.shape[2]
                sp.dma_start(e_slot[k][:, 0:n].rearrange("p (c n) -> p c n", c=src.shape[1]), src).then_inc(ld_e[k], 16)

            sp.wait_ge(down_done, EXPERTS)
            sp.wait_ge(over_ready, 1)
            n_over = sp.value_load(over[0:1, 15:16], min_val=0, max_val=MAX_OVER)
            with sp.If(n_over > 0):
                with sp.Fori(0, MAX_OVER) as it:
                    with sp.If(n_over > it):
                        sp.wait_ge(f_acc, it + 1)
                        e = sp.value_load(over[0:1, bass.ds(it, 1)], min_val=0, max_val=EXPERTS - 1)
                        load_expert(bass.ds(e, 1), e_slot[3], ld_f)
            for q in range(QT):
                sp.wait_ge(out_done, q + 1)
                sp.dma_start(out_dram[:, q, :], xnv[:, q, :]).then_inc(o_dma, 16)
            sp.wait_ge(o_dma, 32)

        @block.tensor
        def _(pe):
            def mm(out, lhsT, rhs, start, stop):
                return pe.matmul(out, lhsT, rhs, start=start, stop=stop, skip_group_check=True)

            def norm_T(m):
                for k in range(4):
                    for i in range(2):
                        c = 2 * k + i
                        for q in range(QT):
                            pe.wait_ge(xn_done, 2 * m + q + 1)
                            src = xnv[:, q, c:D:KD] if m == 1 else xnv[:, q, c * P:(c + 1) * P]
                            last = pe.transpose(ps[:, k, (i * 2 + q) * P:(i * 2 + q + 1) * P], src, ident)
                    last.then_inc(xT_done, 1)

            pe.wait_ge(ld_vec, 16 * 9)
            pe.wait_ge(ld_cst, 16)
            pe.transpose(ps[:, 6, 0:V_ALL], vrows[0:V_ALL, :], ident[0:V_ALL, 0:V_ALL]).then_inc(vec_t, 1)
            norm_T(0)

            def project(g):
                name, it, width, parts = GRP[g]
                bank = g % 2
                arrived(pe, it)
                if g == 0:
                    pe.wait_ge(hT_done, 4)
                if g >= 2:
                    pe.wait_ge(seg_ready, g - 1)
                w = weights(it, KD, width)
                at = 0
                for part in parts:
                    kind, c0 = part[:2]
                    if kind == "tokq":
                        todo = [(part[2], lambda c: hTv[:, c, part[3] * P:(part[3] + 1) * P],
                                 lambda c: w[:, c, c0:c0 + part[2]])]
                    elif kind == "tok":
                        todo = [(part[2], lambda c, q=q: hTv[:, c, q * P:(q + 1) * P],
                                 lambda c: w[:, c, c0:c0 + part[2]]) for q in range(QT)]
                    elif kind == "headpair":
                        todo = [(T, lambda c: w[:, c, c0 * P:(c0 + 1) * P], lambda c: hTv[:, c, :])]
                    else:
                        todo = [(T, lambda c: w[:, c, c0:c0 + P], lambda c: hTv[:, c, :])]
                    for n, lhsT, rhs in todo:
                        for c in range(KD):
                            last = mm(ps[:, bank, at:at + n], lhsT(c), rhs(c), c == 0, c == KD - 1)
                        at += n
                last.then_inc(proj_done, 1)

            def scores(s):
                _, kv, qs, j, _ = SLOT_LIST[s]
                if s in (0, 4):
                    pe.wait_ge(seg_ready, 3 if s == 0 else 12)
                if s >= 1:
                    pe.wait_ge(max_done, s)
                kZ = kv[:, 0:512].rearrange("p (g t) -> p g t", g=2)
                q0, q1 = qs[:, j * T:j * T + P], qs[:, j * T + P:(j + 1) * T]
                for u in range(2):
                    mm(ps[:, 2 + u, 0:128], q0, kZ[:, u, 0:128], True, True)
                    mm(ps[:, 2 + u, 128:256], q1, kZ[:, u, 128:256], True, True)
                    last = mm(ps[:, 2 + u, 256:384], q1, kZ[:, u, 0:128], True, True)
                last.then_inc(scores_done, 1)

            def weights_T(s):
                pe.wait_ge(prob_done, s + 1)
                if s >= 1:
                    pe.wait_ge(pT_copied, s)
                for u in range(2):
                    for at, src in ((0, 0), (128, 256), (256, 128)):
                        last = pe.transpose(ps[:, 4 + u, at:at + P], sc[:, u, src:src + P], ident)
                last.then_inc(pT_done, 1)

            def pv(s):
                _, kv, _, j, br = SLOT_LIST[s]
                tile, opens, closes = tile_of(s)
                pe.wait_ge(pT_copied, s + 1)
                if opens and tile >= 2:
                    pe.wait_ge(y_copied, tile - 1)
                if s == 3:
                    pe.wait_ge(cmp_gel, 1)
                v = kv[:, 512:768].rearrange("p (q n) -> p q n", q=2)
                bank = 6 + tile % 2
                if closes and s >= 4:
                    if s == 5:
                        pe.wait_ge(cmp_pTc, 1)
                    for u in range(2):
                        mm(ps[HD * u:HD * (u + 1), bank, 0:T], vcZ[:, u, j, :], csT[:, u, :], False, False)
                for u in range(2):
                    out = ps[HD * u:HD * (u + 1), bank, :]
                    mm(out[:, 0:T], v[:, 0, HD * u:HD * (u + 1)], pT[:, u, 0:256], opens, False)
                    last = mm(out[:, P:T], v[:, 1, HD * u:HD * (u + 1)], pT[:, u, 256:384], False, closes)
                last.then_inc(pv_done, 1)

            def compress_hidden():
                pe.wait_ge(cmp_in, 2)
                pe.wait_ge(y_copied, 2)
                for v, (it, src) in enumerate((("w1k", kcP), ("w1v", vcP))):
                    arrived(pe, it)
                    w = weights(it, CMP_PAIRS, 256)
                    for hc in range(2):
                        at = 256 + (v * 2 + hc) * 2 * N_CMP
                        for l in range(CMP_PAIRS):
                            last = mm(ps[:, 7, at:at + 2 * N_CMP], w[:, l, hc * P:(hc + 1) * P],
                                      src[:, :, l, :], l == 0, l == CMP_PAIRS - 1)
                    last.then_inc(cmp_hid, 1)

            def compress_kv():
                pe.wait_ge(cmp_hready, 1)
                pe.wait_ge(ld_cmp, 16 * 2)
                pe.wait_ge(y_copied, 4)
                for g in range(2):
                    for hc in range(2):
                        mm(ps[HD * g:HD * (g + 1), 7, 256:256 + N_CMP], w2k[:, hc, :],
                           hid[:, 0, hc, g, 0:N_CMP], hc == 0, hc == 1)
                for g in range(2):
                    for r in range(4):
                        for hc in range(2):
                            last = mm(ps[32 * r:32 * (r + 1), 7, 384 + HD * g:384 + HD * (g + 1)],
                                      hid[:, 1, hc, g, :], w2v[:, hc, :], hc == 0, hc == 1)
                last.then_inc(cmp_kv, 1)

            def compress_scores():
                pe.wait_ge(cmp_kvc, 1)
                out = ps[:, 7, 256:496].rearrange("p (g j q c) -> p g j q c", g=2, j=4, q=2)
                for j in range(4):
                    for q in range(QT):
                        last = mm(out[:, :, j, q, :], q_nsa[:, j * T + q * P:j * T + (q + 1) * P], kcZ, True, True)
                last.then_inc(cmp_sc, 1)

            def compress_T():
                pe.wait_ge(cmp_p, 1)
                for g in range(2):
                    for q in range(QT):
                        last = pe.transpose(ps[:, 7, g * T + q * P:g * T + (q + 1) * P], csP[:, q, g, :, :], ident)
                last.then_inc(cmp_pT, 1)

            for g in range(3):
                project(g)
            for s in range(NS):
                scores(s)
                if s >= 1:
                    weights_T(s - 1)
                if s == 5:
                    compress_scores()
                if s == 6:
                    compress_T()
                for g in SLOT_GROUPS[s]:
                    project(g)
                if s >= 1:
                    pv(s - 1)
                if s == 3:
                    project(11)
                    compress_hidden()
                if s == 4:
                    compress_kv()
            weights_T(NS - 1)
            project(20)
            pv(NS - 1)
            for g in range(21, 24):
                project(g)

            def hgrn_A(h):
                pe.wait_ge(h_ops, h + 1)
                if h >= 1:
                    pe.wait_ge(h_Am, h)
                for q in range(QT):
                    o = ps[:, 4, q * P:(q + 1) * P].rearrange("p (c a) -> p c a", c=4)
                    c = slice(q * P, (q + 1) * P)
                    qc = qq[:, c].rearrange("p (c a) -> p c a", c=4)
                    mm(o[:, :, 16:32], kk[:, c], qc[:, :, 16:32], True, True)
                    mm(o[:, :, 0:16], kkL[:, c], qc[:, :, 0:16], True, True)
                for q in range(QT):
                    last = pe.transpose(ps[:, 4, (2 + q) * P:(3 + q) * P], kd[:, q * P:(q + 1) * P], ident)
                last.then_inc(h_A, 1)

            def hgrn_U(h):
                pe.wait_ge(h_Am, h + 1)
                pe.wait_ge(h_iB, h + 1)
                if h >= 1:
                    pe.wait_ge(h_S, h)
                mm(ps[:, 5, :], kdT[:, 0, :], iB[:, 0, :, :], True, True)
                mm(ps[:, 6, 0:384], kdT[:, 1, :], iB[:, 1, 0:3, :], True, True).then_inc(h_U, 1)

            def hgrn_O(h):
                pe.wait_ge(h_S, h + 1)
                if h >= 1:
                    pe.wait_ge(h_osb, h)
                for q in range(QT):
                    mm(ps[:, 7, q * P:(q + 1) * P], Am[:, q, :], hi[:, q * 512 + h * P:q * 512 + (h + 1) * P], True, False)
                    for c in range(4):
                        cc = 4 * q + c
                        if cc == 0:
                            continue
                        last = mm(ps[32 * c:32 * (c + 1), 7, q * P:(q + 1) * P], qe[h % 2][:, 32 * cc:32 * (cc + 1)],
                                  hS[:, cc - 1, :], False, c == 3)
                last.then_inc(h_O, 1)

            def hgrn_T():
                pe.wait_ge(h_y, 1)
                for k in range(2):
                    for i in range(2):
                        for q in range(QT):
                            last = pe.transpose(ps[:, 4 + k, (2 * i + q) * P:(2 * i + q + 1) * P],
                                                osb[:, q, 2 * k + i, :], ident)
                    last.then_inc(h_yT, 1)

            def ssd_X():
                pe.wait_ge(s_silu, 2)
                pe.wait_ge(h_yTc, 2)
                for q in range(QT):
                    for k in range(4):
                        pe.transpose(ps[:, 4 + q, k * P:(k + 1) * P], conv[:, k * T + q * P:k * T + (q + 1) * P], ident)
                for q in range(QT):
                    pe.transpose(ps[:, 6, q * P:(q + 1) * P], conv[:, 4 * T + q * P:4 * T + (q + 1) * P], ident)
                for q in range(QT):
                    mm(ps[:, 6, 256 + 8 * q:264 + 8 * q], tri64, dtA[:, 8 * q:8 * q + 8], True, True)
                    last = mm(ps[:, 6, 272 + 8 * q:280 + 8 * q], blk64, dtA[:, 8 * q:8 * q + 8], True, True)
                last.then_inc(s_X, 1)

            def ssd_B(q):
                if q == 0:
                    pe.wait_ge(s_Xcopy, 1)
                    pe.wait_ge(s_acs, 1)
                else:
                    pe.wait_ge(s_state, 1)
                    pe.wait_ge(s_y, 1)
                for h in range(HEADS):
                    mm(ps[:, 4 + h // 4, (h % 4) * P:(h % 4 + 1) * P],
                       dtA[:, 8 * q + h:8 * q + h + 1].to_broadcast([P, P]), tri64, True, True)
                for g in range(2):
                    last = mm(ps[:, 6, g * P:(g + 1) * P], BZ[:, g, q * P:(q + 1) * P],
                              conv[:, 5 * T + q * P:5 * T + (q + 1) * P], True, True)
                last.then_inc(s_B, 1)

            def ssd_Y(q):
                pe.wait_ge(s_L, q + 1)
                for h in range(HEADS):
                    mm(ps[:, 7, h * HD:(h + 1) * HD], Lm[:, h, :], xdt[:, q, h, :], True, True)
                for c in range(2 - q):
                    last = mm(ps[:, 4 + c, :], Btok[:, q, :], xwB[:, c, :, :], True, True)
                last.then_inc(s_Y, 1)

            def ssd_off(q):
                pe.wait_ge(s_state, q + 1)
                for c in range(2):
                    t0 = 5 * T + (2 * q + c) * S_CHUNK
                    last = mm(ps[S_CHUNK * c:S_CHUNK * (c + 1), 6, :], conv[:, t0:t0 + S_CHUNK], sS[:, 2 * q + c, :],
                              True, True)
                last.then_inc(s_off, 1)

            def ssd_T():
                pe.wait_ge(s_n, 1)
                for k in range(2):
                    for i in range(2):
                        c = (2 * k + i) * P
                        for q in range(QT):
                            last = pe.transpose(ps[:, 4 + k, (2 * i + q) * P:(2 * i + q + 1) * P], yd[:, q, c:c + P], ident)
                    last.then_inc(s_yT, 1)

            def merge_gate(i):
                n, k = ORDER[i // 4], i % 4
                it = f"g{n}{k // 2}"
                arrived(pe, it)
                if i == 0:
                    pe.wait_ge(seg_ready, NG)
                if i >= 2:
                    pe.wait_ge(g_tanh, i - 1)
                w = weights(it, KD, 512)
                for e in range(2):
                    c0 = ((2 * k + e) % 4) * P
                    for c in range(KD):
                        last = mm(ps[:, i % 2, e * T:(e + 1) * T], w[:, c, c0:c0 + P], hTv[:, c, :], c == 0, c == KD - 1)
                last.then_inc(g_done, 1)

            def merge_branch(i):
                n, k = ORDER[i // 4], i % 4
                arrived(pe, f"b{n}")
                if i == 0:
                    pe.wait_ge(y_copied, 8)
                if i >= 2:
                    pe.wait_ge(u_done, i - 1)
                if i == 8:
                    pe.wait_ge(h_yTc, 2)
                if i == 12:
                    pe.wait_ge(s_yTc, 2)
                w = weights(f"b{n}", 4, D)
                yT = (yT_a, yT_b, yT_c, yT_d)[n][:, :].rearrange("p (c t) -> p c t", c=4)
                for e in range(2):
                    c0 = (2 * k + e) * P
                    for c in range(4):
                        last = mm(ps[:, 2 + i % 2, e * T:(e + 1) * T], w[:, c, c0:c0 + P], yT[:, c, :], c == 0, c == 3)
                last.then_inc(yp_done, 1)

            for i in range(16):
                if 1 <= i <= 4:
                    hgrn_O(i - 1)
                if i < 4:
                    hgrn_A(i)
                if i == 5:
                    hgrn_T()
                if i == 7:
                    ssd_X()
                if i == 8:
                    ssd_Y(0)
                if i == 9:
                    ssd_B(1)
                if i == 10:
                    ssd_off(1)
                if i == 11:
                    ssd_T()
                merge_gate(i)
                if i < 4:
                    hgrn_U(i)
                if i == 7:
                    ssd_B(0)
                if i == 8:
                    ssd_off(0)
                if i == 9:
                    ssd_Y(1)
                merge_branch(i)

            for q in range(QT):
                for dh in range(2):
                    arrived(pe, f"wo{dh}")
                    if q == 0 and dh == 0:
                        pe.wait_ge(u_done, 16)
                    w = weights(f"wo{dh}", KD, 512)
                    for c in range(KD):
                        last = mm(ps[:, 4 + 2 * q + dh, :], uT[:, c * T + q * P:c * T + (q + 1) * P], w[:, c, :],
                                  c == 0, c == KD - 1)
                    last.then_inc(wo_done, 1)

            norm_T(1)
            pe.wait_ge(ld_moe, 16 * 5)
            pe.wait_ge(hT_done, 8)
            wrv = wr.rearrange("p (c n) -> p c n", c=KD)
            for q in range(QT):
                for c in range(KD):
                    last = mm(ps[:, 4, 64 * q:64 * q + 36], hTv[:, c, q * P:(q + 1) * P], wrv[:, c, :], c == 0, c == KD - 1)
            last.then_inc(rt_done, 1)
            pe.wait_ge(ld_p, 16)
            for k in range(2):
                for q in range(QT):
                    last = pe.transpose(ps[:, 5, (2 * k + q) * P:(2 * k + q + 1) * P],
                                        p_tok[:, q * PLE + k * P:q * PLE + (k + 1) * P], ident)
            last.then_inc(ple_T, 1)

            pe.wait_ge(m_mask, 1)
            mm(ps[:, 4, 0:32], strict, mask[:, 0, :], True, True)
            mm(ps[:, 4, 32:64], strict, mask[:, 1, :], True, False)
            mm(ps[:, 4, 32:64], ones, mask[:, 0, :], False, True)
            mm(ps[:, 4, 64:96], ones, mask[:, 0, :], True, False)
            mm(ps[:, 4, 64:96], ones, mask[:, 1, :], False, True).then_inc(m_pos, 1)

            def gather(k, first=False):
                pe.wait_ge(m_S, k + 1)
                if not first:
                    pe.wait_ge(m_Gc, k)
                for c in range(KD):
                    for q in range(QT):
                        last = mm(ps[:, 4 + c // 4, (c % 4) * P:(c % 4 + 1) * P], xnv[:, q, c:D:KD],
                                  onehot[:, q * P:(q + 1) * P], q == 0, q == 1)
                last.then_inc(m_G, 1)

            def scatter_matrix(k, first=False):
                pe.wait_ge(m_Sw, k + 1)
                if not first:
                    pe.wait_ge(acc_done, k * 2)
                for q in range(QT):
                    last = pe.transpose(ps[:, 6, q * P:(q + 1) * P], onehot_w[:, q * P:(q + 1) * P], ident)
                last.then_inc(m_ST, 1)

            def act_T(it, i):
                r = slice(CAP * i, CAP * (i + 1))
                for j in range(2):
                    last = pe.transpose(ps[:, i % 2, j * CAP:(j + 1) * CAP], act_tok[r, j:FF:2], ident[r, r])
                last.then_inc(a_T, 1)

            def gate_up(it, i, before=None):
                pe.wait_ge(ld_e[i], it * 48 + 48)
                if i == 0:
                    pe.wait_ge(m_Gc, it + 1)
                w = e_slot[i][:, 0:4096].rearrange("p (b c n) -> p b c n", b=2, c=KD)
                for c in range(KD):
                    if c == KD // 2 and before is not None:
                        pe.wait_ge(act_done, before[0] * 4 + (before[1] + 1))
                    last = mm(ps[CAP * i:CAP * (i + 1), i % 2, :], gath[:, c, CAP * i:CAP * (i + 1)], w[:, :, c, :],
                              c == 0, c == KD - 1)
                    if c == KD // 2 and before is not None:
                        act_T(*before)
                last.then_inc(gu_done, 1)

            def down(it, i):
                pe.wait_ge(a_Tc, it * 4 + (i + 1))
                wv = e_slot[i][:, 4096:6144].rearrange("p (j n) -> p j n", j=2)
                for dh in range(2):
                    for j in range(2):
                        last = mm(ps[CAP * i:CAP * (i + 1), 2 + dh, :], actT[i % 2][:, j * CAP:(j + 1) * CAP],
                                  wv[:, j, dh * 512:(dh + 1) * 512], j == 0, j == 1)
                last.then_inc(down_done, 1)

            def scatter(k, q):
                if q == 0:
                    pe.wait_ge(m_y, k + 1)
                    pe.wait_ge(m_STc, k + 1)
                else:
                    pe.wait_ge(acc_done, k * 2 + 1)
                for dh in range(2):
                    last = mm(ps[:, 6 + dh, :], scat[:, q, :], ys[:, dh * 512:(dh + 1) * 512], True, True)
                last.then_inc(sc_done, 1)

            pe.wait_ge(ple_Tc, 1)
            gather(0, first=True)
            gate_up(0, 0)
            gate_up(0, 1, (0, 0))
            down(0, 0)
            gate_up(0, 2, (0, 1))
            down(0, 1)
            gate_up(0, 3, (0, 2))
            gather(1)
            scatter_matrix(0, first=True)
            down(0, 2)

            def group(it, last_group=False):
                gate_up(it, 0, (it - 1, 3))
                down(it - 1, 3)
                gate_up(it, 1, (it, 0))
                scatter(it - 1, 0)
                down(it, 0)
                gate_up(it, 2, (it, 1))
                scatter(it - 1, 1)
                down(it, 1)
                gate_up(it, 3, (it, 2))
                if not last_group:
                    gather(it + 1)
                scatter_matrix(it)
                down(it, 2)

            with pe.Fori(1, QUADS - 1) as it:
                group(it)
            group(QUADS - 1, last_group=True)
            pe.wait_ge(act_done, EXPERTS)
            act_T(QUADS - 1, 3)
            down(QUADS - 1, 3)
            scatter(QUADS - 1, 0)
            scatter(QUADS - 1, 1)

            pe.wait_ge(over_ready, 1)
            n_over = pe.value_load(over[0:1, 15:16], min_val=0, max_val=MAX_OVER)
            with pe.If(n_over > 0):
                with pe.Fori(0, MAX_OVER) as it:
                    with pe.If(n_over > it):
                        pe.wait_ge(ld_f, it * 48 + 48)
                        for b in range(2):
                            wv = e_slot[3][:, b * 2048:(b + 1) * 2048].rearrange("p (c n) -> p c n", c=KD)
                            for j in range(2):
                                for c in range(KD):
                                    last = mm(ps[:, b, j * T:(j + 1) * T], wv[:, c, j:FF:2], hTv[:, c, :],
                                              c == 0, c == KD - 1)
                        last.then_inc(f_gu, 1)
                        pe.wait_ge(f_act_done, it + 1)
                        wv = e_slot[3][:, 4096:6144].rearrange("p (j n) -> p j n", j=2)
                        av = f_act.rearrange("p (j t) -> p j t", j=2)
                        for q in range(QT):
                            for dh in range(2):
                                for j in range(2):
                                    last = mm(ps[:, 4 + 2 * q + dh, :], av[:, j, q * P:(q + 1) * P],
                                              wv[:, j, dh * 512:(dh + 1) * 512], j == 0, j == 1)
                        last.then_inc(f_down, 1)

            def arrived_ple(k):
                pe.wait_ge(ld_e[k], 48 * QUADS + 16)

            arrived_ple(0)
            pe.wait_ge(ple_Tc, 1)
            pe.wait_ge(x3_done, 1)
            w = e_slot[0][:, 0:2048].rearrange("p (c n) -> p c n", c=2)
            pv_ = pT_ple.rearrange("p (c t) -> p c t", c=2)
            for q in range(QT):
                for dh in range(2):
                    for c in range(2):
                        last = mm(ps[:, 4 + 2 * q + dh, :], pv_[:, c, q * P:(q + 1) * P], w[:, c, dh * 512:(dh + 1) * 512],
                                  c == 0, c == 1)
            last.then_inc(ple_p, 1)
            norm_T(2)
            pe.wait_ge(hT_done, 12)
            for dh in range(2):
                arrived_ple(1 + dh)
                w = e_slot[1 + dh][:, 0:4096].rearrange("p (c n) -> p c n", c=KD)
                for q in range(QT):
                    for c in range(KD):
                        last = mm(ps[:, 2 * q + dh, :], hTv[:, c, q * P:(q + 1) * P], w[:, c, :], c == 0, c == KD - 1)
                    last.then_inc(ple_g, 1)

        @block.scalar
        def _(act):
            cp, A = act.copy, act.activation

            def square_root(m):
                for q in range(QT):
                    if m == 0:
                        act.wait_ge(ld_x[q], 16)
                    elif m == 1:
                        act.wait_ge(x2_done, 2 * (q + 1))
                    elif m == 2:
                        act.wait_ge(x3_done, 1)
                    else:
                        act.wait_ge(x4_done, 4)
                    A(xnv[:, q, :], xv[:, q, :], ACT.Square, accum_out=ssq[:, q:q + 1]).then_inc(ssq_done, 1)
                for q in range(QT):
                    act.wait_ge(ms_done, 2 * m + q + 1)
                    act.sqrt(rms[:, q:q + 1], ms[:, q:q + 1]).then_inc(sqrt_done, 1)

            square_root(0)

            def evac(g):
                name = GRP[g][0]
                b = ps[:, g % 2, :]
                act.wait_ge(proj_done, g + 1)
                if name in ("kv_swa", "kv_slc", "kv_win"):
                    t = {"kv_swa": kv_swa, "kv_slc": kv_slc, "kv_win": kv_win}[name]
                    act.wait_ge(zeroed, 1)
                    cp(t[0:64, 0:256], b[0:64, 0:256])
                    cp(t[64:128, 256:512], b[64:128, 0:256])
                    cp(t[:, 512:768], b[:, 256:512]).then_inc(seg_ready, 1)
                    return
                if name in ("kc", "vc"):
                    t = kc_raw if name == "kc" else vc_raw
                    for g2 in range(2):
                        for m in range(2):
                            last = cp(t[HD * m:HD * (m + 1), g2 * T:(g2 + 1) * T], b[HD * g2:HD * (g2 + 1), 0:T])
                    last.then_inc(seg_ready, 1)
                    return
                dst = {0: q_swa[:, 0:512], 1: q_swa[:, 512:1024], 3: gate_raw[:, :], 4: z_seg[:, 0:512],
                       5: z_seg[:, 512:1024], 10: q_nsa[:, 0:512],
                       11: q_nsa[:, 512:1024], 12: hq[:, 0:512], 13: hq[:, 512:1024], 14: hf[:, 0:512],
                       15: hf[:, 512:1024], 16: hi[:, 0:512], 17: hi[:, 512:1024], 18: hg[:, 0:512],
                       19: hg[:, 512:1024], 20: xbc[:, 0:512], 21: xbc[:, 512:1024], 22: xbc[:, 1024:1536],
                       23: dt_raw[:, :]}[g]
                scale = HD ** -0.5 if name in ("q_swa", "q_nsa") else 1.0
                act.mul(dst, b[:, 0:dst.shape[1]], scale).then_inc(seg_ready, 1)

            def exps(s):
                act.wait_ge(max_done, s + 1)
                for u in range(2):
                    for q, (lo, up) in enumerate(((0, 128), (128, 384))):
                        last = A(sc[:, u, lo:up], sc[:, u, lo:up], ACT.Exp, bias=negm[:, 2 * q + u:2 * q + u + 1],
                                 accum_out=esum[:, 2 * q + u:2 * q + u + 1])
                if s < 4:
                    last = A(es, es, ACT.Exp)
                last.then_inc(exp_done, 1)

            def y_tile(s):
                tile, _, closes = tile_of(s)
                if closes:
                    act.wait_ge(pv_done, s + 1)
                    dst = (yT_a if tile < 4 else yT_c)[:, (tile % 4) * T:(tile % 4 + 1) * T]
                    cp(dst, ps[:, 6 + tile % 2, 0:T]).then_inc(y_copied, 1)

            for g in range(3):
                evac(g)
            for s in range(NS):
                exps(s)
                if s == 6:
                    act.wait_ge(cmp_sub, 1)
                    A(cs, cs, ACT.Exp).then_inc(cmp_exp, 1)
                for g in SLOT_GROUPS[s]:
                    evac(g)
                    if g == 3:
                        act.wait_ge(seg_ready, 4)
                        A(gsig, gate_raw[:, :], ACT.Tanh, scale=0.5).then_inc(gate_tanh, 1)
                if s >= 1:
                    y_tile(s - 1)
                if s == 3:
                    evac(11)
                    act.wait_ge(cmp_gel, 1)
                    A(hidg, hidg, ACT.Tanh, scale=GELU_A).then_inc(cmp_tanh, 1)
                if s == 4:
                    act.wait_ge(cmp_kv, 1)
                    act.wait_ge(zeroed, 1)
                    for g in range(2):
                        act.mul(kcZ[HD * g:HD * (g + 1), g, :], ps[HD * g:HD * (g + 1), 7, 256:256 + N_CMP], 0.5)
                    for r in range(4):
                        last = act.mul(vcZ[32 * r:32 * (r + 1), :, r, :],
                                       ps[32 * r:32 * (r + 1), 7, 384:512].rearrange("p (g d) -> p g d", g=2), 0.5)
                    last.then_inc(cmp_kvc, 1)
            evac(20)
            y_tile(NS - 1)

            act.wait_ge(h_arg, 1)
            A(lbt, lbt, ACT.Exp)
            A(h_k, hf[:, :], ACT.Exp).then_inc(h_exp, 1)
            act.wait_ge(scores_done, NS)
            A(g_th, hg[:, :], ACT.Tanh, scale=0.5).then_inc(hg_tanh, 1)
            act.wait_ge(h_f, 1)
            A(hf[:, :], hf[:, :], ACT.Ln).then_inc(h_log, 1)
            for g in range(21, 24):
                evac(g)

            def hgrn_exps(h):
                act.wait_ge(h_diff, h + 1)
                b = h_b[:, h * T:(h + 1) * T]
                A(e1, t1, ACT.Exp).then_inc(h_e, 1)
                A(e2, t1, ACT.Exp, scale=-1.0).then_inc(h_e, 1)
                A(e3, b, ACT.Exp).then_inc(h_e, 1)
                A(hdec[h % 2], b[:, H_CHUNK - 1:T:H_CHUNK], ACT.Exp)
                A(e4, t4, ACT.Exp).then_inc(h_e, 1)

            def merge_tanh(i):
                act.wait_ge(g_done, i + 1)
                if i >= 2:
                    act.wait_ge(u_done, i - 1)
                A(gth[i % 2][:, :], ps[:, i % 2, :], ACT.Tanh, scale=0.5).then_inc(g_tanh, 1)

            def hgrn_square(h):
                act.wait_ge(h_osb, h + 1)
                for q in range(QT):
                    if h or q:
                        act.wait_ge(h_sq, 2 * h + q)
                    A(square_junk, osb[:, q, h, :], ACT.Square,
                      accum_out=hssq[:, 4 * q + h:4 * q + h + 1]).then_inc(h_sq, 1)

            def ssd_exp(q):
                act.wait_ge(s_Larg, q + 1)
                for g in range(2):
                    for c in range(2):
                        t = S_CHUNK * (c + 1) - 1
                        src = ps[HD * g:HD * (g + 1), 4 + g, t:512:P]
                        A(cdec[HD * g:HD * (g + 1), 4 * (2 * q + c):4 * (2 * q + c) + 4], src, ACT.Exp)
                A(Lb, Lb, ACT.Exp).then_inc(s_Lexp, 1)

            hgrn_exps(0)
            for i in range(16):
                if 1 <= i <= 4:
                    hgrn_square(i - 1)
                if i == 4:
                    act.wait_ge(h_ms, 1)
                    act.sqrt(hrms, hms).then_inc(h_rms, 1)
                if i == 6:
                    for k in range(3):
                        act.wait_ge(s_conv, k + 1)
                        A(conv_th[k], conv[:, k * 512:(k + 1) * 512], ACT.Tanh, scale=0.5).then_inc(s_tanh, 1)
                    A(z_th, z_seg[:, :], ACT.Tanh, scale=0.5).then_inc(s_tanh, 1)
                    act.wait_ge(dt_arg, 1)
                    A(dta, dtr, ACT.Abs).then_inc(act_step, 1)
                    act.wait_ge(act_step, 1)
                    A(dta, dta, ACT.Exp, scale=-1.0).then_inc(act_step, 1)
                    A(alog, alog, ACT.Exp)
                    act.wait_ge(act_step, 2)
                    A(dta, dta, ACT.Ln, bias=1.0).then_inc(dt_log, 1)
                if i == 7:
                    act.wait_ge(s_X, 1)
                    cp(hq[:, 0:512], ps[:, 4, :])
                    cp(hq[:, 512:1024], ps[:, 5, :])
                    act.wait_ge(s_acs, 1)
                    cp(kv_win[:, 0:256], ps[:, 6, 0:256])
                    act.wait_ge(zeroed, 3)
                    for g in range(2):
                        last = cp(BZ[HD * g:HD * (g + 1), g, :], conv[HD * g:HD * (g + 1), 4 * T:5 * T])
                    last.then_inc(s_Xcopy, 1)
                    A(eacs, acs[:, 0:16], ACT.Exp)
                    A(sdec, sdec, ACT.Exp).then_inc(s_dec, 1)
                merge_tanh(i)
                if i < 3:
                    hgrn_exps(i + 1)
                if i == 7:
                    ssd_exp(0)
                if i == 9:
                    ssd_exp(1)
                if i == 10:
                    act.wait_ge(s_y, 2)
                    for q in range(QT):
                        if q:
                            act.wait_ge(s_sq, 1)
                        A(ytmp[:, 1, :, :], yd[:, q, :].rearrange("p (h n) -> p h n", h=8), ACT.Square,
                          accum_out=sssq[:, q:q + 1]).then_inc(s_sq, 1)
                    act.wait_ge(s_ms, 1)
                    act.sqrt(srms, sms).then_inc(s_rms, 1)

            square_root(1)
            act.wait_ge(rt_sub, 1)
            A(gexp, gexp, ACT.Exp).then_inc(rt_exp, 1)
            act.wait_ge(rt_d, 1)
            A(e21, e21, ACT.Exp).then_inc(rt_e, 1)
            act.wait_ge(ple_T, 1)
            cp(pT_ple, ps[:, 5, :]).then_inc(ple_Tc, 1)

            def tokens(k):
                act.wait_ge(m_G, k + 1)
                for half in range(2):
                    last = cp(gath[:, 4 * half:4 * half + 4, :], ps[:, 4 + half, :].rearrange("p (c s) -> p c s", c=4))
                last.then_inc(m_Gc, 1)

            def outputs(k):
                act.wait_ge(down_done, k * 4 + 4)
                for dh in range(2):
                    last = cp(ys[:, dh * 512:(dh + 1) * 512], ps[:, 2 + dh, :])
                last.then_inc(m_y, 1)

            def silu(it, i):
                act.wait_ge(gu_done, it * 4 + (i + 1))
                r = slice(CAP * i, CAP * (i + 1))
                A(sil[r, :], ps[r, i % 2, 0:FF], ACT.Silu).then_inc(silu_done, 1)

            def act_T_copy(it, i):
                act.wait_ge(a_T, it * 4 + (i + 1))
                cp(actT[i % 2], ps[:, i % 2, 0:2 * CAP]).then_inc(a_Tc, 1)

            tokens(0)
            silu(0, 0)
            for i in range(1, 4):
                act_T_copy(0, i - 1)
                silu(0, i)
            tokens(1)

            def group(it, last_group=False):
                act_T_copy(it - 1, 3)
                silu(it, 0)
                outputs(it - 1)
                for i in range(1, 4):
                    act_T_copy(it, i - 1)
                    silu(it, i)
                if not last_group:
                    tokens(it + 1)

            with act.Fori(1, QUADS - 1) as it:
                group(it)
            group(QUADS - 1, last_group=True)
            act_T_copy(QUADS - 1, 3)
            outputs(QUADS - 1)

            act.wait_ge(over_ready, 1)
            n_over = act.value_load(over[0:1, 15:16], min_val=0, max_val=MAX_OVER)
            with act.If(n_over > 0):
                with act.Fori(0, MAX_OVER) as it:
                    with act.If(n_over > it):
                        act.wait_ge(f_gu, it + 1)
                        A(f_sil, ps[:, 0, :], ACT.Silu).then_inc(f_silu, 1)

            square_root(2)
            for dh in range(2):
                for q in range(QT):
                    act.wait_ge(ple_g, 2 * dh + q + 1)
                    A(gth[q][:, :], ps[:, 2 * q + dh, :], ACT.Tanh, scale=0.5).then_inc(ple_tanh, 1)
                if dh == 0:
                    act.wait_ge(x4_done, 2)
            square_root(3)

        @block.vector
        def _(dve):
            step = Count(dve_step)

            def dep(ins):
                step.on(ins)
                dve.wait_ge(dve_step, step.n)

            tt, ts, stt, cp = dve.tensor_tensor, dve.tensor_scalar, dve.scalar_tensor_tensor, dve.tensor_copy

            def norm(m):
                for q in range(QT):
                    dve.wait_ge(ssq_done, 2 * m + q + 1)
                    ts(ms[:, q:q + 1], ssq[:, q:q + 1], 1.0 / D, EPS, ALU.mult, ALU.add).then_inc(ms_done, 1)
                for q in range(QT):
                    dve.wait_ge(sqrt_done, 2 * m + q + 1)
                    dep(dve.reciprocal(rstd[:, q:q + 1], rms[:, q:q + 1]))
                    if m == 1:
                        stt(xnv[:, q, :], xv[:, q, :], rstd[:, q:q + 1], gffn, ALU.mult, ALU.mult).then_inc(xn_done, 1)
                    elif m < 3:
                        ts(xnv[:, q, :], xv[:, q, :], rstd[:, q:q + 1], None, ALU.mult).then_inc(xn_done, 1)
                    else:
                        stt(xnv[:, q, :], xv[:, q, :], rstd[:, q:q + 1], gf, ALU.mult, ALU.mult).then_inc(out_done, 1)

            def to_hT(m, gain):
                for k in range(4):
                    dve.wait_ge(xT_done, 4 * m + k + 1)
                    if gain is None:
                        cp(hTv[:, 2 * k:2 * k + 2, :], ps[:, k, :].rearrange("p (c t) -> p c t", c=2)).then_inc(hT_done, 1)
                        continue
                    tt(hTv[:, 2 * k:2 * k + 2, :], ps[:, k, :].rearrange("p (c t) -> p c t", c=2),
                       gain[:, 2 * k:2 * k + 2, None].to_broadcast([P, 2, T]), ALU.mult).then_inc(hT_done, 1)

            norm(0)
            dve.wait_ge(vec_t, 1)
            dep(cp(vec[:, :], ps[:, 6, 0:V_ALL]))
            to_hT(0, vec[:, V_GMIX:V_GMIX + 8])
            dve.wait_ge(ld_small, 16 * 4)
            dep(ts(nsinks, sinks, -1.0, None, ALU.mult))
            ts(vgh, vec[:, V_GH:V_GH + 4], 0.5, None, ALU.mult)

            def slot_max(s):
                _, _, _, j, br = SLOT_LIST[s]
                dve.wait_ge(scores_done, s + 1)
                if s == 0:
                    dve.wait_ge(ld_bias, 16)
                tt(sc[:, :, 0:256].rearrange("p u (b k) -> p u b k", b=2),
                   ps[:, 2:4, 0:256].rearrange("p u (b k) -> p u b k", b=2),
                   bias[:, :, j, 0:1, :].to_broadcast([P, 2, 2, P]), ALU.add)
                dep(tt(sc[:, :, 256:384], ps[:, 2:4, 256:384], bias[:, :, j, 1 if br == 0 else 2, :], ALU.add))
                dve.tensor_reduce(negm[:, 0:2], sc[:, :, 0:128], X, ALU.max, negate=True)
                last = dve.tensor_reduce(negm[:, 2:4], sc[:, :, 128:384], X, ALU.max, negate=True)
                if br == 0:
                    dep(last)
                    nv = negm.rearrange("p (q u) -> p q u", q=2)
                    ev = es.rearrange("p (q u) -> p q u", q=2)
                    dep(tt(nv, nv, nsinks[:, None, j:8:4].to_broadcast([P, 2, 2]), ALU.min))
                    last = tt(ev, nv, sinks[:, None, j:8:4].to_broadcast([P, 2, 2]), ALU.add)
                last.then_inc(max_done, 1)

            def slot_norm(s):
                _, _, _, j, br = SLOT_LIST[s]
                dve.wait_ge(exp_done, s + 1)
                if br == 0:
                    dep(tt(esum, esum, es, ALU.add))
                dep(dve.reciprocal(rr, esum))
                if br:
                    rv = rr.rearrange("p (q u) -> p q u", q=2)
                    dep(tt(rv, rv, gsig.rearrange("p (q h b) -> p q h b", q=2, b=3)[:, :, j:8:4, br], ALU.mult))
                for u in range(2):
                    for q, (lo, up) in enumerate(((0, 128), (128, 384))):
                        last = ts(sc[:, u, lo:up], sc[:, u, lo:up], rr[:, 2 * q + u:2 * q + u + 1], None, ALU.mult)
                last.then_inc(prob_done, 1)

            def slot_copy(s):
                dve.wait_ge(pT_done, s + 1)
                cp(pT[:, :, :], ps[:, 4:6, 0:384]).then_inc(pT_copied, 1)

            def compress_inputs():
                dve.wait_ge(seg_ready, 8)
                for raw, dst, at in ((kc_raw, kcP, V_PK), (vc_raw, vcP, V_PV)):
                    for g in range(2):
                        for m in range(2):
                            rows = slice(HD * m, HD * (m + 1))
                            v = raw[rows, g * T + m:g * T + m + 1]
                            windows = bass.AP(v.tensor, v.offset,
                                              [v.ap[0], [2, CMP_PAIRS], [CMP_STRIDE, N_CMP]])
                            last = tt(dst[rows, g, :, :], windows,
                                      vec[rows, at:at + CMP_PAIRS, None].to_broadcast([HD, CMP_PAIRS, N_CMP]), ALU.add)
                    last.then_inc(cmp_in, 1)

            def compress_gelu():
                dve.wait_ge(cmp_hid, 2)
                dep(cp(hidx, ps[:, 7, 256:256 + 120]))
                dep(tt(hidg, hidx, hidx, ALU.mult))
                dep(ts(hidg, hidg, GELU_B, 1.0, ALU.mult, ALU.add))
                tt(hidg, hidg, hidx, ALU.mult).then_inc(cmp_gel, 1)
                dve.wait_ge(cmp_tanh, 1)
                dve.wait_ge(zeroed, 1)
                out = hid.rearrange("p v h g c -> p (v h g) c")[:, :, 0:N_CMP]
                stt(out, hidg.rearrange("p (a c) -> p a c", c=N_CMP), 1.0, hidx.rearrange("p (a c) -> p a c", c=N_CMP),
                    ALU.add, ALU.mult).then_inc(cmp_hready, 1)

            def compress_max():
                dve.wait_ge(cmp_sc, 1)
                dep(tt(cs, ps[:, 7, 256:496].rearrange("p (h q c) -> p h q c", h=8, q=2), cbias, ALU.add))
                cv = cs.rearrange("p h q c -> p (h q) c")
                dep(dve.tensor_reduce(cmx, cv, X, ALU.max, negate=True))
                tt(cv, cv, cmx[:, :, None].to_broadcast([P, 16, N_CMP]), ALU.add).then_inc(cmp_sub, 1)

            def compress_norm():
                dve.wait_ge(cmp_exp, 1)
                dve.wait_ge(zeroed, 1)
                cv = cs.rearrange("p h q c -> p (h q) c")
                dep(dve.tensor_reduce(csum, cv, X, ALU.add))
                dep(dve.reciprocal(csum, csum))
                sv = csum.rearrange("p (h q) -> p h q", q=2)
                dep(tt(sv, sv, gsig.rearrange("p (q h b) -> p h q b", q=2, b=3)[:, :, :, 0], ALU.mult))
                dep(tt(cv, cv, csum[:, :, None].to_broadcast([P, 16, N_CMP]), ALU.mult))
                out = csP.rearrange("p q g r c -> p (g r) q c")[:, :, :, 0:N_CMP]
                tt(out, cs, cvalid[:, None, :, :].to_broadcast([P, 8, 2, N_CMP]), ALU.mult).then_inc(cmp_p, 1)
                dve.wait_ge(cmp_pT, 1)
                cp(csT, ps[:, 7, :].rearrange("p (g t) -> p g t", g=2)).then_inc(cmp_pTc, 1)

            for s in range(NS):
                slot_max(s)
                if s == 1:
                    dve.wait_ge(gate_tanh, 1)
                    dep(ts(gsig, gsig, 1.0, 0.5, ALU.add, ALU.mult))
                slot_norm(s)
                if s == 3:
                    compress_inputs()
                if s == 5:
                    compress_max()
                if s == 6:
                    compress_norm()
                slot_copy(s)
                if s == 3:
                    compress_gelu()

            dve.wait_ge(seg_ready, 20)
            tt(lbt, vec[:, V_LB:V_LB + 4], vec[:, V_LB:V_LB + 4], ALU.subtract)
            ts(hf[:, :], hf[:, :], -1.0, 80.0, ALU.mult, ALU.min).then_inc(h_arg, 1)
            dve.wait_ge(h_exp, 1)
            dep(dve.reciprocal(lbr, lbt))
            dep(tt(lbt, lbt, lbr, ALU.mult))
            dep(tt(lb, lbt, lbt, ALU.subtract))
            dep(ts(olb, lb, -1.0, 1.0, ALU.mult, ALU.add))
            dep(ts(h_b, h_k, 1.0, None, ALU.add))
            dep(dve.reciprocal(h_b, h_b))
            for h in range(H_HEADS):
                c = slice(h * T, (h + 1) * T)
                last = ts(hf[:, c], h_b[:, c], olb[:, h:h + 1], lb[:, h:h + 1], ALU.mult, ALU.add)
            dep(last)
            ts(hf[:, :], hf[:, :], 1e-6, None, ALU.max).then_inc(h_f, 1)
            for h in range(H_HEADS):
                c = slice(h * T, (h + 1) * T)
                last = stt(h_k[:, c], h_k[:, c], olb[:, h:h + 1], h_b[:, c], ALU.mult, ALU.mult)
            dep(last)
            dve.wait_ge(hg_tanh, 1)
            stt(hg[:, :], g_th, 1.0, hg[:, :], ALU.add, ALU.mult)
            dve.wait_ge(h_log, 1)
            for h in range(H_HEADS):
                c = slice(h * T, (h + 1) * T)
                last = dve.tensor_tensor_scan(h_b[:, c], scan_keep, hf[:, c], 0.0, ALU.mult, ALU.add)
            dep(last)

            def hgrn_diff(h):
                b = h_b[:, h * T:(h + 1) * T].rearrange("p (c a) -> p c a", c=H_NC)
                full = [P, H_NC, H_CHUNK]
                mid = b[:, :, H_CHUNK // 2:H_CHUNK // 2 + 1].to_broadcast(full)
                end = b[:, :, H_CHUNK - 1:H_CHUNK].to_broadcast(full)
                tt(t1.rearrange("p (c a) -> p c a", c=H_NC), b, mid, ALU.subtract)
                tt(t4.rearrange("p (c a) -> p c a", c=H_NC), end, b, ALU.subtract).then_inc(h_diff, 1)

            def hgrn_ops(h):
                c = slice(h * T, (h + 1) * T)
                if h >= 1:
                    dve.wait_ge(h_A, h)
                if h >= 2:
                    dve.wait_ge(h_O, h - 1)
                dve.wait_ge(h_e, 4 * h + 1)
                tt(qq, hq[:, c], e1, ALU.mult)
                dve.wait_ge(h_e, 4 * h + 2)
                tt(kk, h_k[:, c], e2, ALU.mult)
                half = lambda v: v.rearrange("p (c a) -> p c a", c=H_NC)[:, :, 0:H_CHUNK // 2]
                tt(half(kkL), half(h_k[:, c]), half(e2), ALU.mult)
                dve.wait_ge(h_e, 4 * h + 3)
                tt(qe[h % 2], hq[:, c], e3, ALU.mult)
                dve.wait_ge(h_e, 4 * h + 4)
                tt(kd, h_k[:, c], e4, ALU.mult).then_inc(h_ops, 1)

            def hgrn_mask(h):
                dve.wait_ge(h_A, h + 1)
                tt(Am, ps[:, 4, 0:256].rearrange("p (q t) -> p q t", q=2), tri32[:, None, :].to_broadcast([P, 2, P]), ALU.mult)
                cp(kdT, ps[:, 4, 256:512].rearrange("p (q t) -> p q t", q=2)).then_inc(h_Am, 1)

            def hgrn_chain(h):
                dve.wait_ge(h_U, h + 1)
                dep(cp(hS[:, 0, :], ps[:, 5, 0:P]))
                for c in range(1, H_NC - 1):
                    u = ps[:, 5 + c // 4, (c % 4) * P:(c % 4 + 1) * P]
                    ins = stt(hS[:, c, :], hS[:, c - 1, :], hdec[h % 2][:, c:c + 1], u, ALU.mult, ALU.add)
                    if c < H_NC - 2:
                        dep(ins)
                ins.then_inc(h_S, 1)

            def hgrn_out(h):
                dve.wait_ge(h_O, h + 1)
                cp(osb[:, :, h, :], ps[:, 7, 0:256].rearrange("p (q v) -> p q v", q=2)).then_inc(h_osb, 1)

            def hgrn_finish():
                dve.wait_ge(h_sq, 8)
                ts(hms, hssq, 1.0 / P, EPS, ALU.mult, ALU.add).then_inc(h_ms, 1)
                dve.wait_ge(h_rms, 1)
                dep(dve.reciprocal(hrstd, hrms))
                dve.wait_ge(h_osb, 4)
                for q in range(QT):
                    for h in range(H_HEADS):
                        last = stt(osb[:, q, h, :], osb[:, q, h, :], hrstd[:, 4 * q + h:4 * q + h + 1],
                                   hg[:, q * 512 + h * P:q * 512 + (h + 1) * P], ALU.mult, ALU.mult)
                last.then_inc(h_y, 1)

            def gain_copy(dst, gain, done, copied):
                for k in range(2):
                    dve.wait_ge(done, k + 1)
                    tt(dst[:, 2 * k * T:(2 * k + 2) * T].rearrange("p (c t) -> p c t", c=2),
                       ps[:, 4 + k, :].rearrange("p (c t) -> p c t", c=2),
                       gain[:, 2 * k:2 * k + 2, None].to_broadcast([P, 2, T]), ALU.mult).then_inc(copied, 1)

            def conv_pair(k):
                dve.wait_ge(seg_ready, 21 + k)
                for f in (2 * k, 2 * k + 1):
                    w = lambda j: vec[:, V_CW + 6 * j + f:V_CW + 6 * j + f + 1]
                    xi, yo = xbc[:, f * T:(f + 1) * T], conv[:, f * T:(f + 1) * T]
                    dep(ts(yo, xi, w(3), vec[:, V_CB + f:V_CB + f + 1], ALU.mult, ALU.add))
                    for j in (2, 1, 0):
                        d = 3 - j
                        ins = stt(yo[:, d:T], xi[:, 0:T - d], w(j), yo[:, d:T], ALU.mult, ALU.add)
                        if j:
                            dep(ins)
                ins.then_inc(s_conv, 1)

            def ssd_silu():
                for k in range(3):
                    dve.wait_ge(s_tanh, k + 1)
                    dep(ts(conv_th[k], conv_th[k], 0.5, 0.5, ALU.mult, ALU.add))
                    c = conv[:, k * 512:(k + 1) * 512]
                    last = tt(c, conv_th[k], c, ALU.mult)
                last.then_inc(s_silu, 1)
                dve.wait_ge(s_tanh, 4)
                dep(ts(z_th, z_th, 0.5, 0.5, ALU.mult, ALU.add))
                dep(tt(z_seg[:, :], z_th, z_seg[:, :], ALU.mult))
                dve.wait_ge(dt_log, 1)
                dep(tt(dt, dtm, dta, ALU.add))
                stt(dtA.rearrange("p (q h) -> p q h", q=2), dt.rearrange("p (q h) -> p q h", q=2), -1.0,
                    alog[:, None, :].to_broadcast([P, 2, 8]), ALU.mult, ALU.mult).then_inc(s_silu, 1)

            def ssd_weights():
                dve.wait_ge(s_X, 1)
                dep(cp(acs, ps[:, 6, 256:288]))
                tt(sdec, acs[:, 16:32], acs[:, 0:16], ALU.subtract).then_inc(s_acs, 1)
                dve.wait_ge(s_dec, 1)
                dep(tt(swt, sdec, dt, ALU.mult))
                dep(tt(swB.rearrange("p (q c h) -> p q c h", q=2, c=2),
                       swt.rearrange("p (q h) -> p q h", q=2)[:, :, None, :].to_broadcast([P, 2, 2, 8]),
                       cm64[:, None, :, None].to_broadcast([P, 2, 2, 8]), ALU.mult))
                dve.wait_ge(s_Xcopy, 1)
                tt(xdt.rearrange("p q h n -> p (q h) n"), xtok.rearrange("p q h n -> p (q h) n"),
                   dt[:, :, None].to_broadcast([P, 16, HD]), ALU.mult)

            def ssd_xw(q):
                for c in range(2 - q):
                    w = swB[:, 16 * q + 8 * c:16 * q + 8 * c + 8, None].to_broadcast([P, 8, HD])
                    tt(xwB[:, c, :, :], xtok[:, q, :, :], w, ALU.mult)

            def ssd_L(q):
                dve.wait_ge(s_B, q + 1)
                b = ps[:, 4:6, :].rearrange("p a (h t) -> p (a h) t", h=4)
                dep(tt(Lb, b, acs[:, 8 * q:8 * q + 8, None].to_broadcast([P, 8, P]), ALU.subtract))
                ts(Lb, Lb, 0.0, None, ALU.min).then_inc(s_Larg, 1)
                dep(tt(CBm[:, q, :, :], ps[:, 6, 0:256].rearrange("p (g t) -> p g t", g=2),
                       tri64[:, None, :].to_broadcast([P, 2, P]), ALU.mult))
                if q:
                    dve.wait_ge(s_Y, 1)
                ssd_xw(q)
                dve.wait_ge(s_Lexp, q + 1)
                tt(Lm.rearrange("p (g r) t -> p g r t", g=2), Lb.rearrange("p (g r) t -> p g r t", g=2),
                   CBm[:, q, :, None, :].to_broadcast([P, 2, 4, P]), ALU.mult).then_inc(s_L, 1)

            def ssd_state(q):
                dve.wait_ge(s_Y, q + 1)
                dve.wait_ge(zeroed, 3)
                if q == 0:
                    for g in range(2):
                        r, c = slice(HD * g, HD * (g + 1)), slice(256 * g, 256 * (g + 1))
                        last = cp(sS[r, 1, c], ps[r, 4, c])
                    dep(last)
                chunk = 1 + q
                for g in range(2):
                    r, c = slice(HD * g, HD * (g + 1)), slice(256 * g, 256 * (g + 1))
                    last = tt(sS[r, chunk + 1, c].rearrange("p (r n) -> p r n", r=4),
                              sS[r, chunk, c].rearrange("p (r n) -> p r n", r=4),
                              cdec[r, 4 * chunk:4 * chunk + 4, None].to_broadcast([HD, 4, HD]), ALU.mult)
                dep(last)
                for g in range(2):
                    r, c = slice(HD * g, HD * (g + 1)), slice(256 * g, 256 * (g + 1))
                    last = tt(sS[r, chunk + 1, c], sS[r, chunk + 1, c], ps[r, 5 - q, c], ALU.add)
                last.then_inc(s_state, 1)

            def ssd_y(q):
                dve.wait_ge(s_off, q + 1)
                y1, y2 = ytmp[:, 0, :, :], ytmp[:, 1, :, :]
                hn = lambda v: v.rearrange("p (h n) -> p h n", h=8)
                tt(y2, xtok[:, q, :, :], dskip[:, :, None].to_broadcast([P, 8, HD]), ALU.mult)
                dep(tt(y1, hn(ps[:, 6, :]), eacs[:, 8 * q:8 * q + 8, None].to_broadcast([P, 8, HD]), ALU.mult))
                dep(tt(y1, y1, hn(ps[:, 7, :]), ALU.add))
                dep(tt(y1, y1, y2, ALU.add))
                tt(hn(yd[:, q, :]), y1, hn(z_seg[:, q * 512:(q + 1) * 512]), ALU.mult).then_inc(s_y, 1)

            def merge_update(i):
                k = i % 4
                dve.wait_ge(yp_done, i + 1)
                dve.wait_ge(g_tanh, i + 1)
                u = uT[:, 2 * k * T:(2 * k + 2) * T]
                b = gth[i % 2][:, :]
                if i < 4:
                    stt(u, b, 1.0, ps[:, 2 + i % 2, :], ALU.add, ALU.mult).then_inc(u_done, 1)
                else:
                    dep(stt(b, b, 1.0, ps[:, 2 + i % 2, :], ALU.add, ALU.mult))
                    tt(u, u, b, ALU.add).then_inc(u_done, 1)

            dve.wait_ge(pv_done, NS)
            hgrn_diff(0)
            dve.wait_ge(zeroed, 2)
            hgrn_ops(0)
            for i in range(16):
                if 1 <= i <= 4:
                    hgrn_out(i - 1)
                if i < 4:
                    hgrn_mask(i)
                    if i < 3:
                        hgrn_diff(i + 1)
                    hgrn_chain(i)
                    if i < 3:
                        hgrn_ops(i + 1)
                if i == 4:
                    hgrn_finish()
                    conv_pair(0)
                if i == 5:
                    gain_copy(yT_b, vgh, h_yT, h_yTc)
                    conv_pair(1)
                    conv_pair(2)
                    dep(tt(dtr.rearrange("p (q h) -> p q h", q=2), dt_raw[:, :].rearrange("p (q h) -> p q h", q=2),
                           dtb[:, None, :].to_broadcast([P, 2, 8]), ALU.add))
                    ts(dtm, dtr, 0.0, None, ALU.max).then_inc(dt_arg, 1)
                if i == 6:
                    ssd_silu()
                if i == 7:
                    ssd_weights()
                    ssd_L(0)
                if i == 8:
                    ssd_state(0)
                    ssd_y(0)
                if i == 9:
                    ssd_L(1)
                    ssd_state(1)
                if i == 10:
                    ssd_y(1)
                    dve.wait_ge(s_sq, 2)
                    ts(sms, sssq, 1.0 / 512, EPS, ALU.mult, ALU.add).then_inc(s_ms, 1)
                    dve.wait_ge(s_rms, 1)
                    dep(dve.reciprocal(srstd, srms))
                    dve.wait_ge(s_y, 2)
                    for q in range(QT):
                        last = ts(yd[:, q, :], yd[:, q, :], srstd[:, q:q + 1], None, ALU.mult)
                    last.then_inc(s_n, 1)
                if i == 11:
                    gain_copy(yT_d, vec[:, V_GS:V_GS + 4], s_yT, s_yTc)
                merge_update(i)

            for n in range(4):
                dve.wait_ge(wo_done, n + 1)
                c = x[:, n * 512:(n + 1) * 512]
                stt(c, ps[:, 4 + n, :], 0.5, c, ALU.mult, ALU.add).then_inc(x2_done, 1)

            dve.wait_ge(x2_done, 4)
            dve.wait_ge(ld_moe, 16 * 5)
            norm(1)
            to_hT(1, None)
            dve.wait_ge(rt_done, 1)
            lv = lg.rearrange("p (q n) -> p q n", q=2)
            dep(cp(lv, ps[:, 4, 0:128].rearrange("p (q n) -> p q n", q=2)[:, :, 0:36]))
            L4, L32 = lv[:, :, 0:4], lv[:, :, 4:36]

            def b3(v, n):
                return v[:, :, None].to_broadcast([P, 2, n])

            def first_max(out, vals, top, n):
                dep(tt(cand[:, :, 0:n], vals, b3(top, n), ALU.is_equal))
                dep(tt(cand[:, :, 0:n], cand[:, :, 0:n], iom[:, None, 0:n].to_broadcast([P, 2, n]), ALU.mult))
                dep(dve.tensor_reduce(mn, cand[:, :, 0:n], X, ALU.min))
                dep(tt(out, cand[:, :, 0:n], b3(mn, n), ALU.is_equal))

            dep(ts(iom, iota, -64.0, None, ALU.add))
            dep(dve.tensor_reduce(gm, L4, X, ALU.max))
            tt(gexp.rearrange("p (q n) -> p q n", q=2), L4, b3(gm, 4), ALU.subtract).then_inc(rt_sub, 1)
            first_max(goh, L4, gm, 4)
            dep(ts(gpen, goh, -1.0, 1e30, ALU.add, ALU.mult))
            v4 = vmask.rearrange("p q (g e) -> p q g e", g=GROUPS)
            dep(tt(v4, L32.rearrange("p q (g e) -> p q g e", g=GROUPS), goh[:, :, :, None].to_broadcast([P, 2, GROUPS, EPG]), ALU.mult))
            dep(tt(v4, v4, gpen[:, :, :, None].to_broadcast([P, 2, GROUPS, EPG]), ALU.add))
            dep(dve.tensor_reduce(m1, vmask, X, ALU.max))
            first_max(oh1, vmask, m1, EXPERTS)
            dep(stt(vmask, oh1, -3e30, vmask, ALU.mult, ALU.add))
            dep(dve.tensor_reduce(m2, vmask, X, ALU.max))
            tt(e21, m2, m1, ALU.subtract).then_inc(rt_d, 1)
            first_max(oh2, vmask, m2, EXPERTS)
            tt(mask, oh1, oh2, ALU.add).then_inc(m_mask, 1)
            dve.wait_ge(m_mask, 1)
            dep(ts(nmask, mask, -1000.0, 1000.0, ALU.mult, ALU.add))
            dve.wait_ge(rt_exp, 1)
            dep(dve.tensor_reduce(gw, gexp.rearrange("p (q n) -> p q n", q=2), X, ALU.add))
            dep(dve.reciprocal(gw, gw))
            dve.wait_ge(rt_e, 1)
            dep(ts(w1, e21, 1.0, None, ALU.add))
            dep(dve.reciprocal(w1, w1))
            dep(tt(w1, w1, gw, ALU.mult))
            dep(tt(w2, w1, e21, ALU.mult))
            dep(tt(oh1, oh1, b3(w1, EXPERTS), ALU.mult))
            dep(tt(oh2, oh2, b3(w2, EXPERTS), ALU.mult))
            cv = comb.rearrange("p (q e) -> p q e", q=2)
            dep(tt(cv, oh1, oh2, ALU.add))

            dve.wait_ge(m_pos, 1)
            dve.memset(posm[:, :, EXPERTS:36], 1000.0)
            dep(tt(posm[:, :, 0:EXPERTS], ps[:, 4, 0:64].rearrange("p (q e) -> p q e", q=2), nmask, ALU.add))
            dep(cp(cnt, ps[:, 4, 64:96]))

            def one_hot(k, first=False):
                if not first:
                    dve.wait_ge(m_G, k)
                    dve.wait_ge(m_Sw, k)
                out = onehot.rearrange("p (q i s) -> p q i s", q=2, i=4)
                tt(out, iota[:, None, None, :].to_broadcast([P, 2, 4, CAP]),
                   posm[:, :, bass.ds(k * 4, 4), None].to_broadcast([P, 2, 4, CAP]), ALU.is_equal).then_inc(m_S, 1)

            def one_hot_weights(k):
                dve.wait_ge(m_S, k + 1)
                tt(onehot_w.rearrange("p (q i s) -> p q i s", q=2, i=4), onehot.rearrange("p (q i s) -> p q i s", q=2, i=4),
                   cv[:, :, bass.ds(k * 4, 4), None].to_broadcast([P, 2, 4, CAP]), ALU.mult).then_inc(m_Sw, 1)

            def copy_scatter_matrix(k):
                dve.wait_ge(m_ST, k + 1)
                cp(scat, ps[:, 6, 0:256].rearrange("p (q t) -> p q t", q=2)).then_inc(m_STc, 1)

            def expert_act(it, i):
                dve.wait_ge(silu_done, it * 4 + (i + 1))
                r = slice(CAP * i, CAP * (i + 1))
                tt(act_tok[r, :], sil[r, :], ps[r, i % 2, FF:2 * FF], ALU.mult).then_inc(act_done, 1)

            def accumulate(k, q):
                dve.wait_ge(sc_done, k * 2 + (q + 1))
                c = xv[:, q, :].rearrange("p (a n) -> p a n", a=2)
                tt(c, c, ps[:, 6:8, :], ALU.add).then_inc(acc_done, 1)

            one_hot(0, first=True)
            one_hot_weights(0)
            one_hot(1)

            dep(stt(comb_over, posm[:, :, 0:EXPERTS], float(CAP), cv, ALU.is_ge, ALU.mult))
            dep(ts(isover, cnt, float(CAP), None, ALU.is_gt))
            dep(dve.tensor_tensor_scan(rank, ones[:, 0:EXPERTS], isover, 0.0, ALU.mult, ALU.add))
            dep(tt(pick, rank[:, None, :].to_broadcast([P, MAX_OVER, EXPERTS]),
                   iota[:, 1:MAX_OVER + 1, None].to_broadcast([P, MAX_OVER, EXPERTS]), ALU.is_equal))
            dep(tt(pick, pick, isover[:, None, :].to_broadcast([P, MAX_OVER, EXPERTS]), ALU.mult))
            dep(tt(pick, pick, iota[:, None, :].to_broadcast([P, MAX_OVER, EXPERTS]), ALU.mult))
            dve.tensor_reduce(over_f[:, 0:MAX_OVER], pick, X, ALU.add)
            dep(cp(over_f[:, 15:16], rank[:, EXPERTS - 1:EXPERTS]))
            cp(over[:, :], over_f).then_inc(over_ready, 1)

            for i in range(4):
                expert_act(0, i)
            copy_scatter_matrix(0)
            one_hot_weights(1)
            one_hot(2)

            def group(it, last_group=False):
                expert_act(it, 0)
                expert_act(it, 1)
                accumulate(it - 1, 0)
                expert_act(it, 2)
                accumulate(it - 1, 1)
                expert_act(it, 3)
                copy_scatter_matrix(it)
                if not last_group:
                    one_hot_weights(it + 1)
                    one_hot(it + 2)

            with dve.Fori(1, QUADS - 1) as it:
                group(it)
            group(QUADS - 1, last_group=True)
            accumulate(QUADS - 1, 0)
            accumulate(QUADS - 1, 1)

            dve.wait_ge(over_ready, 1)
            dve.memset(over_f[:, 0:1], 0.0).then_inc(f_acc, 1)
            n_over = dve.value_load(over[0:1, 15:16], min_val=0, max_val=MAX_OVER)
            with dve.If(n_over > 0):
                with dve.Fori(0, MAX_OVER) as it:
                    with dve.If(n_over > it):
                        e = dve.value_load(over[0:1, bass.ds(it, 1)], min_val=0, max_val=EXPERTS - 1)
                        dve.wait_ge(f_silu, it + 1)
                        tt(f_act, f_sil, ps[:, 1, :], ALU.mult).then_inc(f_act_done, 1)
                        dve.wait_ge(f_down, it + 1)
                        dve.wait_ge(f_acc, it + 1)
                        for q in range(QT):
                            for dh in range(2):
                                c = xv[:, q, dh * 512:(dh + 1) * 512]
                                last = stt(c, ps[:, 4 + 2 * q + dh, :], comb_over[:, q, bass.ds(e, 1)], c, ALU.mult, ALU.add)
                        last.then_inc(f_acc, 1)

            dve.memset(over_f[:, 1:2], 0.0).then_inc(x3_done, 1)
            norm(2)
            to_hT(2, vec[:, V_GPLE:V_GPLE + 8])
            dve.wait_ge(ple_p, 1)
            for dh in range(2):
                for q in range(QT):
                    dve.wait_ge(ple_tanh, 2 * dh + q + 1)
                    b = gth[q][:, :]
                    dep(stt(b, b, 1.0, ps[:, 4 + 2 * q + dh, :], ALU.add, ALU.mult))
                    c = xv[:, q, dh * 512:(dh + 1) * 512]
                    stt(c, b, 0.5, c, ALU.mult, ALU.add).then_inc(x4_done, 1)
            dve.wait_ge(x4_done, 4)
            norm(3)

        @block.gpsimd
        def _(pool):
            pstep = Count(pool_step)

            def clear(dst):
                pstep.on(pool.memset(dst, 0.0))
                pool.wait_ge(pool_step, pstep.n)

            for kv in (kv_swa, kv_slc, kv_win):
                clear(kv[:, 0:512])
            clear(kcZ)
            clear(vcZ)
            clear(hid)
            pool.memset(csP, 0.0).then_inc(zeroed, 1)
            pool.wait_ge(pv_done, NS)
            pool.wait_ge(zeroed, 1)
            pool.memset(kkL, 0.0).then_inc(zeroed, 1)
            pool.wait_ge(seg_ready, 18)
            pool.wait_ge(zeroed, 2)
            for h in range(H_HEADS):
                if h >= 1:
                    pool.wait_ge(h_U, h)
                    pool.wait_ge(h_iB, h)
                v = hi[:, :].rearrange("p (q n) -> p q n", q=2)[:, :, None, h * P:(h + 1) * P].to_broadcast([P, 2, 4, P])
                pool.tensor_tensor(iB, v, cm32[:, None, :, None].to_broadcast([P, 2, 4, P]), ALU.mult).then_inc(h_iB, 1)
            pool.wait_ge(h_yTc, 2)
            pool.wait_ge(h_iB, 4)
            clear(BZ)
            pool.memset(sS, 0.0).then_inc(zeroed, 1)


_INS = ['x', 'p', 'w_in', 'g_mix', 'attn_sinks', 'hgrn_lower_bounds', 'hgrn_norm_g', 'nsa_pos_k', 'nsa_pos_v',
        'nsa_cmp_w1_k', 'nsa_cmp_w2_k', 'nsa_cmp_w1_v', 'nsa_cmp_w2_v', 'ssm_conv_w', 'ssm_conv_b', 'ssm_dt_bias',
        'ssm_A_log', 'ssm_D', 'ssm_norm_g', 'w_branch', 'w_out', 'g_ffn', 'w_router_grp', 'w_router_exp',
        'w_exp_gate', 'w_exp_up', 'w_exp_down', 'g_ple', 'w_ple_gate', 'w_ple_proj', 'g_final']


def kernel(**inputs):
    import concourse.bacc as _bacc
    from concourse.bass_utils import run_bass_kernel_spmd as _run

    nc = _bacc.Bacc("TRN2", target_bir_lowering=False, num_devices=1)
    arrays = {name: np.ascontiguousarray(inputs[name]) for name in _INS}
    arrays["cst"] = shape_constants()
    args = {name: nc.dram_tensor(name, v.shape, mybir.dt.from_np(v.dtype), kind="ExternalInput").ap()
            for name, v in arrays.items()}
    args["out"] = nc.dram_tensor("out", (1, T, D), F32, kind="ExternalOutput").ap()
    hybrid_layer(nc, args)
    r = _run(nc, [arrays], core_ids=[0])
    return r.results[0]["out"]
```

```python
from contextlib import ExitStack

import concourse.bass as bass
import numpy as np
from concourse import mybir

F32, I32 = mybir.dt.float32, mybir.dt.int32
ALU = mybir.AluOpType
ACT = mybir.ActivationFunctionType
X = mybir.AxisListType.X

P = 128
T = 256
QT = T // P
D = 1024
KD = D // P
HEADS, HD = 8, 64
CMP_LEN, CMP_STRIDE = 32, 16
N_CMP = (T - CMP_LEN) // CMP_STRIDE + 1
CMP_PAIRS = CMP_LEN // 2
H_HEADS, H_CHUNK, H_NC = 4, 32, T // 32
S_CHUNK = 64
GROUPS, EXPERTS, FF = 4, 32, 256
CAP = 32
QUADS = EXPERTS // 4
MAX_OVER = 2 * T // (CAP + 1)
EPG = EXPERTS // GROUPS
PLE = 256
EPS = 1e-6
NEG = -1e30
GELU_A, GELU_B = 0.7978845608028654, 0.044715

SWA_Q, SWA_KV, H_Q, H_F, H_I, H_G, NSA_Q = 0, 512, 768, 1280, 1792, 2304, 2816
NSA_KV, NSA_GATE, SSM_Z, SSM_X, SSM_DT, MERGE = 3328, 4096, 4120, 4632, 5400, 5408

SLOTS = 3
SLOT_E = 3 * KD * FF
SLOT = KD * 776

C_ID, C_TRI64, C_BLK64, C_TRI32 = 0, 128, 256, 384
C_CM32, C_CM64, C_SCAN, C_CBIAS = 512, 516, 518, 774
C_CVALID = C_CBIAS + HEADS * QT * N_CMP
C_IOTA = C_CVALID + QT * N_CMP
C_BIAS = C_IOTA + EXPERTS
C_MOE = C_BIAS + HEADS * 3 * P
C_ALL = C_MOE + 2 * P

V_GMIX, V_GPLE, V_GH, V_GS, V_CB, V_CW, V_LB, V_PK, V_PV, V_ALL = 0, 8, 16, 20, 24, 30, 54, 58, 74, 90


def shape_constants():
    c = np.zeros((P, C_ALL), np.float32)
    i, j = np.arange(P)[:, None], np.arange(P)[None, :]
    c[:, C_ID:C_ID + P] = i == j
    c[:, C_TRI64:C_TRI64 + P] = (i <= j) & (i // S_CHUNK == j // S_CHUNK)
    c[:, C_BLK64:C_BLK64 + P] = i // S_CHUNK == j // S_CHUNK
    c[:, C_TRI32:C_TRI32 + P] = (i <= j) & (i // H_CHUNK == j // H_CHUNK)
    c[:, C_CM32:C_CM32 + 4] = i // H_CHUNK == np.arange(4)[None, :]
    c[:, C_CM64:C_CM64 + 2] = i // S_CHUNK == np.arange(2)[None, :]
    c[:, C_SCAN:C_SCAN + T] = np.arange(T)[None, :] % H_CHUNK != 0
    slopes = 2.0 ** (-8.0 * np.arange(1, HEADS + 1) / HEADS)
    end = np.arange(N_CMP) * CMP_STRIDE + CMP_LEN - 1
    pos = np.arange(T).reshape(QT, P).T
    dist = (pos[:, :, None] - end[None, None, :]).astype(np.float32)
    cb = np.where(dist[:, None] >= 0, -slopes[None, :, None, None] * dist[:, None], NEG)
    c[:, C_CBIAS:C_CVALID] = cb.reshape(P, -1)
    c[:, C_CVALID:C_IOTA] = (dist >= 0).reshape(P, -1)
    c[:, C_IOTA:C_BIAS] = np.arange(EXPERTS)[None, :]
    for h in range(HEADS):
        at = C_BIAS + h * 3 * P
        c[:, at:at + P] = np.where(j <= i, -slopes[h] * (i - j), NEG)
        c[:, at + P:at + 2 * P] = np.where(j > i, -slopes[h] * (i - j + P), NEG)
        c[:, at + 2 * P:at + 3 * P] = -slopes[h] * (i - j + P)
    c[:, C_MOE:C_MOE + P] = i < j
    c[:, C_MOE + P:C_ALL] = 1.0
    return c


class Count:

    def __init__(self, sem):
        self.sem, self.n = sem, 0

    def on(self, ins):
        ins.then_inc(self.sem, 1)
        self.n += 1
        return self.n


def hybrid_layer(nc, a):
    ctx = ExitStack()
    with ctx:
        def sb(name, n):
            return ctx.enter_context(nc.sbuf_tensor("s_" + name, [P, n], F32))

        def sem(name):
            return ctx.enter_context(nc.semaphore(name))

        w_in = a["w_in"][0].rearrange("(c p) n -> p c n", p=P)
        w_branch = a["w_branch"][0]
        w_out = a["w_out"][0].rearrange("(c p) n -> p c n", p=P)
        x_dram = a["x"][0].rearrange("(q p) d -> p q d", p=P)
        out_dram = a["out"][0].rearrange("(q p) d -> p q d", p=P)
        p_dram = a["p"][0, 0].rearrange("(q p) d -> p q d", p=P)

        ring = [sb(f"wslot{i}", SLOT) for i in range(SLOTS)]
        x = sb("x", QT * D)
        xn = sb("xn", QT * D)
        hT = sb("hT", KD * T)
        cst = sb("cst", C_MOE)
        vrows = sb("vrows", P)
        vec = sb("vec", V_ALL)
        kv_swa, kv_slc, kv_win = sb("kv_swa", 768), sb("kv_slc", 768), sb("kv_win", 768)
        q_swa, q_nsa = sb("q_swa", 1024), sb("q_nsa", 1024)
        kvc_raw = sb("kvc_raw", 1024)
        kc_raw, vc_raw = kvc_raw[:, 0:512], kvc_raw[:, 512:1024]
        gate_raw, dt_raw = sb("gate_raw", QT * 24), sb("dt_raw", QT * 8)
        arena = sb("segments", 6656)
        hq, hf, hi, hg = (arena[:, k * 1024:(k + 1) * 1024] for k in range(4))
        xbc, z_seg = arena[:, 4096:5632], arena[:, 5632:6656]
        yT_a, yT_c = sb("yT_a", 1024), sb("yT_c", 1024)
        small = sb("small", 512)
        over = ctx.enter_context(nc.sbuf_tensor("s_over", [P, 16], I32))
        work = sb("work", 8064)

        so = [0]

        def sm(n):
            v = small[:, so[0]:so[0] + n]
            so[0] += n
            assert so[0] <= 512
            return v

        wo = [0]

        def wk(n, at=None):
            if at is not None:
                wo[0] = at
            v = work[:, wo[0]:wo[0] + n]
            wo[0] += n
            assert wo[0] <= 8064, wo[0]
            return v

        ident = cst[:, C_ID:C_ID + P]
        tri64, blk64 = cst[:, C_TRI64:C_TRI64 + P], cst[:, C_BLK64:C_BLK64 + P]
        tri32 = cst[:, C_TRI32:C_TRI32 + P]
        cm32, cm64 = cst[:, C_CM32:C_CM32 + 4], cst[:, C_CM64:C_CM64 + 2]
        scan_keep = cst[:, C_SCAN:C_SCAN + T]
        cbias = cst[:, C_CBIAS:C_CVALID].rearrange("p (h q c) -> p h q c", h=HEADS, q=QT)
        cvalid = cst[:, C_CVALID:C_IOTA].rearrange("p (q c) -> p q c", q=QT)
        iota = cst[:, C_IOTA:C_BIAS]
        bias = cst[:, C_BIAS:C_MOE].rearrange("p (g j b k) -> p g j b k", g=2, j=4, b=3)

        xv = x[:, :].rearrange("p (q d) -> p q d", q=QT)
        xnv = xn[:, :].rearrange("p (q d) -> p q d", q=QT)
        hTv = hT[:, :].rearrange("p (c t) -> p c t", c=KD)
        yT_b, yT_d = q_swa, q_nsa
        uT = cst[:, C_BIAS:C_BIAS + KD * T]
        spare = cst[:, C_BIAS + KD * T:C_MOE]

        sc = wk(768, 0).rearrange("p (u k) -> p u k", u=2)
        pT = wk(768).rearrange("p (u k) -> p u k", u=2)
        kcP = wk(480).rearrange("p (g l c) -> p g l c", g=2, l=CMP_PAIRS)
        vcP = wk(480).rearrange("p (g l c) -> p g l c", g=2, l=CMP_PAIRS)
        hid = wk(256).rearrange("p (v h g c) -> p v h g c", v=2, h=2, g=2)
        hidx, hidg = wk(120), wk(120)
        kcZ = wk(2 * N_CMP).rearrange("p (g c) -> p g c", g=2)
        vcZ = wk(512).rearrange("p (g r d) -> p g r d", g=2, r=4)
        cs = wk(240).rearrange("p (h q c) -> p h q c", h=8, q=2)
        csP = wk(512).rearrange("p (q g r c) -> p q g r c", q=2, g=2, r=4)
        csT = wk(512).rearrange("p (g t) -> p g t", g=2)
        w2k, w2v = wk(128).rearrange("p (c d) -> p c d", c=2), wk(128).rearrange("p (c d) -> p c d", c=2)

        h_k, h_b = xn[:, 0:1024], xn[:, 1024:2048]
        t1, t4 = wk(256, 0), wk(256)
        e1, e2, e3, e4 = wk(256), wk(256), wk(256), wk(256)
        qq, kk, kkL, kd = wk(256), wk(256), wk(256), wk(256)
        qe = [wk(256), wk(256)]
        hS = wk(7 * P).rearrange("p (c v) -> p c v", c=7)
        Am = wk(256).rearrange("p (q t) -> p q t", q=2)
        kdT = wk(256).rearrange("p (q k) -> p q k", q=2)
        iB = wk(1024).rearrange("p (q c v) -> p q c v", q=2, c=4)
        osb = wk(1024).rearrange("p (q h v) -> p q h v", q=2, h=4)
        conv_at = wo[0]
        conv = wk(1536)
        square_junk = vrows[:, :]

        BZ = wk(512, 0).rearrange("p (g t) -> p g t", g=2)
        Lb = wk(1024).rearrange("p (h t) -> p h t", h=8)
        Lm = wk(1024).rearrange("p (h t) -> p h t", h=8)
        xwB = wk(1024).rearrange("p (c h n) -> p c h n", c=2, h=8)
        sS = wk(2048).rearrange("p (c n) -> p c n", c=4)
        assert wo[0] <= conv_at
        CBm = kv_slc[:, 0:512].rearrange("p (q g t) -> p q g t", q=2, g=2)
        Btok = kv_win[:, 0:256].rearrange("p (q n) -> p q n", q=2)
        xtok = hq[:, :].rearrange("p (q h n) -> p q h n", q=2, h=8)
        xdt = hi[:, :].rearrange("p (q h n) -> p q h n", q=2, h=8)
        yd = hg[:, :].rearrange("p (q n) -> p q n", q=2)
        ytmp = hf[:, :].rearrange("p (a h n) -> p a h n", a=2, h=8)
        conv_th = [q_nsa[:, 0:512], q_nsa[:, 512:1024], kc_raw[:, :]]
        z_th = spare
        g_th = q_nsa[:, :]

        gth = [sb("gth0", 512), sb("gth1", 512)]

        ps = ctx.enter_context(nc.psum_tensor("ps", [P, 8, 512], F32))

        ssq, rms, rstd, eps = sm(2), sm(2), sm(2), sm(1)
        negm, esum, rr, es = sm(4), sm(4), sm(4), sm(4)
        sinks, nsinks = sm(8), sm(8)
        gsig = sm(QT * 24)
        lb, olb, lbt, lbr = sm(4), sm(4), sm(4), sm(4)
        vgh = sm(4)
        hdec = [sm(8), sm(8)]
        hssq, hrms, hrstd = sm(8), sm(8), sm(8)
        cmx, csum = sm(16), sm(16)
        alog, dtb, dskip = sm(8), sm(8), sm(8)
        dtr, dta, dtm, dt, dtA = sm(16), sm(16), sm(16), sm(16), sm(16)
        acs, sdec, eacs, swt = sm(32), sm(16), sm(16), sm(16)
        swB = sm(32)
        cdec = sm(16)
        sssq, srms, srstd = sm(2), sm(2), sm(2)
        assert so[0] <= 512, so[0]

        comb = kv_win[:, 0:QT * EXPERTS]
        wr = kv_win[:, 64:64 + KD * 36]
        gffn = yT_a[:, :]
        ys = yT_a[:, :]
        gf = yT_c[:, :]
        sil, act_tok = kv_swa[:, 0:256], kv_swa[:, 256:512]
        actT = [kv_swa[:, 512:576], kv_swa[:, 576:640]]
        strict, ones = kv_slc[:, 0:P], kv_slc[:, P:2 * P]
        gath = work[:, SLOT_E:SLOT_E + 1024].rearrange("p (c s) -> p c s", c=KD)
        onehot = work[:, SLOT_E + 1024:SLOT_E + 1280]
        onehot_w = work[:, SLOT_E + 1280:SLOT_E + 1536]
        scat = work[:, SLOT_E + 1536:SLOT_E + 1792].rearrange("p (q t) -> p q t", q=QT)
        f_sil, f_act = q_swa[:, 512:1024], q_nsa[:, 512:1024]
        rt = kvc_raw[:, :]
        pT_ple = q_nsa[:, 0:512]
        p_tok = q_swa[:, 0:512]

        ld_cmp, ld_vec, ld_cst, ld_bias, ld_small = sem("ld_cmp"), sem("ld_vec"), sem("ld_cst"), sem("ld_bias"), sem("ld_small")
        ld_x = [sem("ld_x0"), sem("ld_x1")]
        ld_moe, ld_p = sem("ld_moe"), sem("ld_p")
        ld_w = [sem(f"ld_w{i}") for i in range(SLOTS)]
        dve_step, act_step, pool_step = sem("dve_step"), sem("act_step"), sem("pool_step")
        ssq_done, rms_done, eps_ready = sem("ssq_done"), sem("rms_done"), sem("eps_ready")
        xn_done, xT_done, hT_done = sem("xn_done"), sem("xT_done"), sem("hT_done")
        vec_t, zeroed = sem("vec_t"), sem("zeroed")
        proj_done, seg_ready = sem("proj_done"), sem("seg_ready")
        scores_done, max_done = sem("scores_done"), sem("max_done")
        exp_done, prob_done = sem("exp_done"), sem("prob_done")
        pT_done, pT_copied, pv_done, y_copied = sem("pT_done"), sem("pT_copied"), sem("pv_done"), sem("y_copied")
        gate_tanh = sem("gate_tanh")
        cmp_in, cmp_hid, cmp_gel, cmp_tanh, cmp_hready = (
            sem("cmp_in"), sem("cmp_hid"), sem("cmp_gel"), sem("cmp_tanh"), sem("cmp_hready"))
        cmp_kv, cmp_kvc, cmp_sc, cmp_sub, cmp_exp, cmp_p, cmp_pT, cmp_pTc = (
            sem("cmp_kv"), sem("cmp_kvc"), sem("cmp_sc"), sem("cmp_sub"), sem("cmp_exp"), sem("cmp_p"),
            sem("cmp_pT"), sem("cmp_pTc"))
        h_arg, h_exp, h_f, h_log, hg_tanh = sem("h_arg"), sem("h_exp"), sem("h_f"), sem("h_log"), sem("hg_tanh")
        h_diff, h_e, h_ops = sem("h_diff"), sem("h_e"), sem("h_ops")
        h_A, h_Am, h_U, h_S, h_O, h_osb, h_iB, h_sq = (
            sem("h_A"), sem("h_Am"), sem("h_U"), sem("h_S"), sem("h_O"), sem("h_osb"), sem("h_iB"), sem("h_sq"))
        h_rms, h_y, h_yT, h_yTc = sem("h_rms"), sem("h_y"), sem("h_yT"), sem("h_yTc")
        dt_arg, dt_log, s_conv, s_tanh, s_silu = sem("dt_arg"), sem("dt_log"), sem("s_conv"), sem("s_tanh"), sem("s_silu")
        s_X, s_Xcopy, s_acs, s_dec, s_B, s_Larg, s_Lexp, s_L = (
            sem("s_X"), sem("s_Xcopy"), sem("s_acs"), sem("s_dec"), sem("s_B"), sem("s_Larg"), sem("s_Lexp"), sem("s_L"))
        s_Y, s_state, s_off, s_y, s_sq, s_rms, s_n, s_yT, s_yTc = (
            sem("s_Y"), sem("s_state"), sem("s_off"), sem("s_y"), sem("s_sq"), sem("s_rms"), sem("s_n"),
            sem("s_yT"), sem("s_yTc"))
        g_done, g_tanh, yp_done, u_done = sem("g_done"), sem("g_tanh"), sem("yp_done"), sem("u_done")
        wo_done, x2_done = sem("wo_done"), sem("x2_done")
        rt_done, rt_sub, rt_exp, rt_d, rt_e = sem("rt_done"), sem("rt_sub"), sem("rt_exp"), sem("rt_d"), sem("rt_e")
        gu_done, silu_done, act_done, down_done, sc_done, acc_done = (
            sem("gu_done"), sem("silu_done"), sem("act_done"), sem("down_done"), sem("sc_done"), sem("acc_done"))
        m_mask, m_pos, m_S, m_Sw, m_G, m_Gc, m_ST, m_STc, m_y = (
            sem("m_mask"), sem("m_pos"), sem("m_S"), sem("m_Sw"), sem("m_G"), sem("m_Gc"), sem("m_ST"), sem("m_STc"),
            sem("m_y"))
        a_T, a_Tc = sem("a_T"), sem("a_Tc")
        ld_e0, ld_d0, ld_wo1, ld_ple = sem("ld_expert0"), sem("ld_down0"), sem("ld_wo1"), sem("ld_ple")
        ld_d = [sem(f"ld_d{i}") for i in range(4)]
        ld_e = [sem(f"ld_e{i}") for i in range(4)]
        over_ready, ld_f, f_gu, f_silu, f_act_done, f_down, f_acc = (
            sem("over_ready"), sem("ld_f"), sem("f_gu"), sem("f_silu"), sem("f_act"), sem("f_down"), sem("f_acc"))
        x3_done = sem("x3_done")
        ple_T, ple_Tc, ple_p, ple_g, ple_tanh, x4_done = (
            sem("ple_T"), sem("ple_Tc"), sem("ple_p"), sem("ple_g"), sem("ple_tanh"), sem("x4_done"))
        out_done, o_dma = sem("out_done"), sem("o_dma")

        def cols(c0, n):
            return [(0, KD * n, w_in[:, :, c0:c0 + n])]

        def pair_cols(c0):
            return [(g * HD, w_in[:, :, c0 + g * 256:c0 + (g + 1) * 256]) for g in range(2)]

        items = []

        def item(name, parts, freed_by, count):
            items.append((name, parts, freed_by, count))

        item("gz", cols(NSA_GATE, 536), proj_done, 3)
        item("swa", [("pairs", 768, v) for v in pair_cols(SWA_Q)] + [("plain", 768, (512, w_in[:, :, SWA_KV:SWA_KV + 256]))], proj_done, 6)
        item("nkv", cols(NSA_KV, 768), proj_done, 10)
        item("nq", [("pairs", 512, v) for v in pair_cols(NSA_Q)], proj_done, 12)
        item("w1k", [(0, 4096, a["nsa_cmp_w1_k"][0].rearrange("(c p) n -> p c n", p=P))], cmp_hid, 1)
        item("w1v", [(0, 4096, a["nsa_cmp_w1_v"][0].rearrange("(c p) n -> p c n", p=P))], cmp_hid, 2)
        item("hq", cols(H_Q, 512), proj_done, 14)
        item("hf", cols(H_F, 512), proj_done, 16)
        item("hi", cols(H_I, 512), proj_done, 18)
        item("hg", cols(H_G, 512), proj_done, 20)
        item("xd", cols(SSM_X, 776), proj_done, 24)
        ORDER = (0, 2, 1, 3)
        for ni, n in enumerate(ORDER):
            if n in (0, 2):
                wb = w_branch[n].rearrange("(g j d) e -> g d j e", g=2, d=HD)
                parts = [(0, 4096, wb[0], 0), (0, 4096, wb[1], HD)]
            else:
                parts = [(0, 4096, w_branch[n].rearrange("(c p) e -> p c e", p=P))]
            item(f"g{n}0", cols(MERGE + n * D, 512), g_done, 4 * ni + 2)
            item(f"b{n}", parts, yp_done, 4 * ni + 4)
            item(f"g{n}1", cols(MERGE + n * D + 512, 512), g_done, 4 * ni + 4)
        item("wo0", [(0, 4096, w_out[:, :, 0:512])], wo_done, 3)

        landed, slot_of = {}, {}
        count = [0] * SLOTS
        for i, (name, parts, *_) in enumerate(items):
            count[i % SLOTS] += 16 * sum(KD if part[0] == "pairs" else 1 for part in parts)
            landed[name], slot_of[name] = count[i % SLOTS], i % SLOTS

        def weights(name, c, n):
            return ring[slot_of[name]][:, 0:c * n].rearrange("p (c n) -> p c n", c=c)

        def arrived(eng, name):
            eng.wait_ge(ld_w[slot_of[name]], landed[name])

        GRP = []
        GRP.append(("gate", "gz", 536, [("tok", 0, 24)]))
        for q in range(2):
            GRP.append((f"z{q}", "gz", 536, [("tokq", 24, 512, q)]))
        for half in range(2):
            GRP.append(("q_swa", "swa", 768, [("headpair", 2 * half + i, 0) for i in range(2)]))
        GRP.append(("kv_swa", "swa", 768, [("feat", 512, 128), ("tok", 640, 128)]))
        GRP.append(("kc", "nkv", 768, [("feat", 0, 128)]))
        GRP.append(("vc", "nkv", 768, [("feat", 128, 128)]))
        GRP.append(("kv_slc", "nkv", 768, [("feat", 256, 128), ("tok", 384, 128)]))
        GRP.append(("kv_win", "nkv", 768, [("feat", 512, 128), ("tok", 640, 128)]))
        for half in range(2):
            GRP.append(("q_nsa", "nq", 512, [("headpair", 2 * half + i, 0) for i in range(2)]))
        for nm in ("hq", "hf"):
            for half in range(2):
                GRP.append((nm, nm, 512, [("feat", (2 * half + i) * P, P) for i in range(2)]))
        for nm in ("hi", "hg"):
            for q in range(2):
                GRP.append((nm, nm, 512, [("tokq", 0, 512, q)]))
        for k in range(3):
            GRP.append(("xbc", "xd", 776, [("feat", (2 * k + i) * P, P) for i in range(2)]))
        GRP.append(("dt", "xd", 776, [("tok", 768, 8)]))
        NG = len(GRP)
        assert NG == 24


        first_free = [ring[(len(items) + k) % SLOTS] for k in range(SLOTS)]
        e_slot = [first_free[2], first_free[1], first_free[0], arena]
        w_ple_gate = [e_slot[k][:, 0:4096].rearrange("p (c n) -> p c n", c=KD) for k in range(2)]
        w_ple = uT[:, :].rearrange("p (c n) -> p c n", c=2)
        w_out1 = arena[:, 0:4096].rearrange("p (c n) -> p c n", c=KD)

        lg = rt[:, 0:72]
        mask = rt[:, 416:480].rearrange("p (q n) -> p q n", q=2)
        nmask = rt[:, 480:544].rearrange("p (q n) -> p q n", q=2)
        posm = rt[:, 544:616].rearrange("p (q n) -> p q n", q=2)
        comb_over = rt[:, 616:680].rearrange("p (q n) -> p q n", q=2)
        cnt, isover, rank, over_f = rt[:, 680:712], rt[:, 712:744], rt[:, 744:776], rt[:, 776:792]
        pick = q_swa[:, 512:512 + MAX_OVER * EXPERTS].rearrange("p (k e) -> p k e", k=MAX_OVER)
        gexp, gm, m1, m2, mn = rt[:, 72:80], rt[:, 80:82], rt[:, 82:84], rt[:, 84:86], rt[:, 86:88]
        gw, e21, w1, w2 = rt[:, 88:90], rt[:, 90:92], rt[:, 92:94], rt[:, 94:96]
        goh = rt[:, 96:104].rearrange("p (q n) -> p q n", q=2)
        gpen = rt[:, 104:112].rearrange("p (q n) -> p q n", q=2)
        iom = rt[:, 128:160]
        cand = rt[:, 160:224].rearrange("p (q n) -> p q n", q=2)
        vmask = rt[:, 224:288].rearrange("p (q n) -> p q n", q=2)
        oh1 = rt[:, 288:352].rearrange("p (q n) -> p q n", q=2)
        oh2 = rt[:, 352:416].rearrange("p (q n) -> p q n", q=2)

        SLOT_LIST = [("swa", kv_swa, q_swa, j, 0) for j in range(4)]
        for j in range(4):
            SLOT_LIST += [("slc", kv_slc, q_nsa, j, 1), ("win", kv_win, q_nsa, j, 2)]
        NS = len(SLOT_LIST)
        SLOT_GROUPS = [[6, 7], [8, 9], [10, 11], []] + [[12 + i] for i in range(8)]

        def tile_of(s):
            if s < 4:
                return s, True, True
            return 4 + (s - 4) // 2, s % 2 == 0, s % 2 == 1

        block = ctx.enter_context(nc.Block())

        @block.sync
        def _(sp):
            def load(i):
                name, parts, _, _ = items[i]
                if i >= SLOTS:
                    sp.wait_ge(items[i - SLOTS][2], items[i - SLOTS][3])
                for part in parts:
                    if part[0] in ("pairs", "plain"):
                        kind, width, (at, src) = part
                        wide = ring[i % SLOTS][:, 0:KD * width].rearrange("p (c n) -> p c n", c=KD)
                        if kind == "pairs":
                            for c in range(KD):
                                dst = wide[:, c, 0:512].rearrange("p (j h d) -> p j h d", j=4, h=2)[:, :, at // HD, :]
                                sp.dma_start(dst, src[:, c, :].rearrange("p (j d) -> p j d", j=4)).then_inc(ld_w[i % SLOTS], 16)
                        else:
                            sp.dma_start(wide[:, :, at:at + src.shape[2]], src).then_inc(ld_w[i % SLOTS], 16)
                        continue
                    at, n, src = part[:3]
                    p0 = part[3] if len(part) > 3 else 0
                    np_, c, w = src.shape
                    dst = ring[i % SLOTS][p0:p0 + np_, at:at + n].rearrange("p (c n) -> p c n", c=c)
                    sp.dma_start(dst, src).then_inc(ld_w[i % SLOTS], 16)

            def rows(at, src, n):
                sp.dma_start(vrows[at:at + n, :], src).then_inc(ld_vec, 16)

            for q in range(QT):
                sp.dma_start(xv[:, q, :], x_dram[:, q, :]).then_inc(ld_x[q], 16)
            sp.dma_start(cst[:, 0:C_BIAS], a["cst"][:, 0:C_BIAS]).then_inc(ld_cst, 16)
            rows(V_GMIX, a["g_mix"][0].rearrange("(c p) -> c p", p=P), 8)
            rows(V_GPLE, a["g_ple"][0].rearrange("(c p) -> c p", p=P), 8)
            rows(V_GH, a["hgrn_norm_g"][0].rearrange("(c p) -> c p", p=P), 4)
            rows(V_GS, a["ssm_norm_g"][0].rearrange("(c p) -> c p", p=P), 4)
            rows(V_CB, a["ssm_conv_b"][0].rearrange("(c p) -> c p", p=P), 6)
            rows(V_CW, a["ssm_conv_w"][0].rearrange("j (c p) -> (j c) p", p=P), 24)
            rows(V_LB, a["hgrn_lower_bounds"][0].rearrange("(c p) -> c p", p=P), 4)
            rows(V_PK, a["nsa_pos_k"][0].rearrange("(l m) d -> l (m d)", m=2), 16)
            rows(V_PV, a["nsa_pos_v"][0].rearrange("(l m) d -> l (m d)", m=2), 16)
            load(0)
            for dst, src in ((sinks, "attn_sinks"), (alog, "ssm_A_log"), (dtb, "ssm_dt_bias"), (dskip, "ssm_D")):
                sp.dma_start(dst, a[src][0].partition_broadcast(P)).then_inc(ld_small, 16)
            load(1)
            sp.dma_start(cst[:, C_BIAS:C_MOE], a["cst"][:, C_BIAS:C_MOE]).then_inc(ld_bias, 16)
            sp.dma_start(w2k, a["nsa_cmp_w2_k"][0].rearrange("(c p) d -> p c d", p=P)).then_inc(ld_cmp, 16)
            sp.dma_start(w2v, a["nsa_cmp_w2_v"][0].rearrange("(c p) d -> p c d", p=P)).then_inc(ld_cmp, 16)
            for i in range(2, len(items) - 1):
                load(i)

            sp.wait_ge(s_yTc, 2)
            wrv = wr.rearrange("p (c n) -> p c n", c=KD)
            sp.dma_start(wrv[:, :, 0:GROUPS], a["w_router_grp"][0].rearrange("(p c) n -> p c n", c=KD)).then_inc(ld_moe, 16)
            sp.dma_start(wrv[:, :, GROUPS:36], a["w_router_exp"][0].rearrange("(p c) n -> p c n", c=KD)).then_inc(ld_moe, 16)
            sp.dma_start(kv_slc[:, 0:2 * P], a["cst"][:, C_MOE:C_ALL]).then_inc(ld_moe, 16)
            sp.dma_start(gf, a["g_final"].partition_broadcast(P)).then_inc(ld_moe, 16)

            w_gate = a["w_exp_gate"][0].rearrange("e (p c) n -> e p (c n)", c=KD)
            w_up = a["w_exp_up"][0].rearrange("e (p c) n -> e p (c n)", c=KD)
            w_down = a["w_exp_down"][0].rearrange("e (p c) n -> e p (c n)", c=2)

            def load_expert(e, slot, arrived, arrived_down, before=None):
                for at, src, used, sem_ in ((0, w_gate, gu_done, arrived), (2048, w_up, gu_done, arrived),
                                            (4096, w_down, down_done, arrived_down)):
                    if before is not None:
                        sp.wait_ge(used, before)
                    sp.dma_start(slot[:, at:at + 2048], src[e]).then_inc(sem_, 16)

            sp.dma_start(w_out1, w_out[:, :, 512:1024]).then_inc(ld_wo1, 16)
            load(len(items) - 1)
            sp.wait_ge(yp_done, 12)
            sp.dma_start(p_tok.rearrange("p (q n) -> p q n", q=2), p_dram).then_inc(ld_p, 16)
            load_expert(0, work, ld_e0, ld_d0)
            sp.wait_ge(yp_done, 16)
            sp.dma_start(gffn, a["g_ffn"][0].partition_broadcast(P)).then_inc(ld_moe, 16)
            sp.wait_ge(g_done, 16)
            load_expert(1, e_slot[1], ld_e[1], ld_d[1])
            load_expert(2, e_slot[2], ld_e[2], ld_d[2])
            sp.wait_ge(wo_done, 4)
            load_expert(3, e_slot[3], ld_e[3], ld_d[3])
            load_expert(4, e_slot[0], ld_e[0], ld_d[0])
            sp.dma_start(w_ple, a["w_ple_proj"][0].rearrange("(c p) n -> p c n", p=P)).then_inc(ld_ple, 16)
            load_expert(5, work, ld_e0, ld_d0, 1)
            for e in range(6, 9):
                load_expert(e, e_slot[e % 4], ld_e[e % 4], ld_d[e % 4], e - 3)
            load_expert(9, e_slot[1], ld_e[1], ld_d[1], 2)
            with sp.Fori(2, QUADS - 1) as it:
                for k in range(2, 6):
                    load_expert(bass.ds(it * 4 + k, 1), e_slot[k % 4], ld_e[k % 4], ld_d[k % 4], it * 4 + (k - 3))
            for e in range(EXPERTS - 2, EXPERTS):
                load_expert(e, e_slot[e % 4], ld_e[e % 4], ld_d[e % 4], e - 3)
            wg = a["w_ple_gate"][0].rearrange("(c p) n -> p c n", p=P)
            for k in range(2):
                sp.wait_ge(down_done, EXPERTS - 3 + k)
                sp.dma_start(w_ple_gate[k], wg[:, :, k * 512:(k + 1) * 512]).then_inc(ld_e[k], 16)

            sp.wait_ge(down_done, EXPERTS)
            sp.wait_ge(over_ready, 1)
            n_over = sp.value_load(over[0:1, 15:16], min_val=0, max_val=MAX_OVER)
            with sp.If(n_over > 0):
                with sp.Fori(0, MAX_OVER) as it:
                    with sp.If(n_over > it):
                        sp.wait_ge(f_acc, it + 1)
                        e = sp.value_load(over[0:1, bass.ds(it, 1)], min_val=0, max_val=EXPERTS - 1)
                        load_expert(bass.ds(e, 1), e_slot[3], ld_f, ld_f)
            for q in range(QT):
                sp.wait_ge(out_done, q + 1)
                sp.dma_start(out_dram[:, q, :], xnv[:, q, :]).then_inc(o_dma, 16)
            sp.wait_ge(o_dma, 32)

        @block.tensor
        def _(pe):
            def mm(out, lhsT, rhs, start, stop):
                return pe.matmul(out, lhsT, rhs, start=start, stop=stop, skip_group_check=True)

            def norm_T(m, q):
                pe.wait_ge(xn_done, 2 * m + q + 1)
                for half in range(2):
                    for i in range(4):
                        c = 4 * half + i
                        src = xnv[:, q, c:D:KD] if m == 1 else xnv[:, q, c * P:(c + 1) * P]
                        last = pe.transpose(ps[:, 2 * q + half, i * P:(i + 1) * P], src, ident)
                    last.then_inc(xT_done, 1)

            pe.wait_ge(ld_vec, 16 * 9)
            pe.wait_ge(ld_cst, 16)
            pe.transpose(ps[:, 6, 0:V_ALL], vrows[0:V_ALL, :], ident[0:V_ALL, 0:V_ALL]).then_inc(vec_t, 1)
            norm_T(0, 0)
            norm_T(0, 1)

            def project(g):
                name, it, width, parts = GRP[g]
                bank = g % 2
                arrived(pe, it)
                if g == 0:
                    pe.wait_ge(hT_done, 4)
                if g >= 2:
                    pe.wait_ge(seg_ready, g - 1)
                w = weights(it, KD, width)
                at = 0
                for part in parts:
                    kind, c0 = part[:2]
                    if kind == "tokq":
                        todo = [(part[2], lambda c: hTv[:, c, part[3] * P:(part[3] + 1) * P],
                                 lambda c: w[:, c, c0:c0 + part[2]])]
                    elif kind == "tok":
                        todo = [(part[2], lambda c, q=q: hTv[:, c, q * P:(q + 1) * P],
                                 lambda c: w[:, c, c0:c0 + part[2]]) for q in range(QT)]
                    elif kind == "headpair":
                        todo = [(T, lambda c: w[:, c, c0 * P:(c0 + 1) * P], lambda c: hTv[:, c, :])]
                    else:
                        todo = [(T, lambda c: w[:, c, c0:c0 + P], lambda c: hTv[:, c, :])]
                    for n, lhsT, rhs in todo:
                        for c in range(KD):
                            last = mm(ps[:, bank, at:at + n], lhsT(c), rhs(c), c == 0, c == KD - 1)
                        at += n
                last.then_inc(proj_done, 1)

            def scores(s):
                _, kv, qs, j, _ = SLOT_LIST[s]
                if s in (0, 4):
                    pe.wait_ge(seg_ready, 6 if s == 0 else 12)
                if s >= 1:
                    pe.wait_ge(max_done, s)
                kZ = kv[:, 0:512].rearrange("p (g t) -> p g t", g=2)
                q0, q1 = qs[:, j * T:j * T + P], qs[:, j * T + P:(j + 1) * T]
                for u in range(2):
                    mm(ps[:, 2 + u, 0:128], q0, kZ[:, u, 0:128], True, True)
                    mm(ps[:, 2 + u, 128:256], q1, kZ[:, u, 128:256], True, True)
                    last = mm(ps[:, 2 + u, 256:384], q1, kZ[:, u, 0:128], True, True)
                last.then_inc(scores_done, 1)

            def weights_T(s):
                pe.wait_ge(prob_done, s + 1)
                if s >= 1:
                    pe.wait_ge(pT_copied, s)
                for u in range(2):
                    for at, src in ((0, 0), (128, 256), (256, 128)):
                        last = pe.transpose(ps[:, 4 + u, at:at + P], sc[:, u, src:src + P], ident)
                last.then_inc(pT_done, 1)

            def pv(s):
                _, kv, _, j, br = SLOT_LIST[s]
                tile, opens, closes = tile_of(s)
                pe.wait_ge(pT_copied, s + 1)
                if opens and tile >= 2:
                    pe.wait_ge(y_copied, tile - 1)
                if s == 3:
                    pe.wait_ge(cmp_gel, 1)
                v = kv[:, 512:768].rearrange("p (q n) -> p q n", q=2)
                bank = 6 + tile % 2
                if closes and s >= 4:
                    if s == 5:
                        pe.wait_ge(cmp_pTc, 1)
                    for u in range(2):
                        mm(ps[HD * u:HD * (u + 1), bank, 0:T], vcZ[:, u, j, :], csT[:, u, :], False, False)
                for u in range(2):
                    out = ps[HD * u:HD * (u + 1), bank, :]
                    mm(out[:, 0:T], v[:, 0, HD * u:HD * (u + 1)], pT[:, u, 0:256], opens, False)
                    last = mm(out[:, P:T], v[:, 1, HD * u:HD * (u + 1)], pT[:, u, 256:384], False, closes)
                last.then_inc(pv_done, 1)

            def compress_hidden():
                pe.wait_ge(cmp_in, 2)
                pe.wait_ge(y_copied, 2)
                for v, (it, src) in enumerate((("w1k", kcP), ("w1v", vcP))):
                    arrived(pe, it)
                    w = weights(it, CMP_PAIRS, 256)
                    for hc in range(2):
                        at = 256 + (v * 2 + hc) * 2 * N_CMP
                        for l in range(CMP_PAIRS):
                            last = mm(ps[:, 7, at:at + 2 * N_CMP], w[:, l, hc * P:(hc + 1) * P],
                                      src[:, :, l, :], l == 0, l == CMP_PAIRS - 1)
                    last.then_inc(cmp_hid, 1)

            def compress_kv():
                pe.wait_ge(cmp_hready, 1)
                pe.wait_ge(ld_cmp, 16 * 2)
                pe.wait_ge(y_copied, 4)
                for g in range(2):
                    for hc in range(2):
                        mm(ps[HD * g:HD * (g + 1), 7, 256:256 + N_CMP], w2k[:, hc, :],
                           hid[:, 0, hc, g, 0:N_CMP], hc == 0, hc == 1)
                for g in range(2):
                    for r in range(4):
                        for hc in range(2):
                            last = mm(ps[32 * r:32 * (r + 1), 7, 384 + HD * g:384 + HD * (g + 1)],
                                      hid[:, 1, hc, g, :], w2v[:, hc, :], hc == 0, hc == 1)
                last.then_inc(cmp_kv, 1)

            def compress_scores():
                pe.wait_ge(cmp_kvc, 1)
                out = ps[:, 7, 256:496].rearrange("p (g j q c) -> p g j q c", g=2, j=4, q=2)
                for j in range(4):
                    for q in range(QT):
                        last = mm(out[:, :, j, q, :], q_nsa[:, j * T + q * P:j * T + (q + 1) * P], kcZ, True, True)
                last.then_inc(cmp_sc, 1)

            def compress_T():
                pe.wait_ge(cmp_p, 1)
                for g in range(2):
                    for q in range(QT):
                        last = pe.transpose(ps[:, 7, g * T + q * P:g * T + (q + 1) * P], csP[:, q, g, :, :], ident)
                last.then_inc(cmp_pT, 1)

            for g in range(6):
                project(g)
            for s in range(NS):
                scores(s)
                if s >= 1:
                    weights_T(s - 1)
                if s == 5:
                    compress_scores()
                if s == 6:
                    compress_T()
                for g in SLOT_GROUPS[s]:
                    project(g)
                if s >= 1:
                    pv(s - 1)
                if s == 3:
                    compress_hidden()
                if s == 4:
                    compress_kv()
            weights_T(NS - 1)
            project(20)
            pv(NS - 1)
            for g in range(21, 24):
                project(g)

            def hgrn_A(h):
                pe.wait_ge(h_ops, h + 1)
                if h >= 1:
                    pe.wait_ge(h_Am, h)
                for q in range(QT):
                    o = ps[:, 4, q * P:(q + 1) * P].rearrange("p (c a) -> p c a", c=4)
                    c = slice(q * P, (q + 1) * P)
                    qc = qq[:, c].rearrange("p (c a) -> p c a", c=4)
                    mm(o[:, :, 16:32], kk[:, c], qc[:, :, 16:32], True, True)
                    mm(o[:, :, 0:16], kkL[:, c], qc[:, :, 0:16], True, True)
                for q in range(QT):
                    last = pe.transpose(ps[:, 4, (2 + q) * P:(3 + q) * P], kd[:, q * P:(q + 1) * P], ident)
                last.then_inc(h_A, 1)

            def hgrn_U(h):
                pe.wait_ge(h_Am, h + 1)
                pe.wait_ge(h_iB, h + 1)
                if h >= 1:
                    pe.wait_ge(h_S, h)
                mm(ps[:, 5, :], kdT[:, 0, :], iB[:, 0, :, :], True, True)
                mm(ps[:, 6, 0:384], kdT[:, 1, :], iB[:, 1, 0:3, :], True, True).then_inc(h_U, 1)

            def hgrn_O(h):
                pe.wait_ge(h_S, h + 1)
                if h >= 1:
                    pe.wait_ge(h_osb, h)
                for q in range(QT):
                    mm(ps[:, 7, q * P:(q + 1) * P], Am[:, q, :], hi[:, q * 512 + h * P:q * 512 + (h + 1) * P], True, False)
                    for c in range(4):
                        cc = 4 * q + c
                        if cc == 0:
                            continue
                        last = mm(ps[32 * c:32 * (c + 1), 7, q * P:(q + 1) * P], qe[h % 2][:, 32 * cc:32 * (cc + 1)],
                                  hS[:, cc - 1, :], False, c == 3)
                last.then_inc(h_O, 1)

            def hgrn_T():
                pe.wait_ge(h_y, 1)
                for k in range(2):
                    for i in range(2):
                        for q in range(QT):
                            last = pe.transpose(ps[:, 4 + k, (2 * i + q) * P:(2 * i + q + 1) * P],
                                                osb[:, q, 2 * k + i, :], ident)
                    last.then_inc(h_yT, 1)

            def ssd_X():
                pe.wait_ge(s_silu, 2)
                pe.wait_ge(h_yTc, 2)
                for q in range(QT):
                    for k in range(4):
                        pe.transpose(ps[:, 4 + q, k * P:(k + 1) * P], conv[:, k * T + q * P:k * T + (q + 1) * P], ident)
                for q in range(QT):
                    pe.transpose(ps[:, 6, q * P:(q + 1) * P], conv[:, 4 * T + q * P:4 * T + (q + 1) * P], ident)
                for q in range(QT):
                    mm(ps[:, 6, 256 + 8 * q:264 + 8 * q], tri64, dtA[:, 8 * q:8 * q + 8], True, True)
                    last = mm(ps[:, 6, 272 + 8 * q:280 + 8 * q], blk64, dtA[:, 8 * q:8 * q + 8], True, True)
                last.then_inc(s_X, 1)

            def ssd_B(q):
                if q == 0:
                    pe.wait_ge(s_Xcopy, 1)
                    pe.wait_ge(s_acs, 1)
                else:
                    pe.wait_ge(s_state, 1)
                    pe.wait_ge(s_y, 1)
                for h in range(HEADS):
                    mm(ps[:, 4 + h // 4, (h % 4) * P:(h % 4 + 1) * P],
                       dtA[:, 8 * q + h:8 * q + h + 1].to_broadcast([P, P]), tri64, True, True)
                for g in range(2):
                    last = mm(ps[:, 6, g * P:(g + 1) * P], BZ[:, g, q * P:(q + 1) * P],
                              conv[:, 5 * T + q * P:5 * T + (q + 1) * P], True, True)
                last.then_inc(s_B, 1)

            def ssd_Y(q):
                pe.wait_ge(s_L, q + 1)
                for h in range(HEADS):
                    mm(ps[:, 7, h * HD:(h + 1) * HD], Lm[:, h, :], xdt[:, q, h, :], True, True)
                for c in range(2 - q):
                    last = mm(ps[:, 4 + c, :], Btok[:, q, :], xwB[:, c, :, :], True, True)
                last.then_inc(s_Y, 1)

            def ssd_off(q):
                pe.wait_ge(s_state, q + 1)
                for c in range(2):
                    t0 = 5 * T + (2 * q + c) * S_CHUNK
                    last = mm(ps[S_CHUNK * c:S_CHUNK * (c + 1), 6, :], conv[:, t0:t0 + S_CHUNK], sS[:, 2 * q + c, :],
                              True, True)
                last.then_inc(s_off, 1)

            def ssd_T():
                pe.wait_ge(s_n, 1)
                for k in range(2):
                    for i in range(2):
                        c = (2 * k + i) * P
                        for q in range(QT):
                            last = pe.transpose(ps[:, 4 + k, (2 * i + q) * P:(2 * i + q + 1) * P], yd[:, q, c:c + P], ident)
                    last.then_inc(s_yT, 1)

            def merge_gate(i):
                n, k = ORDER[i // 4], i % 4
                it = f"g{n}{k // 2}"
                arrived(pe, it)
                if i == 0:
                    pe.wait_ge(seg_ready, NG)
                if i >= 2:
                    pe.wait_ge(g_tanh, i - 1)
                w = weights(it, KD, 512)
                for e in range(2):
                    c0 = ((2 * k + e) % 4) * P
                    for c in range(KD):
                        last = mm(ps[:, i % 2, e * T:(e + 1) * T], w[:, c, c0:c0 + P], hTv[:, c, :], c == 0, c == KD - 1)
                last.then_inc(g_done, 1)

            def merge_branch(i):
                n, k = ORDER[i // 4], i % 4
                arrived(pe, f"b{n}")
                if i == 0:
                    pe.wait_ge(y_copied, 8)
                if i >= 2:
                    pe.wait_ge(u_done, i - 1)
                if i == 8:
                    pe.wait_ge(h_yTc, 2)
                if i == 12:
                    pe.wait_ge(s_yTc, 2)
                w = weights(f"b{n}", 4, D)
                yT = (yT_a, yT_b, yT_c, yT_d)[n][:, :].rearrange("p (c t) -> p c t", c=4)
                for e in range(2):
                    c0 = (2 * k + e) * P
                    for c in range(4):
                        last = mm(ps[:, 2 + i % 2, e * T:(e + 1) * T], w[:, c, c0:c0 + P], yT[:, c, :], c == 0, c == 3)
                last.then_inc(yp_done, 1)

            for i in range(16):
                if 1 <= i <= 4:
                    hgrn_O(i - 1)
                if 1 <= i < 4:
                    hgrn_A(i)
                if i == 9:
                    ssd_off(1)
                if i == 11:
                    ssd_T()
                if i < 4 or i % 4 != 1:
                    merge_gate(i)
                if i == 8:
                    ssd_B(1)
                if i >= 4 and i % 4 == 0:
                    merge_gate(i + 1)
                if i == 0:
                    hgrn_A(0)
                if i < 4:
                    hgrn_U(i)
                if i == 6:
                    ssd_X()
                if i == 7:
                    ssd_Y(0)
                if i == 8:
                    ssd_Y(1)
                merge_branch(i)
                if i == 5:
                    hgrn_T()
                if i == 6:
                    ssd_B(0)
                if i == 7:
                    ssd_off(0)

            for q in range(QT):
                for dh in range(2):
                    if q == 1 and dh == 1:
                        pe.wait_ge(ld_p, 16)
                        for k in range(2):
                            for r in range(QT):
                                last = pe.transpose(ps[:, 2, (2 * k + r) * P:(2 * k + r + 1) * P],
                                                    p_tok[:, r * PLE + k * P:r * PLE + (k + 1) * P], ident)
                        last.then_inc(ple_T, 1)
                        norm_T(1, 0)
                    if dh:
                        pe.wait_ge(ld_wo1, 16)
                    else:
                        arrived(pe, "wo0")
                    if q == 0 and dh == 0:
                        pe.wait_ge(u_done, 16)
                    w = w_out1 if dh else weights("wo0", KD, 512)
                    for c in range(KD):
                        last = mm(ps[:, 4 + 2 * q + dh, :], uT[:, c * T + q * P:c * T + (q + 1) * P], w[:, c, :],
                                  c == 0, c == KD - 1)
                    last.then_inc(wo_done, 1)

            pe.wait_ge(ld_moe, 16 * 5)
            wrv = wr.rearrange("p (c n) -> p c n", c=KD)
            for q in range(QT):
                if q == 1:
                    pe.wait_ge(ple_Tc, 1)
                    norm_T(1, 1)
                pe.wait_ge(hT_done, 4 + 2 * q + 2)
                for c in range(KD):
                    last = mm(ps[:, 4, 64 * q:64 * q + 36], hTv[:, c, q * P:(q + 1) * P], wrv[:, c, :], c == 0, c == KD - 1)
            last.then_inc(rt_done, 1)

            pe.wait_ge(m_mask, 1)
            mm(ps[:, 4, 0:32], strict, mask[:, 0, :], True, True)
            mm(ps[:, 4, 32:64], strict, mask[:, 1, :], True, False)
            mm(ps[:, 4, 32:64], ones, mask[:, 0, :], False, True)
            mm(ps[:, 4, 64:96], ones, mask[:, 0, :], True, False)
            mm(ps[:, 4, 64:96], ones, mask[:, 1, :], False, True).then_inc(m_pos, 1)

            def gather(k, first=False):
                pe.wait_ge(m_S, k + 1)
                if not first:
                    pe.wait_ge(m_Gc, k)
                for c in range(KD):
                    for q in range(QT):
                        last = mm(ps[:, 4 + c // 4, (c % 4) * P:(c % 4 + 1) * P], xnv[:, q, c:D:KD],
                                  onehot[:, q * P:(q + 1) * P], q == 0, q == 1)
                last.then_inc(m_G, 1)

            def scatter_matrix(k, first=False):
                pe.wait_ge(m_Sw, k + 1)
                if not first:
                    pe.wait_ge(acc_done, k * 2)
                for q in range(QT):
                    last = pe.transpose(ps[:, 6, q * P:(q + 1) * P], onehot_w[:, q * P:(q + 1) * P], ident)
                last.then_inc(m_ST, 1)

            def act_T(it, i):
                r = slice(CAP * i, CAP * (i + 1))
                for j in range(2):
                    last = pe.transpose(ps[:, i % 2, j * CAP:(j + 1) * CAP], act_tok[r, j:FF:2], ident[r, r])
                last.then_inc(a_T, 1)

            def source(it, i):
                if isinstance(it, int) and (it, i) in ((0, 0), (1, 1)):
                    return work, (ld_e0, 32 * it + 32), (ld_d0, 16 * it + 16)
                n = it + 1 if i >= 2 or (isinstance(it, int) and it == 0) else it
                return e_slot[i], (ld_e[i], n * 32), (ld_d[i], n * 16)

            def gate_up(it, i, before=None):
                if i == 0:
                    pe.wait_ge(m_Gc, it + 1)
                slot, gates_in, _ = source(it, i)
                pe.wait_ge(*gates_in)
                w = slot[:, 0:4096].rearrange("p (b c n) -> p b c n", b=2, c=KD)
                for c in range(KD):
                    if c == KD // 2 and before is not None:
                        pe.wait_ge(act_done, before[0] * 4 + (before[1] + 1))
                    last = mm(ps[CAP * i:CAP * (i + 1), i % 2, :], gath[:, c, CAP * i:CAP * (i + 1)], w[:, :, c, :],
                              c == 0, c == KD - 1)
                    if c == KD // 2 and before is not None:
                        act_T(*before)
                last.then_inc(gu_done, 1)

            def down(it, i):
                pe.wait_ge(a_Tc, it * 4 + (i + 1))
                slot, _, down_in = source(it, i)
                pe.wait_ge(*down_in)
                wv = slot[:, 4096:6144].rearrange("p (j n) -> p j n", j=2)
                for dh in range(2):
                    for j in range(2):
                        last = mm(ps[CAP * i:CAP * (i + 1), 2 + dh, :], actT[i % 2][:, j * CAP:(j + 1) * CAP],
                                  wv[:, j, dh * 512:(dh + 1) * 512], j == 0, j == 1)
                last.then_inc(down_done, 1)

            def ple_proj(q):
                for dh in range(2):
                    for c in range(2):
                        last = mm(ps[:, 4 + 2 * q + dh, :], pT_ple[:, c * T + q * P:c * T + (q + 1) * P],
                                  w_ple[:, c, dh * 512:(dh + 1) * 512], c == 0, c == 1)
                last.then_inc(ple_p, 1)

            def scatter(k, q, own_banks=True):
                if q == 0:
                    pe.wait_ge(m_y, k + 1)
                    pe.wait_ge(m_STc, k + 1)
                elif own_banks:
                    pe.wait_ge(acc_done, k * 2 + 1)
                bank = 6 if own_banks else 0
                for dh in range(2):
                    last = mm(ps[:, bank + dh, :], scat[:, q, :], ys[:, dh * 512:(dh + 1) * 512], True, True)
                last.then_inc(sc_done, 1)

            gather(0, first=True)
            gate_up(0, 0)
            gate_up(0, 1, (0, 0))
            down(0, 0)
            gate_up(0, 2, (0, 1))
            down(0, 1)
            gate_up(0, 3, (0, 2))
            gather(1)
            scatter_matrix(0, first=True)
            down(0, 2)

            def group(it, last_group=False):
                gate_up(it, 0, (it - 1, 3))
                down(it - 1, 3)
                gate_up(it, 1, (it, 0))
                scatter(it - 1, 0)
                down(it, 0)
                gate_up(it, 2, (it, 1))
                scatter(it - 1, 1)
                down(it, 1)
                if last_group:
                    pe.wait_ge(ple_Tc, 1)
                    pe.wait_ge(ld_ple, 16)
                    pe.wait_ge(m_Gc, QUADS)
                    ple_proj(0)
                gate_up(it, 3, (it, 2))
                if not last_group:
                    gather(it + 1)
                scatter_matrix(it)
                down(it, 2)

            group(1)
            with pe.Fori(2, QUADS - 1) as it:
                group(it)
            group(QUADS - 1, last_group=True)
            pe.wait_ge(act_done, EXPERTS)
            act_T(QUADS - 1, 3)
            down(QUADS - 1, 3)
            scatter(QUADS - 1, 0)
            scatter(QUADS - 1, 1, own_banks=False)

            pe.wait_ge(over_ready, 1)
            n_over = pe.value_load(over[0:1, 15:16], min_val=0, max_val=MAX_OVER)
            with pe.If(n_over > 0):
                with pe.Fori(0, MAX_OVER) as it:
                    with pe.If(n_over > it):
                        pe.wait_ge(ld_f, it * 48 + 48)
                        for b in range(2):
                            wv = e_slot[3][:, b * 2048:(b + 1) * 2048].rearrange("p (c n) -> p c n", c=KD)
                            for j in range(2):
                                for c in range(KD):
                                    last = mm(ps[:, 2 + b, j * T:(j + 1) * T], wv[:, c, j:FF:2], hTv[:, c, :],
                                              c == 0, c == KD - 1)
                        last.then_inc(f_gu, 1)
                        pe.wait_ge(f_act_done, it + 1)
                        wv = e_slot[3][:, 4096:6144].rearrange("p (j n) -> p j n", j=2)
                        av = f_act.rearrange("p (j t) -> p j t", j=2)
                        for q in range(QT):
                            for dh in range(2):
                                for j in range(2):
                                    last = mm(ps[:, 6 * q + dh, :], av[:, j, q * P:(q + 1) * P],
                                              wv[:, j, dh * 512:(dh + 1) * 512], j == 0, j == 1)
                        last.then_inc(f_down, 1)

            pe.wait_ge(x3_done, 1)
            ple_proj(1)
            for q in range(QT):
                norm_T(2, q)
            for q in range(QT):
                pe.wait_ge(hT_done, 8 + 2 * q + 2)
                for dh in range(2):
                    pe.wait_ge(ld_e[dh], 32 * (QUADS - 1) + 16)
                    w = w_ple_gate[dh]
                    for c in range(KD):
                        last = mm(ps[:, 2 * q + dh, :], hTv[:, c, q * P:(q + 1) * P], w[:, c, :], c == 0, c == KD - 1)
                    last.then_inc(ple_g, 1)

        @block.scalar
        def _(act):
            cp, A = act.copy, act.activation

            def square(m, q):
                if m == 0:
                    act.wait_ge(ld_x[q], 16)
                elif m == 1:
                    act.wait_ge(x2_done, 2 * (q + 1))
                elif m == 2:
                    act.wait_ge(x3_done, 1)
                else:
                    act.wait_ge(x4_done, 2 * (q + 1))
                A(xnv[:, q, :], xv[:, q, :], ACT.Square, scale=D ** -0.5, accum_out=ssq[:, q:q + 1]).then_inc(ssq_done, 1)
                act.wait_ge(ssq_done, 2 * m + q + 1)
                if m + q == 0:
                    act.wait_ge(eps_ready, 1)
                A(rms[:, q:q + 1], ssq[:, q:q + 1], ACT.Sqrt, bias=eps).then_inc(rms_done, 1)

            for q in range(QT):
                square(0, q)

            def evac(g):
                name = GRP[g][0]
                b = ps[:, g % 2, :]
                act.wait_ge(proj_done, g + 1)
                if name in ("kv_swa", "kv_slc", "kv_win"):
                    t = {"kv_swa": kv_swa, "kv_slc": kv_slc, "kv_win": kv_win}[name]
                    act.wait_ge(zeroed, 1)
                    cp(t[0:64, 0:256], b[0:64, 0:256])
                    cp(t[64:128, 256:512], b[64:128, 0:256])
                    cp(t[:, 512:768], b[:, 256:512]).then_inc(seg_ready, 1)
                    return
                if name in ("kc", "vc"):
                    t = kc_raw if name == "kc" else vc_raw
                    for g2 in range(2):
                        for m in range(2):
                            last = cp(t[HD * m:HD * (m + 1), g2 * T:(g2 + 1) * T], b[HD * g2:HD * (g2 + 1), 0:T])
                    last.then_inc(seg_ready, 1)
                    return
                dst = {0: gate_raw[:, :], 1: z_seg[:, 0:512], 2: z_seg[:, 512:1024],
                       3: q_swa[:, 0:512], 4: q_swa[:, 512:1024], 10: q_nsa[:, 0:512],
                       11: q_nsa[:, 512:1024], 12: hq[:, 0:512], 13: hq[:, 512:1024], 14: hf[:, 0:512],
                       15: hf[:, 512:1024], 16: hi[:, 0:512], 17: hi[:, 512:1024], 18: hg[:, 0:512],
                       19: hg[:, 512:1024], 20: xbc[:, 0:512], 21: xbc[:, 512:1024], 22: xbc[:, 1024:1536],
                       23: dt_raw[:, :]}[g]
                scale = HD ** -0.5 if name in ("q_swa", "q_nsa") else 1.0
                act.mul(dst, b[:, 0:dst.shape[1]], scale).then_inc(seg_ready, 1)

            def exps(s):
                act.wait_ge(max_done, s + 1)
                for u in range(2):
                    for q, (lo, up) in enumerate(((0, 128), (128, 384))):
                        last = A(sc[:, u, lo:up], sc[:, u, lo:up], ACT.Exp, bias=negm[:, 2 * q + u:2 * q + u + 1],
                                 accum_out=esum[:, 2 * q + u:2 * q + u + 1])
                if s < 4:
                    last = A(es, es, ACT.Exp)
                last.then_inc(exp_done, 1)

            def y_tile(s):
                tile, _, closes = tile_of(s)
                if closes:
                    act.wait_ge(pv_done, s + 1)
                    dst = (yT_a if tile < 4 else yT_c)[:, (tile % 4) * T:(tile % 4 + 1) * T]
                    cp(dst, ps[:, 6 + tile % 2, 0:T]).then_inc(y_copied, 1)

            for g in range(6):
                evac(g)
            act.wait_ge(seg_ready, 1)
            A(gsig, gate_raw[:, :], ACT.Tanh, scale=0.5).then_inc(gate_tanh, 1)
            for s in range(NS):
                exps(s)
                if s == 5:
                    act.wait_ge(cmp_sub, 1)
                    A(cs, cs, ACT.Exp).then_inc(cmp_exp, 1)
                for g in SLOT_GROUPS[s]:
                    evac(g)
                if s >= 1:
                    y_tile(s - 1)
                if s == 3:
                    act.wait_ge(cmp_gel, 1)
                    A(hidg, hidg, ACT.Tanh, scale=GELU_A).then_inc(cmp_tanh, 1)
                if s == 4:
                    act.wait_ge(cmp_kv, 1)
                    act.wait_ge(zeroed, 1)
                    for g in range(2):
                        act.mul(kcZ[HD * g:HD * (g + 1), g, :], ps[HD * g:HD * (g + 1), 7, 256:256 + N_CMP], 0.5)
                    for r in range(4):
                        last = act.mul(vcZ[32 * r:32 * (r + 1), :, r, :],
                                       ps[32 * r:32 * (r + 1), 7, 384:512].rearrange("p (g d) -> p g d", g=2), 0.5)
                    last.then_inc(cmp_kvc, 1)
            evac(20)
            y_tile(NS - 1)

            act.wait_ge(h_arg, 1)
            A(lbt, lbt, ACT.Exp)
            A(h_k, hf[:, :], ACT.Exp).then_inc(h_exp, 1)
            act.wait_ge(scores_done, NS)
            A(g_th, hg[:, :], ACT.Tanh, scale=0.5).then_inc(hg_tanh, 1)
            act.wait_ge(h_f, 1)
            A(hf[:, :], hf[:, :], ACT.Ln).then_inc(h_log, 1)
            for g in range(21, 24):
                evac(g)

            def hgrn_exps(h):
                act.wait_ge(h_diff, h + 1)
                b = h_b[:, h * T:(h + 1) * T]
                A(e1, t1, ACT.Exp).then_inc(h_e, 1)
                A(e2, t1, ACT.Exp, scale=-1.0).then_inc(h_e, 1)
                A(e3, b, ACT.Exp).then_inc(h_e, 1)
                A(hdec[h % 2], b[:, H_CHUNK - 1:T:H_CHUNK], ACT.Exp)
                A(e4, t4, ACT.Exp).then_inc(h_e, 1)

            def merge_tanh(i):
                act.wait_ge(g_done, i + 1)
                if i >= 2:
                    act.wait_ge(u_done, i - 1)
                A(gth[i % 2][:, :], ps[:, i % 2, :], ACT.Tanh, scale=0.5).then_inc(g_tanh, 1)

            def hgrn_square(h):
                act.wait_ge(h_osb, h + 1)
                for q in range(QT):
                    if h or q:
                        act.wait_ge(h_sq, 2 * h + q)
                    A(square_junk, osb[:, q, h, :], ACT.Square,
                      accum_out=hssq[:, 4 * q + h:4 * q + h + 1]).then_inc(h_sq, 1)

            def ssd_exp(q):
                act.wait_ge(s_Larg, q + 1)
                for g in range(2):
                    for c in range(2):
                        t = S_CHUNK * (c + 1) - 1
                        src = ps[HD * g:HD * (g + 1), 4 + g, t:512:P]
                        A(cdec[HD * g:HD * (g + 1), 4 * (2 * q + c):4 * (2 * q + c) + 4], src, ACT.Exp)
                A(Lb, Lb, ACT.Exp).then_inc(s_Lexp, 1)

            hgrn_exps(0)
            for i in range(16):
                if 1 <= i <= 4:
                    hgrn_square(i - 1)
                if i == 4:
                    act.wait_ge(h_sq, 8)
                    A(hrms, hssq, ACT.Sqrt, scale=1.0 / P, bias=eps).then_inc(h_rms, 1)
                    for k in range(3):
                        act.wait_ge(s_conv, k + 1)
                        A(conv_th[k], conv[:, k * 512:(k + 1) * 512], ACT.Tanh, scale=0.5).then_inc(s_tanh, 1)
                if i == 5:
                    A(z_th, z_seg[:, :], ACT.Tanh, scale=0.5).then_inc(s_tanh, 1)
                    act.wait_ge(dt_arg, 1)
                    A(dta, dtr, ACT.Abs).then_inc(act_step, 1)
                    act.wait_ge(act_step, 1)
                    A(dta, dta, ACT.Exp, scale=-1.0).then_inc(act_step, 1)
                    A(alog, alog, ACT.Exp)
                    act.wait_ge(act_step, 2)
                    A(dta, dta, ACT.Ln, bias=1.0).then_inc(dt_log, 1)
                if i == 6:
                    merge_tanh(6)
                    act.wait_ge(s_X, 1)
                    cp(hq[:, 0:512], ps[:, 4, :])
                    cp(hq[:, 512:1024], ps[:, 5, :])
                    act.wait_ge(s_acs, 1)
                    cp(kv_win[:, 0:256], ps[:, 6, 0:256])
                    act.wait_ge(zeroed, 3)
                    for g in range(2):
                        last = cp(BZ[HD * g:HD * (g + 1), g, :], conv[HD * g:HD * (g + 1), 4 * T:5 * T])
                    last.then_inc(s_Xcopy, 1)
                    A(eacs, acs[:, 0:16], ACT.Exp)
                    A(sdec, sdec, ACT.Exp).then_inc(s_dec, 1)
                if i != 6:
                    merge_tanh(i)
                if i < 3:
                    hgrn_exps(i + 1)
                if i == 6:
                    ssd_exp(0)
                if i == 8:
                    ssd_exp(1)
                if i == 9:
                    act.wait_ge(s_y, 2)
                    for q in range(QT):
                        if q:
                            act.wait_ge(s_sq, 1)
                        A(ytmp[:, 1, :, :], yd[:, q, :].rearrange("p (h n) -> p h n", h=8), ACT.Square,
                          accum_out=sssq[:, q:q + 1]).then_inc(s_sq, 1)
                    act.wait_ge(s_sq, 2)
                    A(srms, sssq, ACT.Sqrt, scale=1.0 / 512, bias=eps).then_inc(s_rms, 1)

            square(1, 0)
            act.wait_ge(ple_T, 1)
            cp(pT_ple, ps[:, 2, :]).then_inc(ple_Tc, 1)
            square(1, 1)
            act.wait_ge(rt_sub, 1)
            A(gexp, gexp, ACT.Exp).then_inc(rt_exp, 1)
            act.wait_ge(rt_d, 1)
            A(e21, e21, ACT.Exp).then_inc(rt_e, 1)

            def tokens(k):
                act.wait_ge(m_G, k + 1)
                for half in range(2):
                    last = cp(gath[:, 4 * half:4 * half + 4, :], ps[:, 4 + half, :].rearrange("p (c s) -> p c s", c=4))
                last.then_inc(m_Gc, 1)

            def outputs(k):
                act.wait_ge(down_done, k * 4 + 4)
                for dh in range(2):
                    last = cp(ys[:, dh * 512:(dh + 1) * 512], ps[:, 2 + dh, :])
                last.then_inc(m_y, 1)

            def silu(it, i):
                act.wait_ge(gu_done, it * 4 + (i + 1))
                r = slice(CAP * i, CAP * (i + 1))
                A(sil[r, :], ps[r, i % 2, 0:FF], ACT.Silu).then_inc(silu_done, 1)

            def act_T_copy(it, i):
                act.wait_ge(a_T, it * 4 + (i + 1))
                cp(actT[i % 2], ps[:, i % 2, 0:2 * CAP]).then_inc(a_Tc, 1)

            tokens(0)
            silu(0, 0)
            for i in range(1, 4):
                act_T_copy(0, i - 1)
                silu(0, i)
            tokens(1)

            def group(it, last_group=False):
                act_T_copy(it - 1, 3)
                silu(it, 0)
                outputs(it - 1)
                for i in range(1, 4):
                    act_T_copy(it, i - 1)
                    silu(it, i)
                if not last_group:
                    tokens(it + 1)

            with act.Fori(1, QUADS - 1) as it:
                group(it)
            group(QUADS - 1, last_group=True)
            act_T_copy(QUADS - 1, 3)
            outputs(QUADS - 1)

            act.wait_ge(over_ready, 1)
            n_over = act.value_load(over[0:1, 15:16], min_val=0, max_val=MAX_OVER)
            with act.If(n_over > 0):
                with act.Fori(0, MAX_OVER) as it:
                    with act.If(n_over > it):
                        act.wait_ge(f_gu, it + 1)
                        A(f_sil, ps[:, 2, :], ACT.Silu).then_inc(f_silu, 1)

            for q in range(QT):
                square(2, q)
            for i in range(4):
                q, dh = i // 2, i % 2
                act.wait_ge(ple_g, i + 1)
                if i >= 2:
                    act.wait_ge(x4_done, i - 1)
                A(gth[i % 2][:, :], ps[:, i, :], ACT.Tanh, scale=0.5).then_inc(ple_tanh, 1)
                if i == 2:
                    square(3, 0)
            square(3, 1)

        @block.vector
        def _(dve):
            step = Count(dve_step)

            def dep(ins):
                step.on(ins)
                dve.wait_ge(dve_step, step.n)

            tt, ts, stt, cp = dve.tensor_tensor, dve.tensor_scalar, dve.scalar_tensor_tensor, dve.tensor_copy

            def norm(m, q):
                dve.wait_ge(rms_done, 2 * m + q + 1)
                dep(dve.reciprocal(rstd[:, q:q + 1], rms[:, q:q + 1]))
                if m == 1:
                    stt(xnv[:, q, :], xv[:, q, :], rstd[:, q:q + 1], gffn, ALU.mult, ALU.mult).then_inc(xn_done, 1)
                elif m == 3:
                    stt(xnv[:, q, :], xv[:, q, :], rstd[:, q:q + 1], gf, ALU.mult, ALU.mult).then_inc(out_done, 1)
                else:
                    ts(xnv[:, q, :], xv[:, q, :], rstd[:, q:q + 1], None, ALU.mult).then_inc(xn_done, 1)

            def to_hT(m, q, gain):
                for half in range(2):
                    dve.wait_ge(xT_done, 4 * m + 2 * q + half + 1)
                    c = slice(4 * half, 4 * half + 4)
                    out, src = hTv[:, c, q * P:(q + 1) * P], ps[:, 2 * q + half, :].rearrange("p (c t) -> p c t", c=4)
                    if gain is None:
                        cp(out, src).then_inc(hT_done, 1)
                    else:
                        tt(out, src, gain[:, c, None].to_broadcast([P, 4, P]), ALU.mult).then_inc(hT_done, 1)

            for q in range(QT):
                norm(0, q)
            dve.wait_ge(vec_t, 1)
            dep(cp(vec[:, :], ps[:, 6, 0:V_ALL]))
            for q in range(QT):
                to_hT(0, q, vec[:, V_GMIX:V_GMIX + 8])
            dve.wait_ge(ld_small, 16 * 4)
            dep(ts(nsinks, sinks, -1.0, None, ALU.mult))
            ts(vgh, vec[:, V_GH:V_GH + 4], 0.5, None, ALU.mult)

            def slot_max(s):
                _, _, _, j, br = SLOT_LIST[s]
                dve.wait_ge(scores_done, s + 1)
                if s == 0:
                    dve.wait_ge(ld_bias, 16)
                tt(sc[:, :, 0:256].rearrange("p u (b k) -> p u b k", b=2),
                   ps[:, 2:4, 0:256].rearrange("p u (b k) -> p u b k", b=2),
                   bias[:, :, j, 0:1, :].to_broadcast([P, 2, 2, P]), ALU.add)
                dep(tt(sc[:, :, 256:384], ps[:, 2:4, 256:384], bias[:, :, j, 1 if br == 0 else 2, :], ALU.add))
                dve.tensor_reduce(negm[:, 0:2], sc[:, :, 0:128], X, ALU.max, negate=True)
                last = dve.tensor_reduce(negm[:, 2:4], sc[:, :, 128:384], X, ALU.max, negate=True)
                if br == 0:
                    dep(last)
                    nv = negm.rearrange("p (q u) -> p q u", q=2)
                    ev = es.rearrange("p (q u) -> p q u", q=2)
                    dep(tt(nv, nv, nsinks[:, None, j:8:4].to_broadcast([P, 2, 2]), ALU.min))
                    last = tt(ev, nv, sinks[:, None, j:8:4].to_broadcast([P, 2, 2]), ALU.add)
                last.then_inc(max_done, 1)

            def slot_norm(s):
                _, _, _, j, br = SLOT_LIST[s]
                dve.wait_ge(exp_done, s + 1)
                if br == 0:
                    dep(tt(esum, esum, es, ALU.add))
                dep(dve.reciprocal(rr, esum))
                if br:
                    rv = rr.rearrange("p (q u) -> p q u", q=2)
                    dep(tt(rv, rv, gsig.rearrange("p (q h b) -> p q h b", q=2, b=3)[:, :, j:8:4, br], ALU.mult))
                for u in range(2):
                    for q, (lo, up) in enumerate(((0, 128), (128, 384))):
                        last = ts(sc[:, u, lo:up], sc[:, u, lo:up], rr[:, 2 * q + u:2 * q + u + 1], None, ALU.mult)
                last.then_inc(prob_done, 1)

            def slot_copy(s):
                dve.wait_ge(pT_done, s + 1)
                cp(pT[:, :, :], ps[:, 4:6, 0:384]).then_inc(pT_copied, 1)

            def compress_inputs():
                dve.wait_ge(seg_ready, 8)
                for raw, dst, at in ((kc_raw, kcP, V_PK), (vc_raw, vcP, V_PV)):
                    for g in range(2):
                        for m in range(2):
                            rows = slice(HD * m, HD * (m + 1))
                            v = raw[rows, g * T + m:g * T + m + 1]
                            windows = bass.AP(v.tensor, v.offset,
                                              [v.ap[0], [2, CMP_PAIRS], [CMP_STRIDE, N_CMP]])
                            last = tt(dst[rows, g, :, :], windows,
                                      vec[rows, at:at + CMP_PAIRS, None].to_broadcast([HD, CMP_PAIRS, N_CMP]), ALU.add)
                    last.then_inc(cmp_in, 1)

            def compress_gelu():
                dve.wait_ge(cmp_hid, 2)
                dep(cp(hidx, ps[:, 7, 256:256 + 120]))
                dep(tt(hidg, hidx, hidx, ALU.mult))
                dep(ts(hidg, hidg, GELU_B, 1.0, ALU.mult, ALU.add))
                tt(hidg, hidg, hidx, ALU.mult).then_inc(cmp_gel, 1)
                dve.wait_ge(cmp_tanh, 1)
                dve.wait_ge(zeroed, 1)
                out = hid.rearrange("p v h g c -> p (v h g) c")[:, :, 0:N_CMP]
                stt(out, hidg.rearrange("p (a c) -> p a c", c=N_CMP), 1.0, hidx.rearrange("p (a c) -> p a c", c=N_CMP),
                    ALU.add, ALU.mult).then_inc(cmp_hready, 1)

            def compress_max():
                dve.wait_ge(cmp_sc, 1)
                dep(tt(cs, ps[:, 7, 256:496].rearrange("p (h q c) -> p h q c", h=8, q=2), cbias, ALU.add))
                cv = cs.rearrange("p h q c -> p (h q) c")
                dep(dve.tensor_reduce(cmx, cv, X, ALU.max, negate=True))
                tt(cv, cv, cmx[:, :, None].to_broadcast([P, 16, N_CMP]), ALU.add).then_inc(cmp_sub, 1)

            def compress_norm():
                dve.wait_ge(cmp_exp, 1)
                dve.wait_ge(zeroed, 1)
                cv = cs.rearrange("p h q c -> p (h q) c")
                dep(dve.tensor_reduce(csum, cv, X, ALU.add))
                dep(dve.reciprocal(csum, csum))
                sv = csum.rearrange("p (h q) -> p h q", q=2)
                dep(tt(sv, sv, gsig.rearrange("p (q h b) -> p h q b", q=2, b=3)[:, :, :, 0], ALU.mult))
                dep(tt(cv, cv, csum[:, :, None].to_broadcast([P, 16, N_CMP]), ALU.mult))
                out = csP.rearrange("p q g r c -> p (g r) q c")[:, :, :, 0:N_CMP]
                tt(out, cs, cvalid[:, None, :, :].to_broadcast([P, 8, 2, N_CMP]), ALU.mult).then_inc(cmp_p, 1)

            def compress_copy():
                dve.wait_ge(cmp_pT, 1)
                cp(csT, ps[:, 7, :].rearrange("p (g t) -> p g t", g=2)).then_inc(cmp_pTc, 1)

            for s in range(NS):
                slot_max(s)
                if s == 1:
                    dve.wait_ge(gate_tanh, 1)
                    dep(ts(gsig, gsig, 1.0, 0.5, ALU.add, ALU.mult))
                if s == 5:
                    compress_max()
                if s == 6:
                    compress_copy()
                slot_norm(s)
                if s == 1:
                    compress_inputs()
                if s == 5:
                    compress_norm()
                slot_copy(s)
                if s == 3:
                    compress_gelu()

            dve.wait_ge(seg_ready, 20)
            tt(lbt, vec[:, V_LB:V_LB + 4], vec[:, V_LB:V_LB + 4], ALU.subtract)
            ts(hf[:, :], hf[:, :], -1.0, 80.0, ALU.mult, ALU.min).then_inc(h_arg, 1)
            dve.wait_ge(h_exp, 1)
            dep(dve.reciprocal(lbr, lbt))
            dep(tt(lbt, lbt, lbr, ALU.mult))
            dep(tt(lb, lbt, lbt, ALU.subtract))
            dep(ts(olb, lb, -1.0, 1.0, ALU.mult, ALU.add))
            dep(ts(h_b, h_k, 1.0, None, ALU.add))
            dep(dve.reciprocal(h_b, h_b))
            for h in range(H_HEADS):
                c = slice(h * T, (h + 1) * T)
                last = ts(hf[:, c], h_b[:, c], olb[:, h:h + 1], lb[:, h:h + 1], ALU.mult, ALU.add)
            dep(last)
            ts(hf[:, :], hf[:, :], 1e-6, None, ALU.max).then_inc(h_f, 1)
            for h in range(H_HEADS):
                c = slice(h * T, (h + 1) * T)
                last = stt(h_k[:, c], h_k[:, c], olb[:, h:h + 1], h_b[:, c], ALU.mult, ALU.mult)
            dep(last)
            dve.wait_ge(hg_tanh, 1)
            stt(hg[:, :], g_th, 1.0, hg[:, :], ALU.add, ALU.mult)
            dve.wait_ge(h_log, 1)
            for h in range(H_HEADS):
                c = slice(h * T, (h + 1) * T)
                last = dve.tensor_tensor_scan(h_b[:, c], scan_keep, hf[:, c], 0.0, ALU.mult, ALU.add)
            dep(last)

            def hgrn_diff(h):
                b = h_b[:, h * T:(h + 1) * T].rearrange("p (c a) -> p c a", c=H_NC)
                full = [P, H_NC, H_CHUNK]
                mid = b[:, :, H_CHUNK // 2:H_CHUNK // 2 + 1].to_broadcast(full)
                end = b[:, :, H_CHUNK - 1:H_CHUNK].to_broadcast(full)
                tt(t1.rearrange("p (c a) -> p c a", c=H_NC), b, mid, ALU.subtract)
                tt(t4.rearrange("p (c a) -> p c a", c=H_NC), end, b, ALU.subtract).then_inc(h_diff, 1)

            def hgrn_ops(h):
                c = slice(h * T, (h + 1) * T)
                if h >= 1:
                    dve.wait_ge(h_A, h)
                if h >= 2:
                    dve.wait_ge(h_O, h - 1)
                dve.wait_ge(h_e, 4 * h + 1)
                tt(qq, hq[:, c], e1, ALU.mult)
                dve.wait_ge(h_e, 4 * h + 2)
                tt(kk, h_k[:, c], e2, ALU.mult)
                half = lambda v: v.rearrange("p (c a) -> p c a", c=H_NC)[:, :, 0:H_CHUNK // 2]
                tt(half(kkL), half(h_k[:, c]), half(e2), ALU.mult)
                dve.wait_ge(h_e, 4 * h + 3)
                tt(qe[h % 2], hq[:, c], e3, ALU.mult)
                dve.wait_ge(h_e, 4 * h + 4)
                tt(kd, h_k[:, c], e4, ALU.mult).then_inc(h_ops, 1)

            def hgrn_mask(h):
                dve.wait_ge(h_A, h + 1)
                tt(Am, ps[:, 4, 0:256].rearrange("p (q t) -> p q t", q=2), tri32[:, None, :].to_broadcast([P, 2, P]), ALU.mult)
                cp(kdT, ps[:, 4, 256:512].rearrange("p (q t) -> p q t", q=2)).then_inc(h_Am, 1)

            def hgrn_chain(h):
                dve.wait_ge(h_U, h + 1)
                dep(cp(hS[:, 0, :], ps[:, 5, 0:P]))
                for c in range(1, H_NC - 1):
                    u = ps[:, 5 + c // 4, (c % 4) * P:(c % 4 + 1) * P]
                    ins = stt(hS[:, c, :], hS[:, c - 1, :], hdec[h % 2][:, c:c + 1], u, ALU.mult, ALU.add)
                    if c < H_NC - 2:
                        dep(ins)
                ins.then_inc(h_S, 1)

            def hgrn_out(h):
                dve.wait_ge(h_O, h + 1)
                cp(osb[:, :, h, :], ps[:, 7, 0:256].rearrange("p (q v) -> p q v", q=2)).then_inc(h_osb, 1)

            def hgrn_finish():
                dve.wait_ge(h_sq, 8)
                dve.wait_ge(h_rms, 1)
                dep(dve.reciprocal(hrstd, hrms))
                dve.wait_ge(h_osb, 4)
                for q in range(QT):
                    for h in range(H_HEADS):
                        last = stt(osb[:, q, h, :], osb[:, q, h, :], hrstd[:, 4 * q + h:4 * q + h + 1],
                                   hg[:, q * 512 + h * P:q * 512 + (h + 1) * P], ALU.mult, ALU.mult)
                last.then_inc(h_y, 1)

            def gain_copy(dst, gain, done, copied):
                for k in range(2):
                    dve.wait_ge(done, k + 1)
                    tt(dst[:, 2 * k * T:(2 * k + 2) * T].rearrange("p (c t) -> p c t", c=2),
                       ps[:, 4 + k, :].rearrange("p (c t) -> p c t", c=2),
                       gain[:, 2 * k:2 * k + 2, None].to_broadcast([P, 2, T]), ALU.mult).then_inc(copied, 1)

            def conv_pair(k):
                dve.wait_ge(seg_ready, 21 + k)
                for f in (2 * k, 2 * k + 1):
                    w = lambda j: vec[:, V_CW + 6 * j + f:V_CW + 6 * j + f + 1]
                    xi, yo = xbc[:, f * T:(f + 1) * T], conv[:, f * T:(f + 1) * T]
                    dep(ts(yo, xi, w(3), vec[:, V_CB + f:V_CB + f + 1], ALU.mult, ALU.add))
                    for j in (2, 1, 0):
                        d = 3 - j
                        ins = stt(yo[:, d:T], xi[:, 0:T - d], w(j), yo[:, d:T], ALU.mult, ALU.add)
                        if j:
                            dep(ins)
                ins.then_inc(s_conv, 1)

            def ssd_silu():
                for k in range(3):
                    dve.wait_ge(s_tanh, k + 1)
                    dep(ts(conv_th[k], conv_th[k], 0.5, 0.5, ALU.mult, ALU.add))
                    c = conv[:, k * 512:(k + 1) * 512]
                    last = tt(c, conv_th[k], c, ALU.mult)
                last.then_inc(s_silu, 1)
                dve.wait_ge(s_tanh, 4)
                dep(ts(z_th, z_th, 0.5, 0.5, ALU.mult, ALU.add))
                dep(tt(z_seg[:, :], z_th, z_seg[:, :], ALU.mult))
                dve.wait_ge(dt_log, 1)
                dep(tt(dt, dtm, dta, ALU.add))
                stt(dtA.rearrange("p (q h) -> p q h", q=2), dt.rearrange("p (q h) -> p q h", q=2), -1.0,
                    alog[:, None, :].to_broadcast([P, 2, 8]), ALU.mult, ALU.mult).then_inc(s_silu, 1)

            def ssd_weights():
                dve.wait_ge(s_X, 1)
                dep(cp(acs, ps[:, 6, 256:288]))
                tt(sdec, acs[:, 16:32], acs[:, 0:16], ALU.subtract).then_inc(s_acs, 1)
                dve.wait_ge(s_dec, 1)
                dep(tt(swt, sdec, dt, ALU.mult))
                dep(tt(swB.rearrange("p (q c h) -> p q c h", q=2, c=2),
                       swt.rearrange("p (q h) -> p q h", q=2)[:, :, None, :].to_broadcast([P, 2, 2, 8]),
                       cm64[:, None, :, None].to_broadcast([P, 2, 2, 8]), ALU.mult))
                dve.wait_ge(s_Xcopy, 1)
                tt(xdt.rearrange("p q h n -> p (q h) n"), xtok.rearrange("p q h n -> p (q h) n"),
                   dt[:, :, None].to_broadcast([P, 16, HD]), ALU.mult)

            def ssd_xw(q):
                for c in range(2 - q):
                    w = swB[:, 16 * q + 8 * c:16 * q + 8 * c + 8, None].to_broadcast([P, 8, HD])
                    tt(xwB[:, c, :, :], xtok[:, q, :, :], w, ALU.mult)

            def ssd_L(q):
                dve.wait_ge(s_B, q + 1)
                b = ps[:, 4:6, :].rearrange("p a (h t) -> p (a h) t", h=4)
                dep(tt(Lb, b, acs[:, 8 * q:8 * q + 8, None].to_broadcast([P, 8, P]), ALU.subtract))
                ts(Lb, Lb, 0.0, None, ALU.min).then_inc(s_Larg, 1)
                dep(tt(CBm[:, q, :, :], ps[:, 6, 0:256].rearrange("p (g t) -> p g t", g=2),
                       tri64[:, None, :].to_broadcast([P, 2, P]), ALU.mult))
                if q:
                    dve.wait_ge(s_Y, 1)
                ssd_xw(q)
                dve.wait_ge(s_Lexp, q + 1)
                tt(Lm.rearrange("p (g r) t -> p g r t", g=2), Lb.rearrange("p (g r) t -> p g r t", g=2),
                   CBm[:, q, :, None, :].to_broadcast([P, 2, 4, P]), ALU.mult).then_inc(s_L, 1)

            def ssd_state(q):
                dve.wait_ge(s_Y, q + 1)
                dve.wait_ge(zeroed, 3)
                if q == 0:
                    for g in range(2):
                        r, c = slice(HD * g, HD * (g + 1)), slice(256 * g, 256 * (g + 1))
                        last = cp(sS[r, 1, c], ps[r, 4, c])
                    dep(last)
                chunk = 1 + q
                for g in range(2):
                    r, c = slice(HD * g, HD * (g + 1)), slice(256 * g, 256 * (g + 1))
                    last = tt(sS[r, chunk + 1, c].rearrange("p (r n) -> p r n", r=4),
                              sS[r, chunk, c].rearrange("p (r n) -> p r n", r=4),
                              cdec[r, 4 * chunk:4 * chunk + 4, None].to_broadcast([HD, 4, HD]), ALU.mult)
                dep(last)
                for g in range(2):
                    r, c = slice(HD * g, HD * (g + 1)), slice(256 * g, 256 * (g + 1))
                    last = tt(sS[r, chunk + 1, c], sS[r, chunk + 1, c], ps[r, 5 - q, c], ALU.add)
                last.then_inc(s_state, 1)

            def ssd_y(q):
                dve.wait_ge(s_off, q + 1)
                y1, y2 = ytmp[:, 0, :, :], ytmp[:, 1, :, :]
                hn = lambda v: v.rearrange("p (h n) -> p h n", h=8)
                tt(y2, xtok[:, q, :, :], dskip[:, :, None].to_broadcast([P, 8, HD]), ALU.mult)
                dep(tt(y1, hn(ps[:, 6, :]), eacs[:, 8 * q:8 * q + 8, None].to_broadcast([P, 8, HD]), ALU.mult))
                dep(tt(y1, y1, hn(ps[:, 7, :]), ALU.add))
                dep(tt(y1, y1, y2, ALU.add))
                tt(hn(yd[:, q, :]), y1, hn(z_seg[:, q * 512:(q + 1) * 512]), ALU.mult).then_inc(s_y, 1)

            def merge_update(i):
                k = i % 4
                dve.wait_ge(yp_done, i + 1)
                dve.wait_ge(g_tanh, i + 1)
                u = uT[:, 2 * k * T:(2 * k + 2) * T]
                b = gth[i % 2][:, :]
                if i < 4:
                    stt(u, b, 1.0, ps[:, 2 + i % 2, :], ALU.add, ALU.mult).then_inc(u_done, 1)
                else:
                    dep(stt(b, b, 1.0, ps[:, 2 + i % 2, :], ALU.add, ALU.mult))
                    tt(u, u, b, ALU.add).then_inc(u_done, 1)

            dve.wait_ge(pv_done, NS)
            hgrn_diff(0)
            dve.wait_ge(zeroed, 2)
            hgrn_ops(0)
            for i in range(16):
                if 1 <= i <= 4:
                    hgrn_out(i - 1)
                if i < 4:
                    hgrn_mask(i)
                    if i < 3:
                        hgrn_diff(i + 1)
                    hgrn_chain(i)
                    if i < 3:
                        hgrn_ops(i + 1)
                        conv_pair(i)
                    else:
                        dep(tt(dtr.rearrange("p (q h) -> p q h", q=2), dt_raw[:, :].rearrange("p (q h) -> p q h", q=2),
                               dtb[:, None, :].to_broadcast([P, 2, 8]), ALU.add))
                        ts(dtm, dtr, 0.0, None, ALU.max).then_inc(dt_arg, 1)
                if i == 4:
                    hgrn_finish()
                if i == 8:
                    ssd_L(1)
                if i == 5:
                    ssd_silu()
                    gain_copy(yT_b, vgh, h_yT, h_yTc)
                if i == 6:
                    ssd_weights()
                if i == 7:
                    ssd_state(0)
                if i == 8:
                    ssd_state(1)
                if i == 9:
                    ssd_y(1)
                if i == 11:
                    gain_copy(yT_d, vec[:, V_GS:V_GS + 4], s_yT, s_yTc)
                merge_update(i)
                if i == 6:
                    ssd_L(0)
                if i == 7:
                    ssd_y(0)
                if i == 9:
                    dve.wait_ge(s_sq, 2)
                    dve.wait_ge(s_rms, 1)
                    dep(dve.reciprocal(srstd, srms))
                    dve.wait_ge(s_y, 2)
                    for q in range(QT):
                        last = ts(yd[:, q, :], yd[:, q, :], srstd[:, q:q + 1], None, ALU.mult)
                    last.then_inc(s_n, 1)

            dve.wait_ge(ld_moe, 16 * 5)
            for q in range(QT):
                for n in (2 * q, 2 * q + 1):
                    dve.wait_ge(wo_done, n + 1)
                    c = x[:, n * 512:(n + 1) * 512]
                    stt(c, ps[:, 4 + n, :], 0.5, c, ALU.mult, ALU.add).then_inc(x2_done, 1)
                norm(1, q)
                if q == 0:
                    to_hT(1, 0, None)

            to_hT(1, 1, None)
            dve.wait_ge(rt_done, 1)
            lv = lg.rearrange("p (q n) -> p q n", q=2)
            dep(cp(lv, ps[:, 4, 0:128].rearrange("p (q n) -> p q n", q=2)[:, :, 0:36]))
            L4, L32 = lv[:, :, 0:4], lv[:, :, 4:36]

            def b3(v, n):
                return v[:, :, None].to_broadcast([P, 2, n])

            def first_max(out, vals, top, n):
                dep(tt(cand[:, :, 0:n], vals, b3(top, n), ALU.is_equal))
                dep(tt(cand[:, :, 0:n], cand[:, :, 0:n], iom[:, None, 0:n].to_broadcast([P, 2, n]), ALU.mult))
                dep(dve.tensor_reduce(mn, cand[:, :, 0:n], X, ALU.min))
                dep(tt(out, cand[:, :, 0:n], b3(mn, n), ALU.is_equal))

            dep(ts(iom, iota, -64.0, None, ALU.add))
            dep(dve.tensor_reduce(gm, L4, X, ALU.max))
            tt(gexp.rearrange("p (q n) -> p q n", q=2), L4, b3(gm, 4), ALU.subtract).then_inc(rt_sub, 1)
            first_max(goh, L4, gm, 4)
            dep(ts(gpen, goh, -1.0, 1e30, ALU.add, ALU.mult))
            v4 = vmask.rearrange("p q (g e) -> p q g e", g=GROUPS)
            dep(tt(v4, L32.rearrange("p q (g e) -> p q g e", g=GROUPS), goh[:, :, :, None].to_broadcast([P, 2, GROUPS, EPG]), ALU.mult))
            dep(tt(v4, v4, gpen[:, :, :, None].to_broadcast([P, 2, GROUPS, EPG]), ALU.add))
            dep(dve.tensor_reduce(m1, vmask, X, ALU.max))
            first_max(oh1, vmask, m1, EXPERTS)
            dep(stt(vmask, oh1, -3e30, vmask, ALU.mult, ALU.add))
            dep(dve.tensor_reduce(m2, vmask, X, ALU.max))
            tt(e21, m2, m1, ALU.subtract).then_inc(rt_d, 1)
            first_max(oh2, vmask, m2, EXPERTS)
            tt(mask, oh1, oh2, ALU.add).then_inc(m_mask, 1)
            dve.wait_ge(m_mask, 1)
            dep(ts(nmask, mask, -1000.0, 1000.0, ALU.mult, ALU.add))
            cv = comb.rearrange("p (q e) -> p q e", q=2)
            dve.memset(posm[:, :, EXPERTS:36], 1000.0)
            dve.wait_ge(m_pos, 1)
            dep(tt(posm[:, :, 0:EXPERTS], ps[:, 4, 0:64].rearrange("p (q e) -> p q e", q=2), nmask, ALU.add))
            dep(cp(cnt, ps[:, 4, 64:96]))

            def one_hot(k, first=False):
                if not first:
                    dve.wait_ge(m_G, k)
                    dve.wait_ge(m_Sw, k)
                out = onehot.rearrange("p (q i s) -> p q i s", q=2, i=4)
                tt(out, iota[:, None, None, :].to_broadcast([P, 2, 4, CAP]),
                   posm[:, :, bass.ds(k * 4, 4), None].to_broadcast([P, 2, 4, CAP]), ALU.is_equal).then_inc(m_S, 1)

            def one_hot_weights(k):
                dve.wait_ge(m_S, k + 1)
                tt(onehot_w.rearrange("p (q i s) -> p q i s", q=2, i=4), onehot.rearrange("p (q i s) -> p q i s", q=2, i=4),
                   cv[:, :, bass.ds(k * 4, 4), None].to_broadcast([P, 2, 4, CAP]), ALU.mult).then_inc(m_Sw, 1)

            def copy_scatter_matrix(k):
                dve.wait_ge(m_ST, k + 1)
                cp(scat, ps[:, 6, 0:256].rearrange("p (q t) -> p q t", q=2)).then_inc(m_STc, 1)

            def expert_act(it, i):
                dve.wait_ge(silu_done, it * 4 + (i + 1))
                r = slice(CAP * i, CAP * (i + 1))
                tt(act_tok[r, :], sil[r, :], ps[r, i % 2, FF:2 * FF], ALU.mult).then_inc(act_done, 1)

            def accumulate(k, q, bank=6):
                dve.wait_ge(sc_done, k * 2 + (q + 1))
                c = xv[:, q, :].rearrange("p (a n) -> p a n", a=2)
                tt(c, c, ps[:, bank:bank + 2, :], ALU.add).then_inc(acc_done, 1)

            one_hot(0, first=True)

            dve.wait_ge(rt_exp, 1)
            dep(dve.tensor_reduce(gw, gexp.rearrange("p (q n) -> p q n", q=2), X, ALU.add))
            dep(dve.reciprocal(gw, gw))
            dve.wait_ge(rt_e, 1)
            dep(ts(w1, e21, 1.0, None, ALU.add))
            dep(dve.reciprocal(w1, w1))
            dep(tt(w1, w1, gw, ALU.mult))
            dep(tt(w2, w1, e21, ALU.mult))
            dep(tt(oh1, oh1, b3(w1, EXPERTS), ALU.mult))
            dep(tt(oh2, oh2, b3(w2, EXPERTS), ALU.mult))
            dep(tt(cv, oh1, oh2, ALU.add))

            one_hot_weights(0)
            one_hot(1)

            dep(stt(comb_over, posm[:, :, 0:EXPERTS], float(CAP), cv, ALU.is_ge, ALU.mult))
            dep(ts(isover, cnt, float(CAP), None, ALU.is_gt))
            dep(dve.tensor_tensor_scan(rank, ones[:, 0:EXPERTS], isover, 0.0, ALU.mult, ALU.add))
            dep(tt(pick, rank[:, None, :].to_broadcast([P, MAX_OVER, EXPERTS]),
                   iota[:, 1:MAX_OVER + 1, None].to_broadcast([P, MAX_OVER, EXPERTS]), ALU.is_equal))
            dep(tt(pick, pick, isover[:, None, :].to_broadcast([P, MAX_OVER, EXPERTS]), ALU.mult))
            dep(tt(pick, pick, iota[:, None, :].to_broadcast([P, MAX_OVER, EXPERTS]), ALU.mult))
            dve.tensor_reduce(over_f[:, 0:MAX_OVER], pick, X, ALU.add)
            dep(cp(over_f[:, 15:16], rank[:, EXPERTS - 1:EXPERTS]))
            cp(over[:, :], over_f).then_inc(over_ready, 1)

            for i in range(4):
                expert_act(0, i)
            copy_scatter_matrix(0)
            one_hot_weights(1)
            one_hot(2)

            def group(it, last_group=False):
                expert_act(it, 0)
                expert_act(it, 1)
                accumulate(it - 1, 0)
                expert_act(it, 2)
                accumulate(it - 1, 1)
                expert_act(it, 3)
                copy_scatter_matrix(it)
                if not last_group:
                    one_hot_weights(it + 1)
                    one_hot(it + 2)

            with dve.Fori(1, QUADS - 1) as it:
                group(it)
            group(QUADS - 1, last_group=True)
            accumulate(QUADS - 1, 0)
            accumulate(QUADS - 1, 1, bank=0)

            dve.wait_ge(over_ready, 1)
            dve.memset(over_f[:, 0:1], 0.0).then_inc(f_acc, 1)
            n_over = dve.value_load(over[0:1, 15:16], min_val=0, max_val=MAX_OVER)
            with dve.If(n_over > 0):
                with dve.Fori(0, MAX_OVER) as it:
                    with dve.If(n_over > it):
                        e = dve.value_load(over[0:1, bass.ds(it, 1)], min_val=0, max_val=EXPERTS - 1)
                        dve.wait_ge(f_silu, it + 1)
                        tt(f_act, f_sil, ps[:, 3, :], ALU.mult).then_inc(f_act_done, 1)
                        dve.wait_ge(f_down, it + 1)
                        dve.wait_ge(f_acc, it + 1)
                        for q in range(QT):
                            for dh in range(2):
                                c = xv[:, q, dh * 512:(dh + 1) * 512]
                                last = stt(c, ps[:, 6 * q + dh, :], comb_over[:, q, bass.ds(e, 1)], c, ALU.mult, ALU.add)
                        last.then_inc(f_acc, 1)

            dve.memset(over_f[:, 1:2], 0.0).then_inc(x3_done, 1)
            for q in range(QT):
                norm(2, q)
            for q in range(QT):
                to_hT(2, q, vec[:, V_GPLE:V_GPLE + 8])
            for q in range(QT):
                dve.wait_ge(ple_p, q + 1)
                for dh in range(2):
                    i = 2 * q + dh
                    dve.wait_ge(ple_tanh, i + 1)
                    b = gth[dh][:, :]
                    dep(stt(b, b, 1.0, ps[:, 4 + i, :], ALU.add, ALU.mult))
                    c = xv[:, q, dh * 512:(dh + 1) * 512]
                    stt(c, b, 0.5, c, ALU.mult, ALU.add).then_inc(x4_done, 1)
                    if i == 2:
                        norm(3, 0)
            norm(3, 1)

        @block.gpsimd
        def _(pool):
            pstep = Count(pool_step)

            def clear(dst):
                pstep.on(pool.memset(dst, 0.0))
                pool.wait_ge(pool_step, pstep.n)

            pool.memset(eps, EPS).then_inc(eps_ready, 1)
            pool.wait_ge(eps_ready, 1)
            for kv in (kv_swa, kv_slc, kv_win):
                clear(kv[:, 0:512])
            clear(kcZ)
            clear(vcZ)
            clear(hid)
            pool.memset(csP, 0.0).then_inc(zeroed, 1)
            pool.wait_ge(pv_done, NS)
            pool.wait_ge(zeroed, 1)
            pool.memset(kkL, 0.0).then_inc(zeroed, 1)
            pool.wait_ge(seg_ready, 18)
            pool.wait_ge(zeroed, 2)
            for h in range(H_HEADS):
                if h >= 1:
                    pool.wait_ge(h_U, h)
                    pool.wait_ge(h_iB, h)
                v = hi[:, :].rearrange("p (q n) -> p q n", q=2)[:, :, None, h * P:(h + 1) * P].to_broadcast([P, 2, 4, P])
                pool.tensor_tensor(iB, v, cm32[:, None, :, None].to_broadcast([P, 2, 4, P]), ALU.mult).then_inc(h_iB, 1)
            pool.wait_ge(h_yTc, 2)
            pool.wait_ge(h_iB, 4)
            clear(BZ)
            pool.memset(sS, 0.0).then_inc(zeroed, 1)


_INS = ['x', 'p', 'w_in', 'g_mix', 'attn_sinks', 'hgrn_lower_bounds', 'hgrn_norm_g', 'nsa_pos_k', 'nsa_pos_v',
        'nsa_cmp_w1_k', 'nsa_cmp_w2_k', 'nsa_cmp_w1_v', 'nsa_cmp_w2_v', 'ssm_conv_w', 'ssm_conv_b', 'ssm_dt_bias',
        'ssm_A_log', 'ssm_D', 'ssm_norm_g', 'w_branch', 'w_out', 'g_ffn', 'w_router_grp', 'w_router_exp',
        'w_exp_gate', 'w_exp_up', 'w_exp_down', 'g_ple', 'w_ple_gate', 'w_ple_proj', 'g_final']


def kernel(**inputs):
    import concourse.bacc as _bacc
    from concourse.bass_utils import run_bass_kernel_spmd as _run

    nc = _bacc.Bacc("TRN2", target_bir_lowering=False, num_devices=1)
    arrays = {name: np.ascontiguousarray(inputs[name]) for name in _INS}
    arrays["cst"] = shape_constants()
    args = {name: nc.dram_tensor(name, v.shape, mybir.dt.from_np(v.dtype), kind="ExternalInput").ap()
            for name, v in arrays.items()}
    args["out"] = nc.dram_tensor("out", (1, T, D), F32, kind="ExternalOutput").ap()
    hybrid_layer(nc, args)
    r = _run(nc, [arrays], core_ids=[0])
    return r.results[0]["out"]
```
